# Optimizing a Trainium2 kernel written in Bass

```python
import jax, jax.numpy as jnp
from jax import lax
import numpy as np

D_MODEL = 1024
BATCH = 1
SEQ = 256
DEPTH = 2

N_A_LAYERS = DEPTH // 2
N_B_LAYERS = DEPTH - N_A_LAYERS
N_DENSE = (DEPTH + 1) // 2
N_MOE = DEPTH // 2
NORM_EPS = 1e-6

MLSTM_HEADS = 4
MLSTM_DQK = D_MODEL // (2 * MLSTM_HEADS)
MLSTM_DV = D_MODEL // MLSTM_HEADS
MLSTM_CHUNK = 64
MLSTM_PROJ = MLSTM_HEADS * (2 * MLSTM_DQK + 2 * MLSTM_DV + 2)
MLSTM_SPLITS = (MLSTM_HEADS * MLSTM_DQK,
                2 * MLSTM_HEADS * MLSTM_DQK,
                2 * MLSTM_HEADS * MLSTM_DQK + MLSTM_HEADS * MLSTM_DV,
                2 * MLSTM_HEADS * MLSTM_DQK + 2 * MLSTM_HEADS * MLSTM_DV,
                2 * MLSTM_HEADS * MLSTM_DQK + 2 * MLSTM_HEADS * MLSTM_DV + MLSTM_HEADS)

ATT_HEADS = 8
ATT_KV_HEADS = 2
HEAD_DIM = D_MODEL // ATT_HEADS
MOBA_BLOCK = 256
MOBA_TOPK = 3
QUERY_BLOCK = 128
ROPE_THETA = 500000.0
ROT_DIM = HEAD_DIM // 4

D_FF = 2816
N_EXPERTS = 8
TOP_K_EXPERTS = 2
D_EXPERT = 3584

kernel_name = 'yoco_mlstm_moba_moe_block'

def rmsnorm(x, gain):
    xf = x.astype(jnp.float32)
    y = xf * lax.rsqrt(jnp.mean(xf * xf, axis=-1, keepdims=True) + NORM_EPS)
    return (y * gain.astype(jnp.float32)).astype(x.dtype)

def rope_partial(x, cos, sin):
    c = cos.astype(x.dtype)
    s = sin.astype(x.dtype)
    half = ROT_DIM // 2
    x1 = x[..., :half]
    x2 = x[..., half:ROT_DIM]
    return jnp.concatenate([x1 * c - x2 * s, x2 * c + x1 * s, x[..., ROT_DIM:]], axis=-1)

def swiglu(x, w_gu, w_down):
    g, u = jnp.split(x @ w_gu, 2, axis=-1)
    return (jax.nn.silu(g) * u) @ w_down

def mlstm_mixer(xn, w_in, b_if, out_gain, w_out):
    B, S, _ = xn.shape
    nc = S // MLSTM_CHUNK
    H, L = MLSTM_HEADS, MLSTM_CHUNK
    f32 = jnp.float32
    proj = xn @ w_in
    q, k, v, o, ig, fg = jnp.split(proj, MLSTM_SPLITS, axis=-1)

    def heads(t, d):
        return t.reshape(B, S, H, d).transpose(0, 2, 1, 3).reshape(B, H, nc, L, d).astype(f32)

    q = heads(q, MLSTM_DQK) * (MLSTM_DQK ** -0.5)
    k = heads(k, MLSTM_DQK)
    v = heads(v, MLSTM_DV)
    ig = (ig.astype(f32) + b_if[0].astype(f32)).transpose(0, 2, 1).reshape(B, H, nc, L)
    logf = jax.nn.log_sigmoid(fg.astype(f32) + b_if[1].astype(f32)).transpose(0, 2, 1).reshape(B, H, nc, L)

    bcum = jnp.cumsum(logf, axis=-1)
    g_tot = bcum[..., -1]
    a_end = g_tot[..., None] - bcum + ig

    def step(carry, xs):
        C, n, m = carry
        k_c, v_c, a_c, g_c = xs
        m_new = jnp.maximum(g_c + m, jnp.max(a_c, axis=-1))
        w = jnp.exp(a_c - m_new[..., None])
        decay = jnp.exp(g_c + m - m_new)
        C_new = decay[..., None, None] * C + jnp.einsum('bhlv,bhlk->bhvk', w[..., None] * v_c, k_c)
        n_new = decay[..., None] * n + jnp.einsum('bhl,bhlk->bhk', w, k_c)
        return (C_new, n_new, m_new), (C, n, m)

    init = (jnp.zeros((B, H, MLSTM_DV, MLSTM_DQK), f32),
            jnp.zeros((B, H, MLSTM_DQK), f32),
            jnp.zeros((B, H), f32))
    xs = (jnp.moveaxis(k, 2, 0), jnp.moveaxis(v, 2, 0), jnp.moveaxis(a_end, 2, 0), jnp.moveaxis(g_tot, 2, 0))
    _, (C_s, n_s, m_s) = lax.scan(step, init, xs)
    C_s = jnp.moveaxis(C_s, 0, 2)
    n_s = jnp.moveaxis(n_s, 0, 2)
    m_s = jnp.moveaxis(m_s, 0, 2)

    causal = jnp.tril(jnp.ones((L, L), dtype=bool))
    D = bcum[..., :, None] - bcum[..., None, :] + ig[..., None, :]
    D = jnp.where(causal, D, -jnp.inf)
    inter = bcum + m_s[..., None]
    m_t = jnp.maximum(inter, jnp.max(D, axis=-1))
    P = jnp.einsum('bhctk,bhcsk->bhcts', q, k) * jnp.exp(D - m_t[..., None])
    inter_w = jnp.exp(inter - m_t)
    num = jnp.einsum('bhcts,bhcsv->bhctv', P, v) + inter_w[..., None] * jnp.einsum('bhcvk,bhctk->bhctv', C_s, q)
    nq = jnp.sum(P, axis=-1) + inter_w * jnp.einsum('bhck,bhctk->bhct', n_s, q)
    den = jnp.maximum(jnp.abs(nq), jnp.exp(-m_t))
    h = num / den[..., None]

    h = h.reshape(B, H, S, MLSTM_DV).transpose(0, 2, 1, 3)
    h = h * lax.rsqrt(jnp.mean(h * h, axis=-1, keepdims=True) + NORM_EPS)
    h = h * out_gain.astype(f32).reshape(H, MLSTM_DV)
    h = h * jax.nn.sigmoid(o.astype(f32)).reshape(B, S, H, MLSTM_DV)
    return h.reshape(B, S, H * MLSTM_DV).astype(xn.dtype) @ w_out

def shared_kv(x, kv_norm, kv_w, cos, sin):
    B, S, _ = x.shape
    kv = rmsnorm(x, kv_norm) @ kv_w
    k, v = jnp.split(kv, 2, axis=-1)
    k = k.reshape(B, S, ATT_KV_HEADS, HEAD_DIM).transpose(0, 2, 1, 3)
    v = v.reshape(B, S, ATT_KV_HEADS, HEAD_DIM).transpose(0, 2, 1, 3)
    k = rope_partial(k, cos, sin)
    nb = -(-S // MOBA_BLOCK)
    pad = nb * MOBA_BLOCK - S
    k = jnp.pad(k, ((0, 0), (0, 0), (0, pad), (0, 0)))
    v = jnp.pad(v, ((0, 0), (0, 0), (0, pad), (0, 0)))
    k_blocks = k.reshape(B, ATT_KV_HEADS, nb, MOBA_BLOCK, HEAD_DIM)
    v_blocks = v.reshape(B, ATT_KV_HEADS, nb, MOBA_BLOCK, HEAD_DIM)
    k_means = jnp.mean(k_blocks.astype(jnp.float32), axis=3)
    return k_blocks, v_blocks, k_means

def moba_mixer(xn, w_q, w_o, k_blocks, v_blocks, k_means, cos, sin):
    B, S, _ = xn.shape
    H = ATT_HEADS
    nb = k_blocks.shape[2]
    nqb = S // QUERY_BLOCK
    kk = min(MOBA_TOPK, nb)
    f32 = jnp.float32
    q = (xn @ w_q).reshape(B, S, H, HEAD_DIM).transpose(0, 2, 1, 3)
    q = rope_partial(q, cos, sin)
    kv_of_head = jnp.arange(H) // (H // ATT_KV_HEADS)

    gate = jnp.einsum('bhtd,bhnd->bhtn', q.astype(f32), k_means[:, kv_of_head])
    own = jnp.arange(S) // MOBA_BLOCK
    past = jnp.arange(nb)[None, :] < own[:, None]
    gate = jnp.where(past, gate, -jnp.inf)
    _, sel = lax.top_k(gate, kk)

    def to_items(t):
        t = t.reshape(B, H, nqb, QUERY_BLOCK, *t.shape[3:])
        t = jnp.moveaxis(t, 2, 1)
        return t.reshape(B * nqb, H, QUERY_BLOCK, *t.shape[4:])

    b_ids = jnp.repeat(jnp.arange(B, dtype=jnp.int32), nqb)
    qb_ids = jnp.tile(jnp.arange(nqb, dtype=jnp.int32), B)
    scale = HEAD_DIM ** -0.5

    def attend(item):
        q_i, sel_i, b_i, qb_i = item
        kb = k_blocks[b_i]
        vb = v_blocks[b_i]
        own_blk = (qb_i * QUERY_BLOCK) // MOBA_BLOCK
        k_sel = kb[kv_of_head[:, None, None], sel_i]
        v_sel = vb[kv_of_head[:, None, None], sel_i]
        k_own = kb[kv_of_head, own_blk]
        v_own = vb[kv_of_head, own_blk]
        s_sel = jnp.einsum('htd,htjsd->htjs', q_i, k_sel).astype(f32) * scale
        slot_ok = jnp.arange(kk) < own_blk
        s_sel = jnp.where(slot_ok[:, None], s_sel, -jnp.inf)
        s_own = jnp.einsum('htd,hsd->hts', q_i, k_own).astype(f32) * scale
        t_pos = qb_i * QUERY_BLOCK + jnp.arange(QUERY_BLOCK)
        s_pos = own_blk * MOBA_BLOCK + jnp.arange(MOBA_BLOCK)
        s_own = jnp.where(s_pos[None, :] <= t_pos[:, None], s_own, -jnp.inf)
        scores = jnp.concatenate([s_sel.reshape(H, QUERY_BLOCK, kk * MOBA_BLOCK), s_own], axis=-1)
        p = jax.nn.softmax(scores, axis=-1).astype(v_sel.dtype)
        p_sel = p[..., :kk * MOBA_BLOCK].reshape(H, QUERY_BLOCK, kk, MOBA_BLOCK)
        p_own = p[..., kk * MOBA_BLOCK:]
        return jnp.einsum('htjs,htjsd->htd', p_sel, v_sel) + jnp.einsum('hts,hsd->htd', p_own, v_own)

    out = lax.map(attend, (to_items(q), to_items(sel), b_ids, qb_ids))
    out = out.reshape(B, nqb, H, QUERY_BLOCK, HEAD_DIM).transpose(0, 1, 3, 2, 4).reshape(B, S, H * HEAD_DIM)
    return out @ w_o

def moe_ffn(xn, router, w_gu, w_down):
    B, S, D = xn.shape
    xt = xn.reshape(B * S, D)
    logits = (xt @ router).astype(jnp.float32)
    top_logits, top_idx = lax.top_k(logits, TOP_K_EXPERTS)
    top_w = jax.nn.softmax(top_logits, axis=-1)
    combine = jnp.einsum('nk,nke->ne', top_w, jax.nn.one_hot(top_idx, N_EXPERTS, dtype=jnp.float32)).astype(xn.dtype)
    y = jnp.zeros_like(xt)
    for e in range(N_EXPERTS):
        y = y + combine[:, e:e + 1] * swiglu(xt, w_gu[e], w_down[e])
    return y.reshape(B, S, D)

def setup_inputs(seed: int = 0) -> dict:
    key = jax.random.key(seed)
    ks = jax.random.split(key, 20)
    f32 = jnp.float32

    def w(k, shape, fan_in):
        return jax.random.normal(k, shape, f32) * (fan_in ** -0.5)

    def g(k, shape):
        return 1.0 + 0.02 * jax.random.normal(k, shape, f32)

    x = jax.random.normal(ks[0], (BATCH, SEQ, D_MODEL), f32)
    b_i = 0.1 * jax.random.normal(ks[3], (N_A_LAYERS, MLSTM_HEADS), f32)
    b_f = jnp.linspace(3.0, 6.0, MLSTM_HEADS, dtype=f32)[None, :] + 0.1 * jax.random.normal(ks[4], (N_A_LAYERS, MLSTM_HEADS), f32)
    return {
        'x': x,
        'mlstm_norm': g(ks[1], (N_A_LAYERS, D_MODEL)),
        'mlstm_w_in': w(ks[2], (N_A_LAYERS, D_MODEL, MLSTM_PROJ), D_MODEL),
        'mlstm_b_if': jnp.stack([b_i, b_f], axis=1),
        'mlstm_out_norm': g(ks[5], (N_A_LAYERS, MLSTM_HEADS * MLSTM_DV)),
        'mlstm_w_out': w(ks[6], (N_A_LAYERS, MLSTM_HEADS * MLSTM_DV, D_MODEL), MLSTM_HEADS * MLSTM_DV),
        'ffn_norm': g(ks[7], (DEPTH, D_MODEL)),
        'dense_w_gu': w(ks[8], (N_DENSE, D_MODEL, 2 * D_FF), D_MODEL),
        'dense_w_down': w(ks[9], (N_DENSE, D_FF, D_MODEL), D_FF),
        'moe_router': w(ks[10], (N_MOE, D_MODEL, N_EXPERTS), D_MODEL),
        'moe_w_gu': w(ks[11], (N_MOE, N_EXPERTS, D_MODEL, 2 * D_EXPERT), D_MODEL),
        'moe_w_down': w(ks[12], (N_MOE, N_EXPERTS, D_EXPERT, D_MODEL), D_EXPERT),
        'kv_norm': g(ks[13], (D_MODEL,)),
        'kv_w': w(ks[14], (D_MODEL, 2 * ATT_KV_HEADS * HEAD_DIM), D_MODEL),
        'moba_norm': g(ks[15], (N_B_LAYERS, D_MODEL)),
        'moba_w_q': w(ks[16], (N_B_LAYERS, D_MODEL, ATT_HEADS * HEAD_DIM), D_MODEL),
        'moba_w_o': w(ks[17], (N_B_LAYERS, ATT_HEADS * HEAD_DIM, D_MODEL), ATT_HEADS * HEAD_DIM),
        'final_norm': g(ks[18], (D_MODEL,)),
    }

def reference(x, mlstm_norm, mlstm_w_in, mlstm_b_if, mlstm_out_norm, mlstm_w_out, ffn_norm,
              dense_w_gu, dense_w_down, moe_router, moe_w_gu, moe_w_down, kv_norm, kv_w,
              moba_norm, moba_w_q, moba_w_o, final_norm):
    S = x.shape[1]
    pos = jnp.arange(S, dtype=jnp.float32)
    inv_freq = ROPE_THETA ** (-jnp.arange(0, ROT_DIM, 2, dtype=jnp.float32) / ROT_DIM)
    ang = pos[:, None] * inv_freq[None, :]
    cos, sin = jnp.cos(ang), jnp.sin(ang)

    shared = None
    for l in range(DEPTH):
        if l < N_A_LAYERS:
            x = x + mlstm_mixer(rmsnorm(x, mlstm_norm[l]), mlstm_w_in[l], mlstm_b_if[l],
                                mlstm_out_norm[l], mlstm_w_out[l])
        else:
            if shared is None:
                shared = shared_kv(x, kv_norm, kv_w, cos, sin)
            j = l - N_A_LAYERS
            k_blocks, v_blocks, k_means = shared
            x = x + moba_mixer(rmsnorm(x, moba_norm[j]), moba_w_q[j], moba_w_o[j],
                               k_blocks, v_blocks, k_means, cos, sin)
        hn = rmsnorm(x, ffn_norm[l])
        if l % 2 == 0:
            x = x + swiglu(hn, dense_w_gu[l // 2], dense_w_down[l // 2])
        else:
            x = x + moe_ffn(hn, moe_router[l // 2], moe_w_gu[l // 2], moe_w_down[l // 2])
    return rmsnorm(x, final_norm)


_drawn_inputs = setup_inputs


def setup_inputs(seed=0):
    import zlib

    import numpy as np

    out = dict(_drawn_inputs(seed))
    spreads = {}
    factors = {'kv_norm': 3.171, 'moba_norm': 3.458, 'final_norm': 2.904}
    for name, (base, spread) in spreads.items():
        noise = np.random.default_rng([zlib.crc32(name.encode()), seed]).standard_normal(out[name].shape)
        drawn = base * np.exp(spread * noise) if base else spread * noise
        out[name] = __import__('jax').numpy.asarray(drawn.astype(out[name].dtype))
    for name, factor in factors.items():
        out[name] = (out[name] * factor).astype(out[name].dtype)
    return out
```

```python
from contextlib import ExitStack

import concourse.bass as bass
from concourse import mybir

ALU = mybir.AluOpType
ACT = mybir.ActivationFunctionType
F32 = mybir.dt.float32
F32R = mybir.dt.float32r
I32 = mybir.dt.int32
AX = mybir.AxisListType.X

P = 128
EPS = 1e-6
FAR = 1e30

D = 1024
S = 256
TT = S // P
KT = D // P
MH, MK, MV = 4, 128, 256
AH, KVH, HD = 8, 2, 128
ROT = HD // 4
HALF = ROT // 2
FF = 2816
FC = 256
NFC = FF // FC
NE = 8
FE = 3584
EC = 512
NEC = FE // EC
SLOTS = 128

UNIT = 2048
RAW = 6
SPL = 3
U_IN = 0
U_OUT = U_IN + 12
U_FFN = U_OUT + 4
U_KV = U_FFN + 3 * NFC
U_Q = U_KV + 2
U_O = U_Q + 4
U_MOE = U_O + 4
UE = 6 * NEC
assert UE % RAW == 0 and RAW % SPL == 0


def expert_units():
    order = []
    for j in range(NEC):
        order += [("g", j, 0), ("g", j, 1), ("u", j, 0), ("u", j, 1)]
        if j:
            order += [("d", j - 1, 0), ("d", j - 1, 1)]
    return order + [("d", NEC - 1, 0), ("d", NEC - 1, 1)]


UNITS = expert_units()

PV_BANK = [(0, 7), (1, 2), (3, 4), (5, 6)]
ATT_GROUPS = [(2, 1, 0, S), (2, 1, 2, S), (2, 1, 4, S), (2, 1, 6, S), (4, 0, 0, P), (4, 0, 4, P)]
ATT_SBANK = [4, 5, 6, 7, 0, 1]
ATT_BANK = [2, 3, 4, 5, 6, 7, 0, 1]
SC_BANK = [7, 3, 4, 7]
POOL_ALL = 9


def yoco_block(nc, x_in, mlstm_norm, w_in, b_if, out_norm, w_out, ffn_norm, w_gu, w_down, router,
               e_gu, e_down, kv_norm, kv_w, moba_norm, w_q, w_o, final_norm, rope, out):
    with ExitStack() as ctx:
        def sem(name):
            return ctx.enter_context(nc.semaphore(name))

        def keep(name, shape, dt=F32):
            return ctx.enter_context(nc.sbuf_tensor(name, shape, dt))

        raw = keep("raw", [P, RAW, UNIT])
        wh = keep("wh", [P, SPL, UNIT], F32R)
        wl = keep("wl", [P, SPL, UNIT], F32R)
        x = keep("x", [P, TT, D])
        xr = keep("xr", [P, TT, D])
        xh = keep("xh", [P, KT, S], F32R)
        xl = keep("xl", [P, KT, S], F32R)
        ident = keep("ident", [P, P])
        ones = keep("ones", [P, P])
        onerow = keep("onerow", [MH, S])
        zero = keep("zero", [P, 512], F32R)
        before = keep("before", [P, P])
        late_st = keep("late_st", [P, S])
        late_ts = keep("late_ts", [P, S])
        iota_s = keep("iota_s", [P, SLOTS])
        iota_e = keep("iota_e", [P, TT, NE])
        iota_e8 = keep("iota_e8", [P, TT, NE])
        sel = keep("sel", [MH, MH, P])
        grows = keep("grows", [40, P])
        gains = keep("gains", [P, 40])
        cs = keep("cs", [P, TT, 2, HALF])
        bif = keep("bif", [MH, 2])
        ss = keep("ss", [P, TT])
        var = keep("var", [P, TT])
        lnv = keep("lnv", [P, TT])
        rs = keep("rs", [P, TT])
        t1 = keep("t1", [P, TT])
        rt = keep("rt", [P, KT, NE])
        gfin = keep("gfin", [P, D])
        gmoe = keep("gmoe", [P, D])

        phase = ExitStack()

        def sb(name, shape, dt=F32):
            return phase.enter_context(nc.sbuf_tensor(name, shape, dt))

        graw = sb("graw", [P, KT, 2 * MH])
        gh = sb("gh", [P, KT, 2 * MH], F32R)
        gl = sb("gl", [P, KT, 2 * MH], F32R)
        qT = sb("qT", [P, MH, S])
        kT = sb("kT", [P, MH, S])
        v = sb("v", [P, TT, MH, MV + 1])
        sigo = sb("sigo", [P, TT, D])
        gsb = sb("gsb", [P, TT, 2 * MH])
        rows = sb("rows", [MH, 9, S])
        cols = sb("cols", [P, 4, MH])
        enm = sb("enm", [P, TT, MH])
        E = sb("E", [P, MH, 384])
        den = sb("den", [P, TT, MH])
        rden = sb("rden", [P, TT, MH])
        hss = sb("hss", [P, TT, MH])
        hvar = sb("hvar", [P, TT, MH])
        hln = sb("hln", [P, TT, MH])
        hrs = sb("hrs", [P, TT, MH])
        ht1 = sb("ht1", [P, TT, MH])
        junk = sb("junk", [P, TT, MH, MV])
        phase.close()
        f_sg = sb("f_sg", [P, TT, FC])
        f_h = sb("f_h", [P, TT, FC])
        f_hth = sb("f_hth", [P, 2, S], F32R)
        f_htl = sb("f_htl", [P, 2, S], F32R)
        phase.close()
        yh2 = sb("yh2", [P, KT, S], F32R)
        yl2 = sb("yl2", [P, KT, S], F32R)
        kvs = sb("kvs", [P, TT, 2 * KVH * HD])
        aqT = sb("aqT", [P, AH, S])
        akT = sb("akT", [P, KVH, S])
        tmp = sb("tmp", [P, 4, TT, AH, HALF])
        sc = sb("sc", [P, 6, 512])
        mx = sb("mx", [P, TT, AH])
        nb = sb("nb", [P, TT, AH])
        sm = sb("sm", [P, TT, AH])
        rsm = sb("rsm", [P, TT, AH])
        pT = sb("pT", [P, AH, 384])
        phase.close()
        hnT = sb("hnT", [P, KT, S])
        xrh = sb("xrh", [P, TT, D], F32R)
        xrl = sb("xrl", [P, TT, D], F32R)
        xeh = sb("xeh", [P, KT, SLOTS], F32R)
        xel = sb("xel", [P, KT, SLOTS], F32R)
        ph = sb("ph", [P, TT, SLOTS])
        phr = sb("phr", [P, TT, SLOTS], F32R)
        phT = sb("phT", [SLOTS, S], F32R)
        sg = sb("sg", [P, EC])
        hh = sb("hh", [P, EC])
        hth = sb("hth", [P, 4, SLOTS], F32R)
        htl = sb("htl", [P, 4, SLOTS], F32R)
        ywh = sb("ywh", [SLOTS, D], F32R)
        ywl = sb("ywl", [SLOTS, D], F32R)
        wcol = sb("wcol", [SLOTS, 1])
        lg = sb("lg", [P, TT, NE])
        l2 = sb("l2", [P, TT, NE])
        eq = sb("eq", [P, TT, NE])
        cand = sb("cand", [P, TT, NE])
        oh1 = sb("oh1", [P, TT, NE])
        oh2 = sb("oh2", [P, TT, NE])
        m1 = sb("m1", [P, TT])
        m2 = sb("m2", [P, TT])
        i1 = sb("i1", [P, TT])
        i2 = sb("i2", [P, TT])
        dd = sb("dd", [P, TT])
        ee = sb("ee", [P, TT])
        w1 = sb("w1", [P, TT])
        w2 = sb("w2", [P, TT])
        msk = sb("msk", [P, TT, NE])
        cmb = sb("cmb", [P, TT, NE])
        cmb2 = sb("cmb2", [P, TT, NE])
        rank = sb("rank", [P, NE + 1, TT])
        cw = sb("cw", [P, NE, TT, 2], F32R)
        most = sb("most", [P, 1])
        flag = sb("flag", [1, 1], I32)
        phase.close()

        ps = [ctx.enter_context(nc.psum_tensor(f"ps{b}", [P, 512], F32)) for b in range(8)]

        raw_full = [sem(f"raw_full{i}") for i in range(RAW)]
        hi_split = sem("hi_split")
        lo_split = sem("lo_split")
        unit_done = sem("unit_done")
        x_here = sem("x_here")
        c_here = sem("c_here")
        c_late = sem("c_late")
        pool_ready = sem("pool_ready")
        pool_zero = sem("pool_zero")
        gains_t = sem("gains_t")
        gains_ready = sem("gains_ready")
        nrm_a = sem("nrm_a")
        nrm_d = sem("nrm_d")
        xr0 = sem("xr0")
        xr1 = sem("xr1")
        x_turned = sem("x_turned")
        x_hi = sem("x_hi")
        x_lo = sem("x_lo")
        resid = sem("resid")
        q_out = sem("q_out")
        k_out = sem("k_out")
        va_out = sem("va_out")
        vd_out = sem("vd_out")
        v_one = sem("v_one")
        o_out = sem("o_out")
        g_hi = sem("g_hi")
        g_lo = sem("g_lo")
        g_mm = sem("g_mm")
        g_sb = sem("g_sb")
        g_rows = sem("g_rows")
        chain = sem("chain")
        r_abs = sem("r_abs")
        r_ln = sem("r_ln")
        r_done = sem("r_done")
        z_t = sem("z_t")
        z_cols = sem("z_cols")
        e_nm = sem("e_nm")
        m_bc = sem("m_bc")
        d_done = sem("d_done")
        e_done = sem("e_done")
        s_mm = sem("s_mm")
        p_done = sem("p_done")
        pv_done = sem("pv_done")
        rd_done = sem("rd_done")
        h_raw = sem("h_raw")
        h_var = sem("h_var")
        h_ln = sem("h_ln")
        h_norm = sem("h_norm")
        f_silu = sem("f_silu")
        f_mul = sem("f_mul")
        f_t = sem("f_t")
        f_hi = sem("f_hi")
        f_lo = sem("f_lo")
        kv_out = sem("kv_out")
        aq_out = sem("aq_out")
        k_rope = sem("k_rope")
        q_rope = sem("q_rope")
        k_t = sem("k_t")
        q_t = sem("q_t")
        kt_out = sem("kt_out")
        qt_out = sem("qt_out")
        a_s = sem("a_s")
        a_sc = sem("a_sc")
        a_nb = sem("a_nb")
        a_exp = sem("a_exp")
        a_p = sem("a_p")
        a_pt = sem("a_pt")
        a_pto = sem("a_pto")
        a_o = sem("a_o")
        a_hi = sem("a_hi")
        a_lo = sem("a_lo")
        hn_ready = sem("hn_ready")
        hn_hi = sem("hn_hi")
        hn_lo = sem("hn_lo")
        r_t = sem("r_t")
        r_tout = sem("r_tout")
        r_mm = sem("r_mm")
        top_d = sem("top_d")
        top_e = sem("top_e")
        top_m = sem("top_m")
        rk_mm = sem("rk_mm")
        flag_set = sem("flag_set")
        moe_bank = sem("moe_bank")
        moe_p = sem("moe_p")
        moe_xg = sem("moe_xg")
        moe_xh = sem("moe_xh")
        moe_xl = sem("moe_xl")
        moe_silu = sem("moe_silu")
        moe_h = sem("moe_h")
        moe_t = sem("moe_t")
        moe_hth = sem("moe_hth")
        moe_htl = sem("moe_htl")
        moe_pt = sem("moe_pt")
        moe_ptr = sem("moe_ptr")
        moe_w = sem("moe_w")
        moe_yh = sem("moe_yh")
        moe_yl = sem("moe_yl")
        moe_sc = sem("moe_sc")
        fin = sem("fin")
        stored = sem("stored")

        x_v = x_in[0].rearrange("(t p) d -> p t d", p=P)
        out_v = out[0].rearrange("(t p) d -> p t d", p=P)

        def rows512(w):
            return w.rearrange("(k p) n -> p k n", p=P)

        def kn(buf, slot):
            return buf[:, slot, :].rearrange("p (k n) -> p k n", k=4)

        def kc(buf, slot):
            return buf[:, slot, :].rearrange("p (k n) -> p k n", k=8)

        def fn(buf, slot):
            return buf[:, slot, :].rearrange("p (k n) -> p k n", k=2)

        def f32(ap):
            return ap.bitcast(F32)

        def att_heads(g):
            heads, t, h0, n = ATT_GROUPS[g]
            return [(h0 + a, t, sc[:, g, a * n:(a + 1) * n]) for a in range(heads)]

        block = ctx.enter_context(nc.Block())

        @block.sync
        def _(sp):
            def load(n, i, dst, src, after=None):
                if after is not None:
                    sp.wait_ge(lo_split, after)
                sp.dma_start(dst, src).then_inc(raw_full[i % RAW], 16)

            def free(n):
                return n - RAW + 1 if n >= RAW else None

            def load_kn(n, w, col, half, step=None):
                src = rows512(w)[:, 4 * half:4 * half + 4, col:col + 512]
                load(n, n, kn(raw, n % RAW), src, free(n))

            for t in range(TT):
                sp.dma_start(x[:, t, :], x_v[:, t, :]).then_inc(x_here, 16)
            for j in range(6):
                for half in range(2):
                    load_kn(U_IN + 2 * j + half, w_in[0], 512 * j, half)
            for j in range(2):
                for half in range(2):
                    load_kn(U_OUT + 2 * j + half, w_out[0], 512 * j, half)

            def ffn_gu(i, after, col):
                sp.wait_ge(lo_split, after)
                sp.dma_start(kc(raw, i % RAW), rows512(w_gu[0])[:, :, bass.ds(col, FC)]
                             ).then_inc(raw_full[i % RAW], 16)

            def ffn_down(i, after, row):
                src = w_down[0][bass.ds(row, FC), :].rearrange("(k p) n -> p k n", p=P)
                sp.wait_ge(lo_split, after)
                sp.dma_start(fn(raw, i % RAW), src).then_inc(raw_full[i % RAW], 16)

            ffn_gu(U_FFN, U_FFN - RAW + 1, 0)
            ffn_gu(U_FFN + 1, U_FFN + 1 - RAW + 1, FF)
            with sp.Fori(0, (NFC - 1) // 2) as it:
                for jj in range(2):
                    i = U_FFN + 2 + 3 * jj
                    ffn_gu(i, 6 * it + (i - RAW + 1), (2 * it + (jj + 1)) * FC)
                    ffn_gu(i + 1, 6 * it + (i + 1 - RAW + 1), (2 * it + (jj + 1)) * FC + FF)
                    ffn_down(i + 2, 6 * it + (i + 2 - RAW + 1), (2 * it + jj) * FC)
            ffn_down(U_KV - 1, U_KV - 1 - RAW + 1, (NFC - 1) * FC)

            for half in range(2):
                load_kn(U_KV + half, kv_w, 0, half)
            for j in range(2):
                for half in range(2):
                    load_kn(U_Q + 2 * j + half, w_q[0], 512 * j, half)
            for j in range(2):
                for half in range(2):
                    load_kn(U_O + 2 * j + half, w_o[0], 512 * j, half)

            def load_expert(e, q, first, last):
                gu = e_gu[0].rearrange("e (k p) n -> e p k n", p=P)
                dn = e_down[0].rearrange("e (k p) n -> e p k n", p=P)
                for i in range(first, last):
                    kind, j, half = UNITS[i]
                    n = U_MOE + i
                    if kind == "d":
                        k = 4 * j + 2 * half
                        dst, src = fn(raw, n % RAW), dn[e, :, k:k + 2, :]
                    else:
                        c = EC * j + (FE if kind == "u" else 0)
                        dst, src = kn(raw, n % RAW), gu[e, :, 4 * half:4 * half + 4, c:c + EC]
                    sp.wait_ge(lo_split, q * UE + (n - RAW + 1))
                    sp.dma_start(dst, src).then_inc(raw_full[n % RAW], 16)

            with sp.Fori(0, NE) as e:
                load_expert(e, e, 0, UE)
            load_expert(0, NE, 0, 2)
            sp.wait_ge(flag_set, 1)
            over = sp.value_load(flag[0:1, 0:1], min_val=0, max_val=S)
            with sp.If(over > SLOTS):
                load_expert(0, NE, 2, UE)
                with sp.Fori(1, NE) as e:
                    load_expert(e, e + NE, 0, UE)
                load_expert(0, 2 * NE, 0, 2)
            for t in range(TT):
                sp.wait_ge(fin, t + 1)
                sp.dma_start(out_v[:, t, :], xr[:, t, :]).then_inc(stored, 16)
            sp.wait_ge(stored, 16 * TT)

        @block.gpsimd
        def _(pool):
            pool.memset(ident[:], 0.0).then_inc(pool_zero, 1)
            pool.memset(ones[:], 1.0).then_inc(pool_zero, 1)
            pool.memset(late_st[:], 0.0).then_inc(pool_zero, 1)
            pool.memset(late_ts[:], 0.0).then_inc(pool_zero, 1)
            pool.memset(sel[:], 0.0).then_inc(pool_zero, 1)
            pool.memset(onerow[:], 1.0).then_inc(pool_ready, 1)
            pool.wait_ge(pool_zero, 5)
            pool.affine_select(out=ident[:], in_=ident[:], compare_op=ALU.not_equal, fill=1.0, base=0,
                               pattern=[[-1, P]], channel_multiplier=1).then_inc(pool_ready, 1)
            pool.affine_select(out=before[:], in_=ones[:], compare_op=ALU.is_gt, fill=0.0, base=0,
                               pattern=[[1, P]], channel_multiplier=-1).then_inc(pool_ready, 1)
            pool.affine_select(out=late_st[:, 0:P], in_=late_st[:, 0:P], compare_op=ALU.is_ge, fill=FAR,
                               base=0, pattern=[[1, P]], channel_multiplier=-1).then_inc(pool_ready, 1)
            pool.affine_select(out=late_ts[:, P:S], in_=late_ts[:, P:S], compare_op=ALU.is_ge, fill=-FAR,
                               base=0, pattern=[[-1, P]], channel_multiplier=1).then_inc(pool_ready, 1)
            pool.affine_select(out=sel[:], in_=sel[:], compare_op=ALU.not_equal, fill=1.0, base=0,
                               pattern=[[-1, MH], [0, P]], channel_multiplier=1).then_inc(pool_ready, 1)
            pool.iota(iota_s[:], pattern=[[1, SLOTS]], base=0, channel_multiplier=0,
                      allow_small_or_imprecise_dtypes=True).then_inc(pool_ready, 1)
            pool.iota(iota_e[:], pattern=[[0, TT], [1, NE]], base=0, channel_multiplier=0,
                      allow_small_or_imprecise_dtypes=True).then_inc(pool_ready, 1)
            pool.iota(iota_e8[:], pattern=[[0, TT], [1, NE]], base=NE, channel_multiplier=0,
                      allow_small_or_imprecise_dtypes=True).then_inc(pool_ready, 1)

        @block.scalar
        def _(act):
            def split(i, c=0):
                act.wait_ge(raw_full[i % RAW], 16 * c + 16 * (i // RAW + 1))
                if i >= SPL:
                    act.wait_ge(unit_done, RAW * c + (i - SPL + 1))
                act.activation(wh[:, i % SPL, :], raw[:, i % RAW, :], ACT.Copy).then_inc(hi_split, 1)

            def norm(i, tile0):
                act.wait_ge(*tile0)
                act.activation(xr[:, 0, :], x[:, 0, :], ACT.Square, accum_out=ss[:, 0:1]).then_inc(nrm_a, 1)
                act.wait_ge(nrm_d, 6 * i + 2)
                act.activation(lnv[:], var[:], ACT.Ln).then_inc(nrm_a, 1)
                act.wait_ge(nrm_a, 3 * i + 2)
                act.activation(rs[:], lnv[:], ACT.Exp, scale=-0.5).then_inc(nrm_a, 1)
                if i < 3:
                    act.wait_ge(nrm_d, 6 * i + 6)
                    act.activation(xr[:, 0, :], x[:, 0, :], ACT.Copy, scale=rs[:, 0:1]).then_inc(xr0, 1)

            def turn_hi(c, dst, gain):
                act.activation(dst[:, c, :], ps[c][:, 0:S], ACT.Copy, scale=gains[:, 8 * gain + c:8 * gain + c + 1]
                               ).then_inc(x_hi, 1)

            def turn(k, gain):
                for c in range(KT):
                    act.wait_ge(x_turned, 8 * k + c + 1)
                    turn_hi(c, xh, gain)

            for k, g in enumerate([mlstm_norm[0], out_norm[0], ffn_norm[0], kv_norm, moba_norm[0]]):
                act.dma_start(grows[8 * k:8 * k + 8, :], g.rearrange("(k p) -> k p", p=P)).then_inc(c_here, 16)
            act.dma_start(graw[:], rows512(w_in[0])[:, :, 3072:3080]).then_inc(c_here, 16)
            act.dma_start(bif[:], b_if[0].rearrange("b h -> h b"), allow_slow_non_contiguous=True).then_inc(c_here, 16)
            act.dma_start(cs[:], rope.rearrange("(t p) c h -> p t c h", p=P)).then_inc(c_here, 16)
            act.dma_start(rt[:], rows512(router[0])).then_inc(c_late, 16)
            act.dma_start(gmoe[:], ffn_norm[1].partition_broadcast(P)).then_inc(c_late, 16)
            act.dma_start(gfin[:], final_norm.partition_broadcast(P)).then_inc(c_late, 16)
            norm(0, (x_here, 16 * TT))
            act.wait_ge(c_here, 16 * 8)
            act.activation(gh[:], graw[:], ACT.Copy).then_inc(g_hi, 1)
            split(0)
            act.wait_ge(gains_ready, 1)
            turn(0, 0)
            split(1)
            split(2)
            split(3)
            act.wait_ge(unit_done, 2)
            for h in range(MH):
                act.activation(qT[:, h, :], ps[h][:, 0:S], ACT.Copy).then_inc(q_out, 1)
            split(4)
            split(5)
            split(6)
            split(7)
            act.wait_ge(unit_done, 6)
            act.activation(v[:, 0, 0:2, 0:MV], ps[1][:].rearrange("p (h n) -> p h n", h=2), ACT.Copy).then_inc(va_out, 1)
            act.wait_ge(r_abs, 1)
            act.activation(rows[:, 3, :], rows[:, 2, :], ACT.Exp, scale=-1.0).then_inc(r_ln, 1)
            act.wait_ge(r_ln, 1)
            act.activation(rows[:, 4, :], rows[:, 3, :], ACT.Ln, bias=1.0).then_inc(r_ln, 1)
            split(8)
            split(9)
            act.wait_ge(unit_done, 8)
            act.activation(v[:, 0, 2:4, 0:MV], ps[3][:].rearrange("p (h n) -> p h n", h=2), ACT.Copy).then_inc(va_out, 1)
            split(10)
            act.wait_ge(z_cols, 1)
            act.activation(enm[:], cols[:, 2:4, :], ACT.Exp, scale=-1.0).then_inc(e_nm, 1)
            split(11)
            act.wait_ge(unit_done, 10)
            for t in range(TT):
                act.activation(sigo[:, t, 0:512], ps[5 + t][:], ACT.Sigmoid).then_inc(o_out, 1)
            split(12)
            for h in range(MH):
                act.wait_ge(d_done, h + 1)
                act.activation(E[:, h, :], E[:, h, :], ACT.Exp, scale=-1.0).then_inc(e_done, 1)
            split(13)
            act.wait_ge(unit_done, 12)
            for t in range(TT):
                act.activation(sigo[:, t, 512:1024], ps[1 + t][:], ACT.Sigmoid).then_inc(o_out, 1)
            split(14)
            for h in range(MH):
                for t in range(TT):
                    act.wait_ge(rd_done, 2 * h + t + 1)
                    b = PV_BANK[h][t]
                    act.activation(xr[:, t, h * MV:(h + 1) * MV], ps[b][:, 0:MV], ACT.Copy,
                                   scale=rden[:, t, h:h + 1]).then_inc(h_raw, 1)
                    act.activation(junk[:, t, h, :], ps[b][:, 0:MV], ACT.Square, scale=rden[:, t, h:h + 1],
                                   accum_out=hss[:, t, h:h + 1]).then_inc(h_raw, 1)
            act.wait_ge(h_var, 1)
            act.activation(hln[:], hvar[:], ACT.Ln).then_inc(h_ln, 1)
            act.wait_ge(h_ln, 1)
            act.activation(hrs[:], hln[:], ACT.Exp, scale=-0.5).then_inc(h_ln, 1)
            turn(1, 1)
            split(15)
            split(16)
            split(17)
            act.wait_ge(unit_done, 16)
            norm(1, (resid, 3))
            split(18)
            turn(2, 2)
            split(19)

            def silu_chunk(c, i):
                act.wait_ge(unit_done, RAW * c + (i + 1))
                act.activation(f_sg[:], ps[0][:].rearrange("p (t n) -> p t n", t=TT), ACT.Silu).then_inc(f_silu, 1)

            def ffn_hi(j):
                act.wait_ge(f_t, j)
                act.activation(f_hth[:], ps[2][:].rearrange("p (k s) -> p k s", k=2), ACT.Copy).then_inc(f_hi, 1)

            silu_chunk(0, U_FFN)
            with act.Fori(0, (NFC - 1) // 2) as it:
                for jj in range(2):
                    a = U_FFN + 2 + 3 * jj
                    split(a + 2, it)
                    ffn_hi(2 * it + (jj + 1))
                    split(a + 3, it)
                    act.wait_ge(f_mul, 2 * it + (jj + 1))
                    silu_chunk(it, a)
                    split(a + 4, it)
            ffn_hi(NFC)
            split(U_KV + 1)
            act.wait_ge(unit_done, U_KV)
            norm(2, (resid, 6))
            split(U_KV + 2)
            turn(3, 3)
            for c in range(KT):
                act.wait_ge(x_lo, 24 + c + 1)
                turn_hi(c, yh2, 4)
            split(U_KV + 3)
            act.wait_ge(unit_done, U_Q)
            for t in range(TT):
                act.activation(kvs[:, t, :], ps[t][:], ACT.Copy).then_inc(kv_out, 1)
            split(U_KV + 4)
            split(U_KV + 5)
            act.wait_ge(unit_done, U_Q + 2)
            act.activation(xr[:, 0, 0:512], ps[2][:], ACT.Copy).then_inc(aq_out, 1)
            split(U_KV + 6)
            act.wait_ge(k_t, 1)
            act.activation(akT[:], ps[6][:].rearrange("p (h s) -> p h s", h=KVH), ACT.Copy).then_inc(kt_out, 1)
            split(U_KV + 7)
            act.wait_ge(unit_done, U_Q + 4)
            act.activation(xr[:, 0, 512:1024], ps[4][:], ACT.Copy).then_inc(aq_out, 1)
            split(U_KV + 8)
            for b in (0, 2):
                act.wait_ge(q_t, b + 1)
                act.activation(aqT[:, 2 * b:2 * b + 2, :], ps[b][:].rearrange("p (h s) -> p h s", h=2), ACT.Copy
                               ).then_inc(qt_out, 1)
            for g in range(6):
                act.wait_ge(a_nb, g + 1)
                for h, t, ap in att_heads(g):
                    act.activation(ap, ap, ACT.Exp, bias=nb[:, t, h:h + 1], scale=HD ** -0.5,
                                   accum_out=sm[:, t, h:h + 1])\
                       .then_inc(a_exp, 1)
            for h in range(0, AH, 2):
                act.wait_ge(a_pt, h + 1)
                act.activation(pT[:, h, :], ps[ATT_BANK[h]][:, 0:384], ACT.Copy).then_inc(a_pto, 1)
            for h in range(AH):
                act.wait_ge(a_o, h + 1)
                act.activation(xh[:, h, :], ps[ATT_BANK[h]][:, 0:S], ACT.Copy).then_inc(a_hi, 1)
            split(U_O + 3)
            split(U_O + 4)
            split(U_O + 5)
            act.wait_ge(unit_done, U_MOE)
            norm(3, (resid, 11))
            for c in range(0, KT, 2):
                act.wait_ge(r_t, c + 1)
                act.activation(hnT[:, c, :], ps[c][:, 0:S], ACT.Copy).then_inc(r_tout, 1)
            for t in range(TT):
                act.wait_ge(hn_ready, t + 1)
                act.activation(xrh[:, t, :], xr[:, t, :], ACT.Copy).then_inc(hn_hi, 1)
            act.wait_ge(top_m, 1)
            act.activation(ee[:], dd[:], ACT.Exp).then_inc(top_e, 1)

            def expert_hi(q):
                for b in range(2):
                    act.wait_ge(moe_xg, 2 * q + (b + 1))
                    act.activation(xeh[:, 4 * b:4 * b + 4, :], ps[3 + b][:].rearrange("p (k s) -> p k s", k=4),
                                   ACT.Copy).then_inc(moe_xh, 1)

            expert_hi(0)

            def expert(q):
                c = (UE // RAW) * q

                def hidden_hi(j):
                    act.wait_ge(moe_t, NEC * q + (j + 1))
                    act.activation(hth[:], ps[2][:].rearrange("p (k s) -> p k s", k=4), ACT.Copy).then_inc(moe_hth, 1)

                for i in range(UE):
                    kind, j, half = UNITS[i - 1] if i else ("", 0, 0)
                    if (kind, half) == ("g", 1):
                        act.wait_ge(unit_done, UE * q + (U_MOE + i))
                        if j:
                            act.wait_ge(moe_h, NEC * q + j)
                        act.activation(sg[:], ps[0][:], ACT.Silu).then_inc(moe_silu, 1)
                        if j:
                            hidden_hi(j - 1)
                    if (kind, j, half) == ("u", 2, 1):
                        act.wait_ge(moe_pt, q + 1)
                        act.activation(phT[:], ps[7][:, 0:S], ACT.Copy).then_inc(moe_ptr, 1)
                    if i == UE - 2:
                        hidden_hi(NEC - 1)
                        expert_hi(q + 1)
                    split(U_MOE + i + 2, c)
                act.wait_ge(unit_done, UE * q + (U_MOE + UE))
                act.wait_ge(moe_w, q + 1)
                for b in range(2):
                    act.activation(ywh[:, 512 * b:512 * b + 512], ps[5 + b][:], ACT.Copy, scale=wcol[:, 0:1]
                                   ).then_inc(moe_yh, 1)

            with act.Fori(0, NE) as e:
                expert(e)
            act.wait_ge(flag_set, 1)
            over = act.value_load(flag[0:1, 0:1], min_val=0, max_val=S)
            with act.If(over > SLOTS):
                with act.Fori(0, NE) as e:
                    expert(e + NE)
            norm(4, (nrm_d, 25))

        @block.vector
        def _(dve):
            links = [0]

            def link(ins):
                links[0] += 1
                ins.then_inc(chain, 1)
                dve.wait_ge(chain, links[0])

            def split(i, c=0):
                dve.wait_ge(hi_split, RAW * c + (i + 1))
                dve.tensor_tensor(wl[:, i % SPL, :], raw[:, i % RAW, :], f32(wh[:, i % SPL, :]), ALU.subtract
                                  ).then_inc(lo_split, 1)

            def norm(i, tile1):
                if tile1 is not None:
                    dve.wait_ge(*tile1)
                dve.tensor_tensor_reduce(xr[:, 1, :], x[:, 1, :], x[:, 1, :], 1.0, 0.0, ALU.mult, ALU.add,
                                         ss[:, 1:2]).then_inc(nrm_d, 1)
                dve.wait_ge(nrm_a, 3 * i + 1)
                dve.wait_ge(nrm_d, 6 * i + 1)
                dve.tensor_scalar(var[:], ss[:], 1.0 / D, EPS, ALU.mult, ALU.add).then_inc(nrm_d, 1)
                dve.wait_ge(nrm_a, 3 * i + 3)
                newton(rs, var, t1, lambda k: (nrm_d, 6 * i + 2 + k))
                dve.wait_ge(nrm_d, 6 * i + 6)

            def newton(r, w, t, at):
                dve.tensor_tensor(t[:], r[:], r[:], ALU.mult).then_inc(at(1)[0], 1)
                dve.wait_ge(*at(1))
                dve.tensor_tensor(t[:], t[:], w[:], ALU.mult).then_inc(at(2)[0], 1)
                dve.wait_ge(*at(2))
                dve.tensor_scalar(t[:], t[:], -0.5, 1.5, ALU.mult, ALU.add).then_inc(at(3)[0], 1)
                dve.wait_ge(*at(3))
                dve.tensor_tensor(r[:], r[:], t[:], ALU.mult).then_inc(at(4)[0], 1)

            def scale_tile1():
                dve.tensor_scalar(xr[:, 1, :], x[:, 1, :], rs[:, 1:2], None, ALU.mult).then_inc(xr1, 1)

            def turn_lo(n, c, hi, lo, gain):
                dve.wait_ge(x_hi, n)
                dve.scalar_tensor_tensor(out=lo[:, c, :], in0=ps[c][:, 0:S],
                                         scalar=gains[:, 8 * gain + c:8 * gain + c + 1],
                                         in1=f32(hi[:, c, :]), op0=ALU.mult, op1=ALU.subtract).then_inc(x_lo, 1)

            def turn(k, gain):
                for c in range(KT):
                    turn_lo(8 * k + c + 1, c, xh, xl, gain)

            def add(t, n, bank):
                dve.tensor_tensor(x[:, t, 512 * n:512 * n + 512], x[:, t, 512 * n:512 * n + 512], ps[bank][:],
                                  ALU.add).then_inc(resid, 1)

            dve.memset(f32(zero[:]), 0.0).then_inc(v_one, 1)
            dve.memset(v[:, :, :, MV:MV + 1], 1.0).then_inc(v_one, 1)
            dve.wait_ge(gains_t, 1)
            dve.tensor_copy(gains[:], ps[7][:, 0:40]).then_inc(gains_ready, 1)
            norm(0, (x_here, 16 * TT))
            scale_tile1()
            dve.wait_ge(g_hi, 1)
            dve.tensor_tensor(gl[:], graw[:], f32(gh[:]), ALU.subtract).then_inc(g_lo, 1)
            split(0)
            dve.wait_ge(gains_ready, 1)
            turn(0, 0)
            split(1)
            split(2)
            split(3)
            split(4)
            dve.wait_ge(unit_done, 4)
            for h in range(MH):
                dve.tensor_copy(kT[:, h, :], ps[4 + h][:, 0:S]).then_inc(k_out, 1)
            split(5)
            dve.wait_ge(g_mm, 1)
            dve.tensor_copy(gsb[:], ps[0][:, 0:16].rearrange("p (t g) -> p t g", t=TT)).then_inc(g_sb, 1)
            split(6)
            dve.wait_ge(unit_done, 6)
            dve.tensor_copy(v[:, 1, 0:2, 0:MV], ps[2][:].rearrange("p (h n) -> p h n", h=2)).then_inc(vd_out, 1)
            dve.wait_ge(g_rows, 1)
            dve.tensor_scalar(rows[:, 0, :], ps[0][0:MH, 0:S], bif[:, 0:1], None, ALU.add).then_inc(r_done, 1)
            link(dve.tensor_scalar(rows[:, 1, :], ps[0][0:MH, S:2 * S], bif[:, 1:2], None, ALU.add))
            dve.scalar_tensor_tensor(out=rows[:, 2, :], in0=rows[:, 1, :], scalar=-1.0, in1=rows[:, 1, :],
                                     op0=ALU.mult, op1=ALU.max).then_inc(r_abs, 1)
            split(7)
            dve.wait_ge(r_ln, 2)
            link(dve.scalar_tensor_tensor(out=rows[:, 5, :], in0=rows[:, 1, :], scalar=0.0, in1=rows[:, 4, :],
                                          op0=ALU.min, op1=ALU.subtract))
            dve.wait_ge(pool_ready, POOL_ALL)
            link(dve.tensor_tensor_scan(rows[:, 6, :], onerow[:], rows[:, 5, :], 0.0, ALU.mult, ALU.add))
            dve.wait_ge(r_done, 1)
            link(dve.tensor_tensor(rows[:, 7, :], rows[:, 0, :], rows[:, 6, :], ALU.subtract))
            link(dve.tensor_tensor_scan(rows[:, 8, :], rows[:, 7, :], rows[:, 7, :], 0.0, ALU.max, ALU.max))
            dve.tensor_tensor(rows[:, 0, :], rows[:, 6, :], rows[:, 8, :], ALU.add).then_inc(r_done, 1)
            split(8)
            dve.wait_ge(unit_done, 8)
            dve.tensor_copy(v[:, 1, 2:4, 0:MV], ps[4][:].rearrange("p (h n) -> p h n", h=2)).then_inc(vd_out, 1)
            split(9)
            dve.wait_ge(z_t, 1)
            dve.tensor_copy(cols[:], ps[0][:, 0:16].rearrange("p (a h) -> p a h", a=4)).then_inc(z_cols, 1)
            split(10)
            split(11)
            dve.wait_ge(z_cols, 1)
            for h in range(MH):
                dve.wait_ge(m_bc, h // 2 + 1)
                mb = ps[7 * (h // 2)][:, S * (h % 2):S * (h % 2) + S]
                dve.scalar_tensor_tensor(out=E[:, h, 0:S], in0=mb, scalar=cols[:, 0, h:h + 1], in1=late_st[:],
                                         op0=ALU.subtract, op1=ALU.max)
                dve.scalar_tensor_tensor(out=E[:, h, S:S + P], in0=mb[:, P:S], scalar=cols[:, 1, h:h + 1],
                                         in1=late_st[:, 0:P], op0=ALU.subtract, op1=ALU.max).then_inc(d_done, 1)
            split(12)
            split(13)
            for h in range(MH):
                dve.wait_ge(s_mm, h + 1)
                dve.wait_ge(e_done, h + 1)
                dve.scalar_tensor_tensor(out=E[:, h, :], in0=ps[3 + h][:, 0:384], scalar=MK ** -0.5, in1=E[:, h, :],
                                         op0=ALU.mult, op1=ALU.mult).then_inc(p_done, 1)
            dve.wait_ge(e_nm, 1)
            for h in range(MH):
                for t in range(TT):
                    dve.wait_ge(pv_done, 2 * h + t + 1)
                    nq, d = ps[PV_BANK[h][t]][:, MV:MV + 1], den[:, t, h:h + 1]
                    link(dve.tensor_scalar(d, nq, -1.0, enm[:, t, h:h + 1], ALU.mult, ALU.max))
                    link(dve.tensor_scalar(d, nq, d, None, ALU.max))
                    dve.reciprocal(rden[:, t, h:h + 1], den[:, t, h:h + 1]).then_inc(rd_done, 1)
            dve.wait_ge(h_raw, 4 * MH)
            dve.tensor_scalar(hvar[:], hss[:], 1.0 / MV, EPS, ALU.mult, ALU.add).then_inc(h_var, 1)
            dve.wait_ge(h_var, 1)
            dve.wait_ge(h_ln, 2)
            newton(hrs, hvar, ht1, lambda k: (h_var, 1 + k))
            dve.wait_ge(h_var, 5)
            dve.wait_ge(o_out, 4)
            for t in range(TT):
                for h in range(MH):
                    xs = xr[:, t, h * MV:(h + 1) * MV]
                    dve.scalar_tensor_tensor(out=xs, in0=xs, scalar=hrs[:, t, h:h + 1],
                                             in1=sigo[:, t, h * MV:(h + 1) * MV], op0=ALU.mult, op1=ALU.mult
                                             ).then_inc(h_norm, 1)
            turn(1, 1)
            split(14)
            split(15)
            dve.wait_ge(unit_done, 14)
            for t in range(TT):
                add(t, 0, t)
            split(16)
            dve.wait_ge(unit_done, 16)
            for t in range(TT):
                add(t, 1, 2 + t)
            norm(1, (resid, 4))
            scale_tile1()
            split(17)
            split(18)
            turn(2, 2)
            split(19)

            def ffn_mul(j, up):
                dve.wait_ge(f_silu, j)
                dve.wait_ge(unit_done, up)
                dve.tensor_tensor(f_h[:], f_sg[:], ps[1][:].rearrange("p (t n) -> p t n", t=TT), ALU.mult
                                  ).then_inc(f_mul, 1)

            def ffn_lo(j):
                dve.wait_ge(f_hi, j)
                dve.tensor_tensor(f_htl[:], ps[2][:].rearrange("p (k s) -> p k s", k=2), f32(f_hth[:]), ALU.subtract
                                  ).then_inc(f_lo, 1)

            ffn_mul(1, U_FFN + 2)
            with dve.Fori(0, (NFC - 1) // 2) as it:
                for jj in range(2):
                    a = U_FFN + 2 + 3 * jj
                    split(a + 2, it)
                    ffn_lo(2 * it + (jj + 1))
                    split(a + 3, it)
                    ffn_mul(2 * it + (jj + 2), RAW * it + (a + 2))
                    split(a + 4, it)
            ffn_lo(NFC)
            split(U_KV + 1)
            dve.wait_ge(unit_done, U_KV)
            for t in range(TT):
                for n in range(2):
                    add(t, n, 4 + 2 * t + n)
            norm(2, (resid, 8))
            scale_tile1()
            split(U_KV + 2)
            turn(3, 3)
            for c in range(KT):
                turn_lo(32 + c + 1, c, yh2, yl2, 4)
            split(U_KV + 3)
            split(U_KV + 4)

            def rope_rotate(full, n_heads):
                a, b = full[:, :, :, 0:HALF], full[:, :, :, HALF:ROT]
                for g in range(TT):
                    cos = cs[:, g, 0, :].unsqueeze(1).to_broadcast([P, n_heads, HALF])
                    sin = cs[:, g, 1, :].unsqueeze(1).to_broadcast([P, n_heads, HALF])
                    w = [tmp[:, k, g, 0:n_heads, :] for k in range(4)]
                    dve.tensor_tensor(w[0], a[:, g], cos, ALU.mult)
                    dve.tensor_tensor(w[1], b[:, g], sin, ALU.mult)
                    dve.tensor_tensor(w[2], b[:, g], cos, ALU.mult)
                    link(dve.tensor_tensor(w[3], a[:, g], sin, ALU.mult))
                    dve.tensor_tensor(a[:, g], w[0], w[1], ALU.subtract)
                    last = dve.tensor_tensor(b[:, g], w[2], w[3], ALU.add)
                    if g == 0:
                        link(last)
                return last

            dve.wait_ge(kv_out, 2)
            rope_rotate(kvs[:, :, 0:KVH * HD].rearrange("p t (h d) -> p t h d", h=KVH), KVH).then_inc(k_rope, 1)
            split(U_KV + 5)
            dve.wait_ge(unit_done, U_Q + 2)
            dve.tensor_copy(xr[:, 1, 0:512], ps[3][:]).then_inc(aq_out, 1)
            split(U_KV + 6)
            split(U_KV + 7)
            dve.wait_ge(unit_done, U_Q + 4)
            dve.tensor_copy(xr[:, 1, 512:1024], ps[5][:]).then_inc(aq_out, 1)
            dve.wait_ge(aq_out, 4)
            rope_rotate(xr[:].rearrange("p t (h d) -> p t h d", h=AH), AH).then_inc(q_rope, 1)
            split(U_KV + 8)
            for b in (1, 3):
                dve.wait_ge(q_t, b + 1)
                dve.tensor_copy(aqT[:, 2 * b:2 * b + 2, :], ps[b][:].rearrange("p (h s) -> p h s", h=2)
                                ).then_inc(qt_out, 1)
            for g in range(6):
                heads, t, h0, n = ATT_GROUPS[g]
                dve.wait_ge(a_s, g + 1)
                mask = (late_ts[:] if t else late_ts[:, P:S]).unsqueeze(1).to_broadcast([P, heads, n])
                scg = sc[:, g, :].rearrange("p (h s) -> p h s", h=heads)
                link(dve.tensor_tensor(scg, ps[ATT_SBANK[g]][:].rearrange("p (h s) -> p h s", h=heads), mask, ALU.add))
                link(dve.tensor_reduce(mx[:, t, h0:h0 + heads], scg, AX, ALU.max))
                dve.tensor_scalar(nb[:, t, h0:h0 + heads], mx[:, t, h0:h0 + heads], -HD ** -0.5, None, ALU.mult
                                  ).then_inc(a_nb, 1)
            count = 0
            for g in range(6):
                heads, t, h0, n = ATT_GROUPS[g]
                count += heads
                dve.wait_ge(a_exp, count)
                link(dve.reciprocal(rsm[:, t, h0:h0 + heads], sm[:, t, h0:h0 + heads]))
                scg = sc[:, g, :].rearrange("p (h s) -> p h s", h=heads)
                dve.tensor_tensor(scg, scg, rsm[:, t, h0:h0 + heads].unsqueeze(2).to_broadcast([P, heads, n]), ALU.mult
                                  ).then_inc(a_p, 1)
            for h in range(1, AH, 2):
                dve.wait_ge(a_pt, h + 1)
                dve.tensor_copy(pT[:, h, :], ps[ATT_BANK[h]][:, 0:384]).then_inc(a_pto, 1)
            for h in range(AH):
                dve.wait_ge(a_hi, h + 1)
                dve.tensor_tensor(xl[:, h, :], ps[ATT_BANK[h]][:, 0:S], f32(xh[:, h, :]), ALU.subtract).then_inc(a_lo, 1)
            split(U_O + 3)
            dve.wait_ge(unit_done, U_O + 2)
            for t in range(TT):
                add(t, 0, 2 + t)
            split(U_O + 4)
            dve.wait_ge(unit_done, U_O + 4)
            for t in range(TT):
                add(t, 1, 4 + t)
            norm(3, (resid, 12))
            dve.wait_ge(c_late, 16 * 3)
            for t in range(TT):
                dve.scalar_tensor_tensor(out=xr[:, t, :], in0=x[:, t, :], scalar=rs[:, t:t + 1], in1=gmoe[:],
                                         op0=ALU.mult, op1=ALU.mult).then_inc(hn_ready, 1)
            split(U_O + 5)
            for c in range(1, KT, 2):
                dve.wait_ge(r_t, c + 1)
                dve.tensor_copy(hnT[:, c, :], ps[c][:, 0:S]).then_inc(r_tout, 1)
            dve.wait_ge(hn_hi, TT)
            dve.tensor_tensor(xrl[:], xr[:], f32(xrh[:]), ALU.subtract).then_inc(hn_lo, 1)
            dve.wait_ge(r_mm, 1)
            link(dve.tensor_copy(lg[:], ps[0][:, 0:2 * NE].rearrange("p (t e) -> p t e", t=TT)))

            def wide(col):
                return col[:].unsqueeze(2).to_broadcast([P, TT, NE])

            def first_max(src, m, i, oh):
                link(dve.tensor_reduce(m[:], src[:], AX, ALU.max))
                link(dve.tensor_tensor(eq[:], src[:], wide(m), ALU.is_equal))
                link(dve.scalar_tensor_tensor(out=cand[:], in0=eq[:], scalar=-float(NE), in1=iota_e8[:],
                                              op0=ALU.mult, op1=ALU.add))
                link(dve.tensor_reduce(i[:], cand[:], AX, ALU.min))
                link(dve.tensor_tensor(oh[:], iota_e[:], wide(i), ALU.is_equal))

            first_max(lg, m1, i1, oh1)
            link(dve.scalar_tensor_tensor(out=l2[:], in0=oh1[:], scalar=-3e38, in1=lg[:], op0=ALU.mult, op1=ALU.add))
            first_max(l2, m2, i2, oh2)
            dve.tensor_tensor(dd[:], m2[:], m1[:], ALU.subtract).then_inc(top_m, 1)
            dve.tensor_tensor(msk[:], oh1[:], oh2[:], ALU.add).then_inc(top_d, 1)
            dve.wait_ge(top_e, 1)
            link(dve.tensor_scalar(w2[:], ee[:], 1.0, None, ALU.add))
            link(dve.reciprocal(w1[:], w2[:]))
            link(dve.tensor_tensor(w2[:], ee[:], w1[:], ALU.mult))
            dve.tensor_tensor(cmb[:], oh1[:], wide(w1), ALU.mult)
            link(dve.tensor_tensor(cmb2[:], oh2[:], wide(w2), ALU.mult))
            link(dve.tensor_tensor(cmb[:], cmb[:], cmb2[:], ALU.add))
            cmb_et = cmb[:].rearrange("p t e -> p e t")
            link(dve.tensor_copy(cw[:, :, :, 0], cmb_et))
            dve.tensor_tensor(cw[:, :, :, 1], cmb_et, f32(cw[:, :, :, 0]), ALU.subtract)
            dve.wait_ge(rk_mm, 1)
            dve.wait_ge(top_d, 1)
            link(dve.scalar_tensor_tensor(out=eq[:], in0=ps[1][:, 0:2 * NE].rearrange("p (t e) -> p t e", t=TT),
                                          scalar=1.0, in1=msk[:], op0=ALU.add, op1=ALU.mult))
            link(dve.tensor_scalar(rank[:, 0:NE, :], eq[:].rearrange("p t e -> p e t"), -1.0, None, ALU.add))
            dve.tensor_scalar(rank[:, NE, :], rank[:, 0, :], -float(SLOTS), None, ALU.add)
            link(dve.tensor_reduce(most[:], ps[1][:, 2 * NE:3 * NE], AX, ALU.max))
            dve.tensor_copy(flag[:], most[0:1, :]).then_inc(flag_set, 1)

            def place(e):
                for t in range(TT):
                    last = dve.tensor_scalar(ph[:, t, :], iota_s[:], rank[:, e, t:t + 1], None, ALU.is_equal)
                return last

            def place_r(e):
                for t in range(TT):
                    last = dve.tensor_scalar(phr[:, t, :], iota_s[:], rank[:, e, t:t + 1], None, ALU.is_equal)
                return last

            place_r(0).then_inc(moe_p, 1)
            place(0).then_inc(moe_bank, 4)

            def expert_lo(q):
                for b in range(2):
                    dve.wait_ge(moe_xh, 2 * q + (b + 1))
                    dve.tensor_tensor(xel[:, 4 * b:4 * b + 4, :], ps[3 + b][:].rearrange("p (k s) -> p k s", k=4),
                                      f32(xeh[:, 4 * b:4 * b + 4, :]), ALU.subtract).then_inc(moe_xl, 1)

            expert_lo(0)

            def expert(q, e):
                c = (UE // RAW) * q

                def hidden_lo(j):
                    dve.wait_ge(moe_hth, NEC * q + (j + 1))
                    dve.tensor_tensor(htl[:], ps[2][:].rearrange("p (k s) -> p k s", k=4), f32(hth[:]), ALU.subtract
                                      ).then_inc(moe_htl, 1)

                for i in range(UE):
                    kind, j, half = UNITS[i - 1] if i else ("", 0, 0)
                    if (kind, half) == ("g", 1) and j:
                        hidden_lo(j - 1)
                    if (kind, half) == ("u", 1):
                        dve.wait_ge(unit_done, UE * q + (U_MOE + i))
                        dve.wait_ge(moe_silu, NEC * q + (j + 1))
                        dve.tensor_tensor(hh[:], sg[:], ps[1][:], ALU.mult).then_inc(moe_h, 1)
                    if (kind, j, half) == ("d", 1, 1):
                        dve.wait_ge(moe_ptr, q + 1)
                        dve.tensor_reduce(wcol[:], ps[7][:, S:S + 2], AX, ALU.add).then_inc(moe_w, 1)
                    if (kind, j, half) == ("d", 3, 1):
                        place(e + 1)
                        place_r(e + 1).then_inc(moe_p, 1)
                    if i == UE - 2:
                        hidden_lo(NEC - 1)
                        expert_lo(q + 1)
                    split(U_MOE + i + 2, c)
                for b in range(2):
                    dve.wait_ge(moe_yh, 2 * q + (b + 1))
                    dve.scalar_tensor_tensor(out=ywl[:, 512 * b:512 * b + 512], in0=ps[5 + b][:],
                                             scalar=wcol[:, 0:1], in1=f32(ywh[:, 512 * b:512 * b + 512]),
                                             op0=ALU.mult, op1=ALU.subtract).then_inc(moe_yl, 1)
                dve.wait_ge(moe_bank, 4 * q + 4)
                for k in range(4):
                    t, n = k // 2, k % 2
                    dve.wait_ge(moe_sc, 4 * q + (k + 1))
                    xs = x[:, t, 512 * n:512 * n + 512]
                    dve.tensor_tensor(xs, xs, ps[SC_BANK[k]][:], ALU.add).then_inc(moe_bank, 1)

            with dve.Fori(0, NE) as e:
                expert(e, e)
            dve.wait_ge(moe_bank, 4 * NE + 4)
            dve.wait_ge(flag_set, 1)
            over = dve.value_load(flag[0:1, 0:1], min_val=0, max_val=S)
            with dve.If(over > SLOTS):
                dve.tensor_scalar(rank[:], rank[:], -float(SLOTS), None, ALU.add).then_inc(flag_set, 1)
                dve.wait_ge(flag_set, 2)
                with dve.Fori(0, NE) as e:
                    expert(e + NE, e)
                dve.wait_ge(moe_bank, 8 * NE + 4)
            norm(4, None)
            for t in range(TT):
                dve.scalar_tensor_tensor(out=xr[:, t, :], in0=x[:, t, :], scalar=rs[:, t:t + 1], in1=gfin[:],
                                         op0=ALU.mult, op1=ALU.mult).then_inc(fin, 1)

        @block.tensor
        def _(pe):
            def mm3(bank, sh, sl, mh, ml, start, stop):
                pe.matmul(bank, sh, mh, start=start, stop=False)
                pe.matmul(bank, sh, ml, start=False, stop=False)
                return pe.matmul(bank, sl, mh, start=False, stop=stop)

            def project(i, half, banks, sh, sl, c=0):
                pe.wait_ge(lo_split, RAW * c + (i + 1))
                for t in range(TT):
                    for kk in range(4):
                        f = 4 * half + kk
                        last = mm3(ps[banks[t]][:], sh[:, f, t * P:(t + 1) * P], sl[:, f, t * P:(t + 1) * P],
                                   kn(wh, i % SPL)[:, kk, :], kn(wl, i % SPL)[:, kk, :],
                                   f == 0, f == KT - 1)
                last.then_inc(unit_done, 1)

            def turn(ready):
                for c in range(KT):
                    for t in range(TT):
                        last = pe.transpose(ps[c][:, t * P:(t + 1) * P], xr[:, t, c * P:(c + 1) * P], ident[:])
                    last.then_inc(ready, 1)

            pe.wait_ge(pool_ready, POOL_ALL)
            pe.wait_ge(c_here, 16 * 8)
            pe.transpose(ps[7][:, 0:40], grows[:], ident[0:40, 0:40]).then_inc(gains_t, 1)
            pe.wait_ge(gains_ready, 1)
            pe.wait_ge(xr0, 1)
            pe.wait_ge(xr1, 1)
            turn(x_turned)
            for m in range(2):
                for half in range(2):
                    i = U_IN + 2 * m + half
                    pe.wait_ge(lo_split, i + 1)
                    pe.wait_ge(x_lo, 4 * half + 4 if m == 0 else KT)
                    for h in range(MH):
                        for kk in range(4):
                            f, cols_h = 4 * half + kk, slice(h * MK, (h + 1) * MK)
                            last = mm3(ps[4 * m + h][:, 0:S], kn(wh, i % SPL)[:, kk, cols_h],
                                       kn(wl, i % SPL)[:, kk, cols_h], xh[:, f, :], xl[:, f, :], f == 0, f == KT - 1)
                    last.then_inc(unit_done, 1)
            pe.wait_ge(g_lo, 1)
            pe.wait_ge(q_out, 4)
            for t in range(TT):
                for f in range(KT):
                    last = mm3(ps[0][:, 8 * t:8 * t + 8], xh[:, f, t * P:(t + 1) * P], xl[:, f, t * P:(t + 1) * P],
                               gh[:, f, :], gl[:, f, :], f == 0, f == KT - 1)
            last.then_inc(g_mm, 1)
            for half in range(2):
                project(U_IN + 4 + half, half, (1, 2), xh, xl)
            pe.wait_ge(g_sb, 1)
            for g in range(2):
                for t in range(TT):
                    last = pe.transpose(ps[0][0:MH, g * S + t * P:g * S + (t + 1) * P],
                                        gsb[:, t, g * MH:(g + 1) * MH], ident[:])
            last.then_inc(g_rows, 1)
            pe.wait_ge(k_out, 4)
            for half in range(2):
                project(U_IN + 6 + half, half, (3, 4), xh, xl)
            pe.wait_ge(r_done, 2)
            for a, (row, t) in enumerate([(7, 0), (7, 1), (0, 0), (0, 1)]):
                last = pe.transpose(ps[0][:, 4 * a:4 * a + 4], rows[:, row, t * P:(t + 1) * P], ident[0:MH, 0:MH])
            last.then_inc(z_t, 1)
            for half in range(2):
                project(U_IN + 8 + half, half, (5, 6), xh, xl)
            pe.wait_ge(z_cols, 1)
            for h in range(MH):
                last = pe.matmul(ps[7 * (h // 2)][:, S * (h % 2):S * (h % 2) + S], sel[:, h, :], rows[:, 8, :],
                                 start=True, stop=True)
                if h % 2:
                    last.then_inc(m_bc, 1)
            pe.wait_ge(va_out, 1)
            pe.wait_ge(vd_out, 1)
            for half in range(2):
                project(U_IN + 10 + half, half, (1, 2), xh, xl)
            pe.wait_ge(va_out, 2)
            pe.wait_ge(vd_out, 2)
            for h in range(MH):
                if h == 2:
                    pe.wait_ge(o_out, 2)
                pe.matmul(ps[3 + h][:, 0:S], kT[:, h, 0:P], qT[:, h, :], start=True, stop=True)
                pe.matmul(ps[3 + h][:, S:S + P], kT[:, h, P:S], qT[:, h, P:S], start=True, stop=True
                          ).then_inc(s_mm, 1)
            pe.wait_ge(v_one, 2)
            for h in range(MH):
                pe.wait_ge(p_done, MH if h >= 2 else h + 1)
                if h == 0:
                    pe.wait_ge(d_done, MH)
                if h == 1:
                    pe.wait_ge(o_out, 4)
                pe.matmul(ps[PV_BANK[h][0]][:, 0:MV + 1], E[:, h, 0:P], v[:, 0, h, :], start=True, stop=True
                          ).then_inc(pv_done, 1)
                b = ps[PV_BANK[h][1]][:, 0:MV + 1]
                pe.matmul(b, E[:, h, P:S], v[:, 0, h, :], start=True, stop=False)
                pe.matmul(b, E[:, h, S:S + P], v[:, 1, h, :], start=False, stop=True).then_inc(pv_done, 1)
            pe.wait_ge(h_norm, 8)
            turn(x_turned)
            for n in range(2):
                for half in range(2):
                    pe.wait_ge(x_lo, 8 + 4 * half + 4 if n == 0 else 16)
                    project(U_OUT + 2 * n + half, half, (2 * n, 2 * n + 1), xh, xl)
            pe.wait_ge(xr0, 2)
            pe.wait_ge(xr1, 2)
            turn(x_turned)
            pe.wait_ge(x_lo, 24)

            def gate_up(i, bank, c=0):
                pe.wait_ge(lo_split, RAW * c + (i + 1))
                for t in range(TT):
                    for f in range(KT):
                        last = mm3(ps[bank][:, FC * t:FC * t + FC], xh[:, f, t * P:(t + 1) * P],
                                   xl[:, f, t * P:(t + 1) * P], kc(wh, i % SPL)[:, f, :], kc(wl, i % SPL)[:, f, :],
                                   f == 0, f == KT - 1)
                last.then_inc(unit_done, 1)

            gate_up(U_FFN, 0)
            gate_up(U_FFN + 1, 1)
            for t in range(TT):
                for n in range(2):
                    pe.matmul(ps[4 + 2 * t + n][:], zero[:, 0:P], zero[:], start=True, stop=False)

            def hidden(j):
                pe.wait_ge(f_mul, j)
                for k in range(2):
                    for t in range(TT):
                        last = pe.transpose(ps[2][:, k * S + t * P:k * S + (t + 1) * P], f_h[:, t, k * P:(k + 1) * P],
                                            ident[:])
                last.then_inc(f_t, 1)

            def down(i, j, c, stop):
                pe.wait_ge(lo_split, RAW * c + (i + 1))
                pe.wait_ge(f_lo, j)
                for t in range(TT):
                    for k in range(2):
                        for n in range(2):
                            last = mm3(ps[4 + 2 * t + n][:], f_hth[:, k, t * P:(t + 1) * P],
                                       f_htl[:, k, t * P:(t + 1) * P], fn(wh, i % SPL)[:, k, 512 * n:512 * n + 512],
                                       fn(wl, i % SPL)[:, k, 512 * n:512 * n + 512], False, stop and k == 1)
                last.then_inc(unit_done, 1)

            with pe.Fori(0, (NFC - 1) // 2) as it:
                for jj in range(2):
                    a = U_FFN + 2 + 3 * jj
                    pe.wait_ge(f_silu, 2 * it + (jj + 1))
                    gate_up(a, 0, it)
                    hidden(2 * it + (jj + 1))
                    gate_up(a + 1, 1, it)
                    down(a + 2, 2 * it + (jj + 1), it, False)
            hidden(NFC)
            down(U_KV - 1, NFC, 0, True)
            pe.wait_ge(xr0, 3)
            pe.wait_ge(xr1, 3)
            turn(x_turned)
            pe.wait_ge(x_lo, 40)
            for half in range(2):
                project(U_KV + half, half, (0, 1), xh, xl)
            for half in range(2):
                project(U_Q + half, half, (2, 3), yh2, yl2)
            pe.wait_ge(k_rope, 1)
            for g in range(KVH):
                for t in range(TT):
                    last = pe.transpose(ps[6][:, g * S + t * P:g * S + (t + 1) * P], kvs[:, t, g * HD:(g + 1) * HD],
                                        ident[:])
            last.then_inc(k_t, 1)
            for half in range(2):
                project(U_Q + 2 + half, half, (4, 5), yh2, yl2)
            pe.wait_ge(q_rope, 1)
            for h in range(AH):
                for t in range(TT):
                    last = pe.transpose(ps[h // 2][:, (h % 2) * S + t * P:(h % 2) * S + (t + 1) * P],
                                        xr[:, t, h * HD:(h + 1) * HD], ident[:])
                if h % 2:
                    last.then_inc(q_t, 1)
            pe.wait_ge(kt_out, 1)
            pe.wait_ge(qt_out, 4)
            for g in range(6):
                heads, t, h0, n = ATT_GROUPS[g]
                for a in range(heads):
                    h = h0 + a
                    last = pe.matmul(ps[ATT_SBANK[g]][:, a * n:(a + 1) * n], aqT[:, h, t * P:(t + 1) * P],
                                     akT[:, h // (AH // KVH), 0:n], start=True, stop=True)
                last.then_inc(a_s, 1)
            for h in range(AH):
                pe.wait_ge(a_p, 6)
                b = ps[ATT_BANK[h]]
                g0, a0 = 4 + h // 4, (h % 4) * P
                g1, a1 = h // 2, (h % 2) * S
                pe.transpose(b[:, 0:P], sc[:, g0, a0:a0 + P], ident[:])
                pe.transpose(b[:, P:S], sc[:, g1, a1:a1 + P], ident[:])
                pe.transpose(b[:, S:S + P], sc[:, g1, a1 + P:a1 + S], ident[:]).then_inc(a_pt, 1)
            for h in range(AH):
                pe.wait_ge(a_pto, AH)
                b = ps[ATT_BANK[h]]
                g = KVH * HD + (h // (AH // KVH)) * HD
                pe.matmul(b[:, 0:S], kvs[:, 0, g:g + HD], pT[:, h, 0:S], start=True, stop=False)
                pe.matmul(b[:, P:S], kvs[:, 1, g:g + HD], pT[:, h, S:S + P], start=False, stop=True).then_inc(a_o, 1)
            for n in range(2):
                for half in range(2):
                    pe.wait_ge(a_lo, 4 * half + 4 if n == 0 else AH)
                    project(U_O + 2 * n + half, half, (2 + 2 * n, 3 + 2 * n), xh, xl)
            pe.wait_ge(hn_ready, TT)
            turn(r_t)
            pe.wait_ge(r_tout, KT)
            for t in range(TT):
                for f in range(KT):
                    last = pe.matmul(ps[0][:, NE * t:NE * t + NE], hnT[:, f, t * P:(t + 1) * P], rt[:, f, :],
                                     start=(f == 0), stop=(f == KT - 1))
            last.then_inc(r_mm, 1)
            pe.wait_ge(top_d, 1)
            pe.matmul(ps[1][:, 0:NE], before[:], msk[:, 0, :], start=True, stop=True)
            pe.matmul(ps[1][:, NE:2 * NE], ones[:], msk[:, 0, :], start=True, stop=False)
            pe.matmul(ps[1][:, NE:2 * NE], before[:], msk[:, 1, :], start=False, stop=True)
            pe.matmul(ps[1][:, 2 * NE:3 * NE], ones[:], msk[:, 0, :], start=True, stop=False)
            pe.matmul(ps[1][:, 2 * NE:3 * NE], ones[:], msk[:, 1, :], start=False, stop=True).then_inc(rk_mm, 1)
            pe.wait_ge(hn_lo, 1)

            def gather():
                for b in range(2):
                    for kk in range(4):
                        f = 4 * b + kk
                        for t in range(TT):
                            for k, src in enumerate((xrh, xrl)):
                                last = pe.matmul(ps[3 + b][:, kk * SLOTS:(kk + 1) * SLOTS],
                                                 src[:, t, f * P:(f + 1) * P], phr[:, t, :],
                                                 start=(t == 0 and k == 0), stop=(t == 1 and k == 1))
                    last.then_inc(moe_xg, 1)

            pe.wait_ge(moe_p, 1)
            gather()

            def expert(q, e):
                def hidden(j):
                    pe.wait_ge(moe_h, NEC * q + (j + 1))
                    for k in range(4):
                        last = pe.transpose(ps[2][:, k * P:(k + 1) * P], hh[:, k * P:(k + 1) * P], ident[:])
                    last.then_inc(moe_t, 1)

                pe.wait_ge(moe_xl, 2 * q + 2)
                for i in range(UE):
                    kind, j, half = UNITS[i]
                    n = U_MOE + i
                    if i == UE - 2:
                        hidden(NEC - 1)
                        pe.wait_ge(moe_p, q + 2)
                        pe.wait_ge(moe_bank, 4 * q + 4)
                        gather()
                    if (kind, half) == ("g", 0) and j:
                        pe.wait_ge(moe_silu, NEC * q + j)
                    pe.wait_ge(lo_split, UE * q + (n + 1))
                    if kind in "gu":
                        for kk in range(4):
                            f = 4 * half + kk
                            last = mm3(ps["gu".index(kind)][:], xeh[:, f, :], xel[:, f, :], kn(wh, n % SPL)[:, kk, :],
                                       kn(wl, n % SPL)[:, kk, :], f == 0, f == KT - 1)
                    else:
                        pe.wait_ge(moe_htl, NEC * q + (j + 1))
                        for kk in range(2):
                            f = 2 * half + kk
                            for b in range(2):
                                last = mm3(ps[5 + b][:], hth[:, f, :], htl[:, f, :],
                                           fn(wh, n % SPL)[:, kk, 512 * b:512 * b + 512],
                                           fn(wl, n % SPL)[:, kk, 512 * b:512 * b + 512],
                                           j == 0 and f == 0, j == NEC - 1 and f == 3)
                    last.then_inc(unit_done, 1)
                    if (kind, half) == ("g", 1) and j:
                        hidden(j - 1)
                    if (kind, j, half) == ("u", 2, 1):
                        pe.wait_ge(moe_bank, 4 * q + 4)
                        for t in range(TT):
                            pe.transpose(ps[7][:, t * P:(t + 1) * P], ph[:, t, :], ident[:])
                        for t in range(TT):
                            last = pe.matmul(ps[7][:, S:S + 2], phr[:, t, :], cw[:, e, t, :], start=(t == 0),
                                             stop=(t == 1))
                        last.then_inc(moe_pt, 1)
                pe.wait_ge(moe_yl, 2 * q + 2)
                pe.wait_ge(moe_ptr, q + 1)
                for k in range(4):
                    t, n = k // 2, k % 2
                    if k == 3:
                        pe.wait_ge(moe_bank, 4 * q + 5)
                    pe.matmul(ps[SC_BANK[k]][:], phT[:, t * P:(t + 1) * P], ywh[:, 512 * n:512 * n + 512],
                              start=True, stop=False)
                    pe.matmul(ps[SC_BANK[k]][:], phT[:, t * P:(t + 1) * P], ywl[:, 512 * n:512 * n + 512],
                              start=False, stop=True).then_inc(moe_sc, 1)

            with pe.Fori(0, NE) as e:
                expert(e, e)
            pe.wait_ge(flag_set, 1)
            over = pe.value_load(flag[0:1, 0:1], min_val=0, max_val=S)
            with pe.If(over > SLOTS):
                with pe.Fori(0, NE) as e:
                    expert(e + NE, e)


_INS = ['x', 'mlstm_norm', 'mlstm_w_in', 'mlstm_b_if', 'mlstm_out_norm', 'mlstm_w_out', 'ffn_norm', 'dense_w_gu',
        'dense_w_down', 'moe_router', 'moe_w_gu', 'moe_w_down', 'kv_norm', 'kv_w', 'moba_norm', 'moba_w_q',
        'moba_w_o', 'final_norm']


def rope_table():
    import numpy as _np

    freq = _np.float32(500000.0) ** (-_np.arange(0, ROT, 2, dtype=_np.float32) / _np.float32(ROT))
    angle = _np.arange(S, dtype=_np.float32)[:, None] * freq[None, :]
    return _np.stack([_np.cos(angle), _np.sin(angle)], axis=1).astype(_np.float32)


def kernel(**inputs):
    import numpy as _np
    import concourse.bacc as _bacc
    from concourse import mybir as _mybir
    from concourse.bass_utils import run_bass_kernel_spmd as _run

    nc = _bacc.Bacc("TRN2", target_bir_lowering=False, num_devices=1)
    arrays, args = {}, []
    for name in _INS + ['rope']:
        a = _np.ascontiguousarray(inputs[name]) if name != 'rope' else rope_table()
        arrays[f"in_{name}_dram"] = a
        args.append(nc.dram_tensor(f"in_{name}_dram", a.shape, _mybir.dt.from_np(a.dtype), kind="ExternalInput").ap())
    args.append(nc.dram_tensor("out_0_dram", (1, S, D), F32, kind="ExternalOutput").ap())
    yoco_block(nc, *args)
    r = _run(nc, [arrays], core_ids=[0])
    return r.results[0]["out_0_dram"]
```

```python
from contextlib import ExitStack

import concourse.bass as bass
from concourse import mybir

ALU = mybir.AluOpType
ACT = mybir.ActivationFunctionType
F32 = mybir.dt.float32
F32R = mybir.dt.float32r
I32 = mybir.dt.int32
AX = mybir.AxisListType.X

P = 128
EPS = 1e-6
FAR = 1e30

D = 1024
S = 256
TT = S // P
KT = D // P
MH, MK, MV = 4, 128, 256
AH, KVH, HD = 8, 2, 128
ROT = HD // 4
HALF = ROT // 2
FF = 2816
FC = 256
NFC = FF // FC
NE = 8
FE = 3584
EC = 512
NEC = FE // EC
SLOTS = 128

UNIT = 2048
RAW = 6
SPL = 3
U_IN = 0
U_OUT = U_IN + 12
U_FFN = U_OUT + 4
U_KV = U_FFN + 3 * NFC
U_Q = U_KV + 2
U_O = U_Q + 4
U_MOE = U_O + 4
UE = 6 * NEC
assert UE % RAW == 0 and RAW % SPL == 0


def expert_units():
    order = []
    for j in range(NEC):
        order += [("g", j, 0), ("g", j, 1), ("u", j, 0), ("u", j, 1)]
        if j:
            order += [("d", j - 1, 0), ("d", j - 1, 1)]
    return order + [("d", NEC - 1, 0), ("d", NEC - 1, 1)]


UNITS = expert_units()

TURN_BANKS = [(4, 5, 6, 7), (0, 1, 2, 3), (0, 1, 2, 3), (4, 5, 0, 1), (6, 7, 0, 1)]
GATE_BANK, UP_BANK, HT_BANK = 4, 0, 1
Y_BANK = [(2, 6), (3, 7)]
PV_BANK = [(0, 7), (1, 2), (3, 4), (5, 6)]
ATT_GROUPS = [(2, 1, 0, S), (2, 1, 2, S), (4, 0, 0, P), (2, 1, 4, S), (2, 1, 6, S), (4, 0, 4, P)]
ATT_SBANK = [5, 6, 7, 0, 1, 6]
QT_BANK = [2, 3, 6, 7]
ATT_BANK = [2, 3, 4, 5, 7, 0, 1, 6]
SC_BANK = [7, 3, 4, 7]
POOL_ALL = 9


def yoco_block(nc, x_in, mlstm_norm, w_in, b_if, out_norm, w_out, ffn_norm, w_gu, w_down, router,
               e_gu, e_down, kv_norm, kv_w, moba_norm, w_q, w_o, final_norm, rope, out):
    with ExitStack() as ctx:
        def sem(name):
            return ctx.enter_context(nc.semaphore(name))

        def keep(name, shape, dt=F32):
            return ctx.enter_context(nc.sbuf_tensor(name, shape, dt))

        raw = keep("raw", [P, RAW, UNIT])
        wh = keep("wh", [P, SPL, UNIT], F32R)
        wl = keep("wl", [P, SPL, UNIT], F32R)
        x = keep("x", [P, TT, D])
        xr = keep("xr", [P, TT, D])
        xh = keep("xh", [P, KT, S], F32R)
        xl = keep("xl", [P, KT, S], F32R)
        ident = keep("ident", [P, P])
        ones = keep("ones", [P, P])
        onerow = keep("onerow", [MH, S])
        zero = keep("zero", [P, 512], F32R)
        before = keep("before", [P, P])
        late_st = keep("late_st", [P, S])
        late_ts = keep("late_ts", [P, S])
        iota_s = keep("iota_s", [P, SLOTS])
        iota_e = keep("iota_e", [P, TT, NE])
        iota_e8 = keep("iota_e8", [P, TT, NE])
        sel = keep("sel", [MH, MH, P])
        grows = keep("grows", [48, P])
        gains = keep("gains", [P, 48])
        cs = keep("cs", [P, TT, 2, HALF])
        bif = keep("bif", [MH, 2])
        ss = keep("ss", [P, TT])
        eps = keep("eps", [P, 1])
        warm = keep("warm", [P, 1])
        rms = keep("rms", [P, TT])
        var = keep("var", [P, TT])
        r0 = keep("r0", [P, TT])
        t1 = keep("t1", [P, TT])
        rs = keep("rs", [P, TT])
        rt = keep("rt", [P, KT, NE])
        gfin = keep("gfin", [P, D])
        gmoe = keep("gmoe", [P, D])

        phase = ExitStack()

        def sb(name, shape, dt=F32):
            return phase.enter_context(nc.sbuf_tensor(name, shape, dt))

        graw = sb("graw", [P, KT, 2 * MH])
        gh = sb("gh", [P, KT, 2 * MH], F32R)
        gl = sb("gl", [P, KT, 2 * MH], F32R)
        qT = sb("qT", [P, MH, S])
        kT = sb("kT", [P, MH, S])
        v = sb("v", [P, TT, MH, MV + 1])
        sigo = sb("sigo", [P, TT, D])
        gsb = sb("gsb", [P, TT, 2 * MH])
        rows = sb("rows", [MH, 9, S])
        cols = sb("cols", [P, 4, MH])
        enm = sb("enm", [P, TT, MH])
        E = sb("E", [P, MH, 384])
        den = sb("den", [P, TT, MH])
        rden = sb("rden", [P, TT, MH])
        hss = sb("hss", [P, TT, MH])
        hrms = sb("hrms", [P, TT, MH])
        hrs = sb("hrs", [P, TT, MH])
        hvar = sb("hvar", [P, TT, MH])
        hr0 = sb("hr0", [P, TT, MH])
        ht1 = sb("ht1", [P, TT, MH])
        nqs = sb("nqs", [P, TT, MH])
        junk = sb("junk", [P, TT, MH, MV])
        phase.close()
        f_sg = sb("f_sg", [P, TT, FC])
        f_h = sb("f_h", [P, TT, FC])
        f_hth = sb("f_hth", [P, 2, S], F32R)
        f_htl = sb("f_htl", [P, 2, S], F32R)
        phase.close()
        yh2 = sb("yh2", [P, KT, S], F32R)
        yl2 = sb("yl2", [P, KT, S], F32R)
        kvs = sb("kvs", [P, TT, 2 * KVH * HD])
        aqT = sb("aqT", [P, AH, S])
        akT = sb("akT", [P, KVH, S])
        tmp = sb("tmp", [P, 4, TT, AH, HALF])
        sc = sb("sc", [P, 6, 512])
        mx = sb("mx", [P, TT, AH])
        nb = sb("nb", [P, TT, AH])
        sm = sb("sm", [P, TT, AH])
        rsm = sb("rsm", [P, TT, AH])
        pT = sb("pT", [P, AH, 384])
        phase.close()
        hnT = sb("hnT", [P, KT, S])
        xrh = sb("xrh", [P, TT, D], F32R)
        xrl = sb("xrl", [P, TT, D], F32R)
        xeh = sb("xeh", [P, KT, SLOTS], F32R)
        xel = sb("xel", [P, KT, SLOTS], F32R)
        ph = sb("ph", [P, TT, SLOTS])
        phr = sb("phr", [P, TT, SLOTS], F32R)
        phT = sb("phT", [SLOTS, S], F32R)
        sg = sb("sg", [P, EC])
        hh = sb("hh", [P, EC])
        hth = sb("hth", [P, 4, SLOTS], F32R)
        htl = sb("htl", [P, 4, SLOTS], F32R)
        ywh = sb("ywh", [SLOTS, D], F32R)
        ywl = sb("ywl", [SLOTS, D], F32R)
        wcol = sb("wcol", [SLOTS, 1])
        lg = sb("lg", [P, TT, NE])
        l2 = sb("l2", [P, TT, NE])
        eq = sb("eq", [P, TT, NE])
        cand = sb("cand", [P, TT, NE])
        oh1 = sb("oh1", [P, TT, NE])
        oh2 = sb("oh2", [P, TT, NE])
        m1 = sb("m1", [P, TT])
        m2 = sb("m2", [P, TT])
        i1 = sb("i1", [P, TT])
        i2 = sb("i2", [P, TT])
        dd = sb("dd", [P, TT])
        ee = sb("ee", [P, TT])
        w1 = sb("w1", [P, TT])
        w2 = sb("w2", [P, TT])
        msk = sb("msk", [P, TT, NE])
        cmb = sb("cmb", [P, TT, NE])
        cmb2 = sb("cmb2", [P, TT, NE])
        rank = sb("rank", [P, NE + 1, TT])
        cw = sb("cw", [P, NE, TT, 2], F32R)
        most = sb("most", [P, 1])
        flag = sb("flag", [1, 1], I32)
        phase.close()

        ps = [ctx.enter_context(nc.psum_tensor(f"ps{b}", [P, 512], F32)) for b in range(8)]

        raw_full = [sem(f"raw_full{i}") for i in range(RAW)]
        hi_split = sem("hi_split")
        lo_split = sem("lo_split")
        unit_done = sem("unit_done")
        x_here = sem("x_here")
        gn_here = sem("gn_here")
        c_here = sem("c_here")
        c_late = sem("c_late")
        pool_ready = sem("pool_ready")
        pool_zero = sem("pool_zero")
        gains_t = sem("gains_t")
        gains_ready = sem("gains_ready")
        nrm_a = sem("nrm_a")
        nrm_d = sem("nrm_d")
        xr0 = sem("xr0")
        xr1 = sem("xr1")
        x_turned = sem("x_turned")
        x_hi = sem("x_hi")
        x_lo = sem("x_lo")
        resid = sem("resid")
        q_out = sem("q_out")
        k_out = sem("k_out")
        va_out = sem("va_out")
        vd_out = sem("vd_out")
        v_one = sem("v_one")
        o_out = sem("o_out")
        g_hi = sem("g_hi")
        g_lo = sem("g_lo")
        g_mm = sem("g_mm")
        g_sb = sem("g_sb")
        g_rows = sem("g_rows")
        chain = sem("chain")
        r_abs = sem("r_abs")
        r_ln = sem("r_ln")
        r_done = sem("r_done")
        z_t = sem("z_t")
        z_cols = sem("z_cols")
        e_nm = sem("e_nm")
        m_bc = sem("m_bc")
        d_done = sem("d_done")
        e_done = sem("e_done")
        s_mm = sem("s_mm")
        p_done = sem("p_done")
        pv_done = sem("pv_done")
        rd_done = sem("rd_done")
        h_raw = sem("h_raw")
        h_rms = sem("h_rms")
        h_rs = sem("h_rs")
        h_norm = sem("h_norm")
        y_half = sem("y_half")
        f_silu = sem("f_silu")
        f_mul = sem("f_mul")
        f_t = sem("f_t")
        f_hi = sem("f_hi")
        f_lo = sem("f_lo")
        kv_out = sem("kv_out")
        aq_out = sem("aq_out")
        k_rope = sem("k_rope")
        q_rope = sem("q_rope")
        k_t = sem("k_t")
        q_t = sem("q_t")
        kt_out = sem("kt_out")
        qt_out = sem("qt_out")
        a_s = sem("a_s")
        a_sc = sem("a_sc")
        a_nb = sem("a_nb")
        a_exp = sem("a_exp")
        a_p = sem("a_p")
        a_pt = sem("a_pt")
        a_pto = sem("a_pto")
        a_o = sem("a_o")
        a_hi = sem("a_hi")
        a_lo = sem("a_lo")
        hn_ready = sem("hn_ready")
        hn_hi = sem("hn_hi")
        hn_lo = sem("hn_lo")
        r_tout = sem("r_tout")
        r_mm = sem("r_mm")
        top_d = sem("top_d")
        top_e = sem("top_e")
        top_m = sem("top_m")
        rk_mm = sem("rk_mm")
        flag_set = sem("flag_set")
        moe_bank = sem("moe_bank")
        moe_p = sem("moe_p")
        moe_xg = sem("moe_xg")
        moe_xh = sem("moe_xh")
        moe_xl = sem("moe_xl")
        moe_silu = sem("moe_silu")
        moe_h = sem("moe_h")
        moe_t = sem("moe_t")
        moe_hth = sem("moe_hth")
        moe_htl = sem("moe_htl")
        moe_pt = sem("moe_pt")
        moe_ptr = sem("moe_ptr")
        moe_w = sem("moe_w")
        moe_yh = sem("moe_yh")
        moe_yl = sem("moe_yl")
        moe_sc = sem("moe_sc")
        fin = sem("fin")
        stored = sem("stored")

        x_v = x_in[0].rearrange("(t p) d -> p t d", p=P)
        out_v = out[0].rearrange("(t p) d -> p t d", p=P)

        def rows512(w):
            return w.rearrange("(k p) n -> p k n", p=P)

        def kn(buf, slot):
            return buf[:, slot, :].rearrange("p (k n) -> p k n", k=4)

        def kc(buf, slot):
            return buf[:, slot, :].rearrange("p (k n) -> p k n", k=8)

        def fn(buf, slot):
            return buf[:, slot, :].rearrange("p (k n) -> p k n", k=2)

        def f32(ap):
            return ap.bitcast(F32)

        def att_heads(g):
            heads, t, h0, n = ATT_GROUPS[g]
            return [(h0 + a, t, sc[:, g, a * n:(a + 1) * n]) for a in range(heads)]

        block = ctx.enter_context(nc.Block())

        @block.sync
        def _(sp):
            def load(n, i, dst, src, after=None):
                if after is not None:
                    sp.wait_ge(lo_split, after)
                sp.dma_start(dst, src).then_inc(raw_full[i % RAW], 16)

            def free(n):
                return n - RAW + 1 if n >= RAW else None

            def load_kn(n, w, col, half, step=None):
                src = rows512(w)[:, 4 * half:4 * half + 4, col:col + 512]
                load(n, n, kn(raw, n % RAW), src, free(n))

            for t in range(TT):
                sp.dma_start(x[:, t, :], x_v[:, t, :]).then_inc(x_here, 16)
            for k, g in enumerate([mlstm_norm[0], out_norm[0], ffn_norm[0]]):
                sp.dma_start(grows[8 * k:8 * k + 8, :], g.rearrange("(k p) -> k p", p=P)).then_inc(gn_here, 16)
            sp.wait_ge(gn_here, 16 * 6)
            for j in range(6):
                for half in range(2):
                    load_kn(U_IN + 2 * j + half, w_in[0], 512 * j, half)
            for j in range(2):
                for half in range(2):
                    load_kn(U_OUT + 2 * j + half, w_out[0], 512 * j, half)

            def ffn_gu(i, after, col):
                sp.wait_ge(lo_split, after)
                sp.dma_start(kc(raw, i % RAW), rows512(w_gu[0])[:, :, bass.ds(col, FC)]
                             ).then_inc(raw_full[i % RAW], 16)

            def ffn_down(i, after, row):
                src = w_down[0][bass.ds(row, FC), :].rearrange("(k p) n -> p k n", p=P)
                sp.wait_ge(lo_split, after)
                sp.dma_start(fn(raw, i % RAW), src).then_inc(raw_full[i % RAW], 16)

            ffn_gu(U_FFN, U_FFN - RAW + 1, 0)
            ffn_gu(U_FFN + 1, U_FFN + 1 - RAW + 1, FF)
            with sp.Fori(0, (NFC - 1) // 2) as it:
                for jj in range(2):
                    i = U_FFN + 2 + 3 * jj
                    ffn_gu(i, 6 * it + (i - RAW + 1), (2 * it + (jj + 1)) * FC)
                    ffn_gu(i + 1, 6 * it + (i + 1 - RAW + 1), (2 * it + (jj + 1)) * FC + FF)
                    ffn_down(i + 2, 6 * it + (i + 2 - RAW + 1), (2 * it + jj) * FC)
            ffn_down(U_KV - 1, U_KV - 1 - RAW + 1, (NFC - 1) * FC)

            for half in range(2):
                load_kn(U_KV + half, kv_w, 0, half)
            for j in range(2):
                for half in range(2):
                    load_kn(U_Q + 2 * j + half, w_q[0], 512 * j, half)
            for half in range(2):
                for j in range(2):
                    load_kn(U_O + 2 * half + j, w_o[0], 512 * j, half)

            def load_expert(e, q, first, last):
                gu = e_gu[0].rearrange("e (k p) n -> e p k n", p=P)
                dn = e_down[0].rearrange("e (k p) n -> e p k n", p=P)
                for i in range(first, last):
                    kind, j, half = UNITS[i]
                    n = U_MOE + i
                    if kind == "d":
                        k = 4 * j + 2 * half
                        dst, src = fn(raw, n % RAW), dn[e, :, k:k + 2, :]
                    else:
                        c = EC * j + (FE if kind == "u" else 0)
                        dst, src = kn(raw, n % RAW), gu[e, :, 4 * half:4 * half + 4, c:c + EC]
                    sp.wait_ge(lo_split, q * UE + (n - RAW + 1))
                    sp.dma_start(dst, src).then_inc(raw_full[n % RAW], 16)

            with sp.Fori(0, NE) as e:
                load_expert(e, e, 0, UE)
            load_expert(0, NE, 0, 2)
            sp.wait_ge(flag_set, 1)
            over = sp.value_load(flag[0:1, 0:1], min_val=0, max_val=S)
            with sp.If(over > SLOTS):
                load_expert(0, NE, 2, UE)
                with sp.Fori(1, NE) as e:
                    load_expert(e, e + NE, 0, UE)
                load_expert(0, 2 * NE, 0, 2)
            for t in range(TT):
                sp.wait_ge(fin, t + 1)
                sp.dma_start(out_v[:, t, :], xr[:, t, :]).then_inc(stored, 16)
            sp.wait_ge(stored, 16 * TT)

        @block.gpsimd
        def _(pool):
            pool.memset(ident[:], 0.0).then_inc(pool_zero, 1)
            pool.memset(ones[:], 1.0).then_inc(pool_zero, 1)
            pool.memset(late_st[:], 0.0).then_inc(pool_zero, 1)
            pool.memset(late_ts[:], 0.0).then_inc(pool_zero, 1)
            pool.memset(sel[:], 0.0).then_inc(pool_zero, 1)
            pool.memset(onerow[:], 1.0).then_inc(pool_ready, 1)
            pool.wait_ge(pool_zero, 5)
            pool.affine_select(out=ident[:], in_=ident[:], compare_op=ALU.not_equal, fill=1.0, base=0,
                               pattern=[[-1, P]], channel_multiplier=1).then_inc(pool_ready, 1)
            pool.affine_select(out=before[:], in_=ones[:], compare_op=ALU.is_gt, fill=0.0, base=0,
                               pattern=[[1, P]], channel_multiplier=-1).then_inc(pool_ready, 1)
            pool.affine_select(out=late_st[:, 0:P], in_=late_st[:, 0:P], compare_op=ALU.is_ge, fill=FAR,
                               base=0, pattern=[[1, P]], channel_multiplier=-1).then_inc(pool_ready, 1)
            pool.affine_select(out=late_ts[:, P:S], in_=late_ts[:, P:S], compare_op=ALU.is_ge, fill=-FAR,
                               base=0, pattern=[[-1, P]], channel_multiplier=1).then_inc(pool_ready, 1)
            pool.affine_select(out=sel[:], in_=sel[:], compare_op=ALU.not_equal, fill=1.0, base=0,
                               pattern=[[-1, MH], [0, P]], channel_multiplier=1).then_inc(pool_ready, 1)
            pool.iota(iota_s[:], pattern=[[1, SLOTS]], base=0, channel_multiplier=0,
                      allow_small_or_imprecise_dtypes=True).then_inc(pool_ready, 1)
            pool.iota(iota_e[:], pattern=[[0, TT], [1, NE]], base=0, channel_multiplier=0,
                      allow_small_or_imprecise_dtypes=True).then_inc(pool_ready, 1)
            pool.iota(iota_e8[:], pattern=[[0, TT], [1, NE]], base=NE, channel_multiplier=0,
                      allow_small_or_imprecise_dtypes=True).then_inc(pool_ready, 1)

        @block.scalar
        def _(act):
            def split(i, c=0):
                act.wait_ge(raw_full[i % RAW], 16 * c + 16 * (i // RAW + 1))
                if i >= SPL:
                    act.wait_ge(unit_done, RAW * c + (i - SPL + 1))
                act.activation(wh[:, i % SPL, :], raw[:, i % RAW, :], ACT.Copy).then_inc(hi_split, 1)

            def norm_square(i, tile0):
                act.wait_ge(*tile0)
                act.activation(xr[:, 0, :], x[:, 0, :], ACT.Square, accum_out=ss[:, 0:1]).then_inc(nrm_a, 1)

            def norm_root(i):
                act.wait_ge(nrm_d, 6 * i + 1)
                act.wait_ge(nrm_a, 2 * i + 1)
                act.activation(rms[:], ss[:], ACT.Sqrt, scale=1.0 / D, bias=eps[:, 0:1]).then_inc(nrm_a, 1)

            def turn_hi(k, c, dst, gain):
                act.activation(dst[:, c, :], ps[TURN_BANKS[k][c // 2]][:, c % 2 * S:c % 2 * S + S], ACT.Copy,
                               scale=gains[:, 8 * gain + c:8 * gain + c + 1]).then_inc(x_hi, 1)

            def turn(k, gain, pairs):
                for m in pairs:
                    act.wait_ge(x_turned, 4 * k + m + 1)
                    turn_hi(k, 2 * m, xh, gain)
                    turn_hi(k, 2 * m + 1, xh, gain)

            def gain_rows(k, g):
                act.dma_start(grows[8 * k:8 * k + 8, :], g.rearrange("(k p) -> k p", p=P)).then_inc(gn_here, 16)

            act.wait_ge(v_one, 1)
            act.activation(warm[:], eps[:], ACT.Sqrt)
            gain_rows(3, kv_norm)
            gain_rows(4, moba_norm[0])
            gain_rows(5, ffn_norm[1])
            norm_square(0, (x_here, 16 * TT))
            norm_root(0)
            act.wait_ge(nrm_d, 6)
            act.activation(xr[:, 0, :], x[:, 0, :], ACT.Copy, scale=rs[:, 0:1]).then_inc(xr0, 1)
            split(0)
            act.wait_ge(gains_ready, 1)
            turn(0, 0, range(4))
            act.dma_start(graw[:], rows512(w_in[0])[:, :, 3072:3080]).then_inc(c_here, 16)
            act.dma_start(bif[:], b_if[0].rearrange("b h -> h b"), allow_slow_non_contiguous=True).then_inc(c_here, 16)
            act.dma_start(cs[:], rope.rearrange("(t p) c h -> p t c h", p=P)).then_inc(c_here, 16)
            split(1)
            split(2)
            act.wait_ge(c_here, 16 * 3)
            act.activation(gh[:], graw[:], ACT.Copy).then_inc(g_hi, 1)
            split(3)
            act.dma_start(rt[:], rows512(router[0])).then_inc(c_late, 16)
            act.dma_start(gmoe[:], ffn_norm[1].partition_broadcast(P)).then_inc(c_late, 16)
            act.dma_start(gfin[:], final_norm.partition_broadcast(P)).then_inc(c_late, 16)
            act.wait_ge(unit_done, 2)
            for h in range(MH):
                act.activation(qT[:, h, :], ps[h][:, 0:S], ACT.Copy).then_inc(q_out, 1)
            split(4)
            split(5)
            split(6)
            split(7)
            act.wait_ge(unit_done, 6)
            act.activation(v[:, 0, 0:2, 0:MV], ps[1][:].rearrange("p (h n) -> p h n", h=2), ACT.Copy).then_inc(va_out, 1)
            act.wait_ge(r_abs, 1)
            act.activation(rows[:, 3, :], rows[:, 2, :], ACT.Exp, scale=-1.0).then_inc(r_ln, 1)
            act.wait_ge(r_ln, 1)
            act.activation(rows[:, 4, :], rows[:, 3, :], ACT.Ln, bias=1.0).then_inc(r_ln, 1)
            split(8)
            split(9)
            act.wait_ge(unit_done, 8)
            act.activation(v[:, 0, 2:4, 0:MV], ps[3][:].rearrange("p (h n) -> p h n", h=2), ACT.Copy).then_inc(va_out, 1)
            split(10)
            act.wait_ge(z_cols, 1)
            act.activation(enm[:], cols[:, 2:4, :], ACT.Exp, scale=-1.0).then_inc(e_nm, 1)
            split(11)
            act.wait_ge(unit_done, 10)
            for t in range(TT):
                act.activation(sigo[:, t, 0:512], ps[5 + t][:], ACT.Sigmoid).then_inc(o_out, 1)
            split(12)
            for h in range(MH):
                act.wait_ge(d_done, h + 1)
                act.activation(E[:, h, :], E[:, h, :], ACT.Exp, scale=-1.0).then_inc(e_done, 1)
            split(13)
            act.wait_ge(unit_done, 12)
            for t in range(TT):
                act.activation(sigo[:, t, 512:1024], ps[1 + t][:], ACT.Sigmoid).then_inc(o_out, 1)
            split(14)
            act.activation(warm[:], eps[:], ACT.Sqrt)
            for h in range(MH):
                act.wait_ge(rd_done, h + 1)
                for t in range(TT):
                    act.activation(junk[:, t, h, :], ps[PV_BANK[h][t]][:, 0:MV], ACT.Square,
                                   scale=rden[:, t, h:h + 1], accum_out=hss[:, t, h:h + 1]).then_inc(h_raw, 1)
            act.wait_ge(h_raw, 2 * MH)
            act.activation(hrms[:], hss[:], ACT.Sqrt, scale=1.0 / MV, bias=eps[:, 0:1]).then_inc(h_rms, 1)
            turn(1, 1, range(4))
            split(15)
            split(16)
            turn(2, 2, (0, 1))
            split(17)
            turn(2, 2, (2, 3))
            norm_square(1, (resid, 3))
            norm_root(1)
            split(18)

            def silu_chunk(c, i):
                act.wait_ge(unit_done, RAW * c + (i + 1))
                for t in range(TT):
                    last = act.activation(f_sg[:, t, :], ps[GATE_BANK][:, FC * t:FC * t + FC], ACT.Silu,
                                          scale=rs[:, t:t + 1])
                last.then_inc(f_silu, 1)

            def ffn_hi(j):
                act.wait_ge(f_t, j)
                act.activation(f_hth[:], ps[HT_BANK][:].rearrange("p (k s) -> p k s", k=2), ACT.Copy).then_inc(f_hi, 1)

            act.wait_ge(nrm_d, 12)
            silu_chunk(0, U_FFN)
            split(19)
            with act.Fori(0, (NFC - 1) // 2) as it:
                for jj in range(2):
                    a = U_FFN + 2 + 3 * jj
                    split(a + 2, it)
                    ffn_hi(2 * it + (jj + 1))
                    split(a + 3, it)
                    act.wait_ge(f_mul, 2 * it + (jj + 1))
                    silu_chunk(it, a)
                    split(a + 4, it)
            ffn_hi(NFC)
            split(U_KV + 1)
            turn(3, 3, range(4))
            norm_square(2, (resid, 7))
            norm_root(2)
            split(U_KV + 2)
            for c in range(KT):
                act.wait_ge(x_lo, 24 + c // 2 * 2 + 2)
                turn_hi(3, c, yh2, 4)
            split(U_KV + 3)
            act.wait_ge(nrm_d, 18)
            act.wait_ge(unit_done, U_Q)
            for t in range(TT):
                act.activation(kvs[:, t, :], ps[2 + t][:], ACT.Copy, scale=rs[:, t:t + 1]).then_inc(kv_out, 1)
            split(U_KV + 4)
            split(U_KV + 5)

            def queries_out(n):
                act.wait_ge(unit_done, U_Q + 2 * n + 2)
                act.activation(xr[:, 0, 512 * n:512 * n + 512], ps[(6, 0)[n]][:], ACT.Copy, scale=rs[:, 0:1]
                               ).then_inc(aq_out, 1)

            def queries_turned(b):
                act.wait_ge(q_t, b + 1)
                act.activation(aqT[:, 2 * b:2 * b + 2, :], ps[QT_BANK[b]][:].rearrange("p (h s) -> p h s", h=2),
                               ACT.Copy).then_inc(qt_out, 1)

            def exps(half):
                for g in range(3 * half, 3 * half + 3):
                    act.wait_ge(a_nb, g + 1)
                    for h, t, ap in att_heads(g):
                        act.activation(ap, ap, ACT.Exp, bias=nb[:, t, h:h + 1], scale=HD ** -0.5,
                                       accum_out=sm[:, t, h:h + 1]).then_inc(a_exp, 1)

            def probs_turned(h):
                act.wait_ge(a_pt, h + 1)
                act.activation(pT[:, h, :], ps[ATT_BANK[h]][:, 0:384], ACT.Copy).then_inc(a_pto, 1)

            def heads_hi(half):
                for h in range(4 * half, 4 * half + 4):
                    act.wait_ge(a_o, h + 1)
                    act.activation(xh[:, h, :], ps[ATT_BANK[h]][:, 0:S], ACT.Copy).then_inc(a_hi, 1)

            queries_out(0)
            act.wait_ge(k_t, 1)
            act.activation(akT[:], ps[4][:].rearrange("p (h s) -> p h s", h=KVH), ACT.Copy).then_inc(kt_out, 1)
            split(U_O)
            queries_turned(0)
            split(U_O + 1)
            exps(0)
            queries_out(1)
            for h in range(4):
                probs_turned(h)
            queries_turned(2)
            heads_hi(0)
            split(U_O + 2)
            exps(1)
            split(U_O + 3)
            probs_turned(4)
            probs_turned(6)
            heads_hi(1)
            split(U_O + 4)
            split(U_O + 5)

            def turn_f32(m):
                act.wait_ge(x_turned, 16 + m + 1)
                for c in (2 * m, 2 * m + 1):
                    act.activation(hnT[:, c, :], ps[TURN_BANKS[4][m]][:, c % 2 * S:c % 2 * S + S], ACT.Copy,
                                   scale=gains[:, 40 + c:40 + c + 1]).then_inc(r_tout, 1)

            turn_f32(0)
            norm_square(3, (resid, 11))
            turn_f32(2)
            norm_root(3)
            for t in range(TT):
                act.wait_ge(hn_ready, t + 1)
                act.activation(xrh[:, t, :], xr[:, t, :], ACT.Copy).then_inc(hn_hi, 1)
            act.wait_ge(top_m, 1)
            act.activation(ee[:], dd[:], ACT.Exp).then_inc(top_e, 1)

            def expert_hi(q):
                for b in range(2):
                    act.wait_ge(moe_xg, 2 * q + (b + 1))
                    act.activation(xeh[:, 4 * b:4 * b + 4, :], ps[3 + b][:].rearrange("p (k s) -> p k s", k=4),
                                   ACT.Copy).then_inc(moe_xh, 1)

            expert_hi(0)

            def expert(q):
                c = (UE // RAW) * q

                def hidden_hi(j):
                    act.wait_ge(moe_t, NEC * q + (j + 1))
                    act.activation(hth[:], ps[2][:].rearrange("p (k s) -> p k s", k=4), ACT.Copy).then_inc(moe_hth, 1)

                for i in range(UE):
                    kind, j, half = UNITS[i - 1] if i else ("", 0, 0)
                    if (kind, half) == ("g", 1):
                        act.wait_ge(unit_done, UE * q + (U_MOE + i))
                        if j:
                            act.wait_ge(moe_h, NEC * q + j)
                        act.activation(sg[:], ps[0][:], ACT.Silu).then_inc(moe_silu, 1)
                        if j:
                            hidden_hi(j - 1)
                    if (kind, j, half) == ("u", 2, 1):
                        act.wait_ge(moe_pt, q + 1)
                        act.activation(phT[:], ps[7][:, 0:S], ACT.Copy).then_inc(moe_ptr, 1)
                    if i == UE - 2:
                        hidden_hi(NEC - 1)
                        expert_hi(q + 1)
                    split(U_MOE + i + 2, c)
                act.wait_ge(unit_done, UE * q + (U_MOE + UE))
                act.wait_ge(moe_w, q + 1)
                for b in range(2):
                    act.activation(ywh[:, 512 * b:512 * b + 512], ps[5 + b][:], ACT.Copy, scale=wcol[:, 0:1]
                                   ).then_inc(moe_yh, 1)

            with act.Fori(0, NE) as e:
                expert(e)
            act.wait_ge(flag_set, 1)
            over = act.value_load(flag[0:1, 0:1], min_val=0, max_val=S)
            with act.If(over > SLOTS):
                with act.Fori(0, NE) as e:
                    expert(e + NE)
            norm_square(4, (nrm_d, 25))
            norm_root(4)

        @block.vector
        def _(dve):
            links = [0]

            def link(ins):
                links[0] += 1
                ins.then_inc(chain, 1)
                dve.wait_ge(chain, links[0])

            def split(i, c=0):
                dve.wait_ge(hi_split, RAW * c + (i + 1))
                dve.tensor_tensor(wl[:, i % SPL, :], raw[:, i % RAW, :], f32(wh[:, i % SPL, :]), ALU.subtract
                                  ).then_inc(lo_split, 1)

            def norm_sum(i, tile1=None):
                if tile1 is not None:
                    dve.wait_ge(*tile1)
                dve.tensor_tensor_reduce(xr[:, 1, :], x[:, 1, :], x[:, 1, :], 1.0, 0.0, ALU.mult, ALU.add,
                                         ss[:, 1:2]).then_inc(nrm_d, 1)

            def norm_rs(i):
                dve.wait_ge(nrm_a, 2 * i + 1)
                dve.wait_ge(nrm_d, 6 * i + 1)
                dve.tensor_scalar(var[:], ss[:], 1.0 / D, EPS, ALU.mult, ALU.add).then_inc(nrm_d, 1)
                dve.wait_ge(nrm_a, 2 * i + 2)
                newton(rs, rms, r0, t1, var, nrm_d, 6 * i + 2)
                dve.wait_ge(nrm_d, 6 * i + 6)

            def newton(r, root, first, t, w, done, n):
                dve.reciprocal(first[:], root[:]).then_inc(done, 1)
                dve.wait_ge(done, n + 1)
                dve.scalar_tensor_tensor(out=t[:], in0=first[:], scalar=-0.5, in1=first[:], op0=ALU.mult,
                                         op1=ALU.mult).then_inc(done, 1)
                dve.wait_ge(done, n + 2)
                dve.tensor_tensor(t[:], t[:], w[:], ALU.mult).then_inc(done, 1)
                dve.wait_ge(done, n + 3)
                dve.scalar_tensor_tensor(out=r[:], in0=t[:], scalar=1.5, in1=first[:], op0=ALU.add,
                                         op1=ALU.mult).then_inc(done, 1)

            def turn_lo(k, c, hi, lo, gain):
                dve.scalar_tensor_tensor(out=lo[:, c, :], in0=ps[TURN_BANKS[k][c // 2]][:, c % 2 * S:c % 2 * S + S],
                                         scalar=gains[:, 8 * gain + c:8 * gain + c + 1],
                                         in1=f32(hi[:, c, :]), op0=ALU.mult, op1=ALU.subtract).then_inc(x_lo, 1)

            def turn(k, gain, pairs):
                for m in pairs:
                    dve.wait_ge(x_hi, 8 * k + 2 * m + 2)
                    turn_lo(k, 2 * m, xh, xl, gain)
                    turn_lo(k, 2 * m + 1, xh, xl, gain)

            def add(t, n, bank):
                dve.tensor_tensor(x[:, t, 512 * n:512 * n + 512], x[:, t, 512 * n:512 * n + 512], ps[bank][:],
                                  ALU.add).then_inc(resid, 1)

            dve.memset(eps[:], EPS).then_inc(v_one, 1)
            dve.memset(f32(zero[:]), 0.0).then_inc(v_one, 1)
            dve.memset(v[:, :, :, MV:MV + 1], 1.0).then_inc(v_one, 1)
            norm_sum(0, (x_here, 16 * TT))
            norm_rs(0)
            dve.tensor_scalar(xr[:, 1, :], x[:, 1, :], rs[:, 1:2], None, ALU.mult).then_inc(xr1, 1)
            dve.wait_ge(gains_t, 1)
            dve.tensor_copy(gains[:], ps[0][:, 0:48]).then_inc(gains_ready, 1)
            dve.wait_ge(gains_ready, 1)
            split(0)
            turn(0, 0, range(4))
            split(1)
            split(2)
            split(3)
            dve.wait_ge(g_hi, 1)
            dve.tensor_tensor(gl[:], graw[:], f32(gh[:]), ALU.subtract).then_inc(g_lo, 1)
            split(4)
            dve.wait_ge(unit_done, 4)
            for h in range(MH):
                dve.tensor_copy(kT[:, h, :], ps[4 + h][:, 0:S]).then_inc(k_out, 1)
            split(5)
            dve.wait_ge(g_mm, 1)
            dve.tensor_copy(gsb[:], ps[0][:, 0:16].rearrange("p (t g) -> p t g", t=TT)).then_inc(g_sb, 1)
            split(6)
            dve.wait_ge(unit_done, 6)
            dve.tensor_copy(v[:, 1, 0:2, 0:MV], ps[2][:].rearrange("p (h n) -> p h n", h=2)).then_inc(vd_out, 1)
            dve.wait_ge(g_rows, 1)
            dve.tensor_scalar(rows[:, 0, :], ps[0][0:MH, 0:S], bif[:, 0:1], None, ALU.add).then_inc(r_done, 1)
            link(dve.tensor_scalar(rows[:, 1, :], ps[0][0:MH, S:2 * S], bif[:, 1:2], None, ALU.add))
            dve.scalar_tensor_tensor(out=rows[:, 2, :], in0=rows[:, 1, :], scalar=-1.0, in1=rows[:, 1, :],
                                     op0=ALU.mult, op1=ALU.max).then_inc(r_abs, 1)
            split(7)
            dve.wait_ge(r_ln, 2)
            link(dve.scalar_tensor_tensor(out=rows[:, 5, :], in0=rows[:, 1, :], scalar=0.0, in1=rows[:, 4, :],
                                          op0=ALU.min, op1=ALU.subtract))
            dve.wait_ge(pool_ready, POOL_ALL)
            link(dve.tensor_tensor_scan(rows[:, 6, :], onerow[:], rows[:, 5, :], 0.0, ALU.mult, ALU.add))
            dve.wait_ge(r_done, 1)
            link(dve.tensor_tensor(rows[:, 7, :], rows[:, 0, :], rows[:, 6, :], ALU.subtract))
            link(dve.tensor_tensor_scan(rows[:, 8, :], rows[:, 7, :], rows[:, 7, :], 0.0, ALU.max, ALU.max))
            dve.tensor_tensor(rows[:, 0, :], rows[:, 6, :], rows[:, 8, :], ALU.add).then_inc(r_done, 1)
            split(8)
            dve.wait_ge(unit_done, 8)
            dve.tensor_copy(v[:, 1, 2:4, 0:MV], ps[4][:].rearrange("p (h n) -> p h n", h=2)).then_inc(vd_out, 1)
            split(9)
            dve.wait_ge(z_t, 1)
            dve.tensor_copy(cols[:], ps[0][:, 0:16].rearrange("p (a h) -> p a h", a=4)).then_inc(z_cols, 1)
            split(10)
            split(11)
            dve.wait_ge(z_cols, 1)
            for h in range(MH):
                dve.wait_ge(m_bc, h // 2 + 1)
                mb = ps[7 * (h // 2)][:, S * (h % 2):S * (h % 2) + S]
                dve.scalar_tensor_tensor(out=E[:, h, 0:S], in0=mb, scalar=cols[:, 0, h:h + 1], in1=late_st[:],
                                         op0=ALU.subtract, op1=ALU.max)
                dve.scalar_tensor_tensor(out=E[:, h, S:S + P], in0=mb[:, P:S], scalar=cols[:, 1, h:h + 1],
                                         in1=late_st[:, 0:P], op0=ALU.subtract, op1=ALU.max).then_inc(d_done, 1)
            split(12)
            split(13)
            for h in range(MH):
                dve.wait_ge(s_mm, h + 1)
                dve.wait_ge(e_done, h + 1)
                dve.scalar_tensor_tensor(out=E[:, h, :], in0=ps[3 + h][:, 0:384], scalar=MK ** -0.5, in1=E[:, h, :],
                                         op0=ALU.mult, op1=ALU.mult).then_inc(p_done, 1)
            dve.wait_ge(e_nm, 1)
            for h in range(MH):
                for t in range(TT):
                    dve.wait_ge(pv_done, 2 * h + t + 1)
                    last = dve.tensor_copy(nqs[:, t, h:h + 1], ps[PV_BANK[h][t]][:, MV:MV + 1])
                link(last)
                nq, d = nqs[:, :, h:h + 1], den[:, :, h:h + 1]
                link(dve.scalar_tensor_tensor(out=d, in0=nq, scalar=-1.0, in1=nq, op0=ALU.mult, op1=ALU.max))
                link(dve.tensor_tensor(d, d, enm[:, :, h:h + 1], ALU.max))
                dve.reciprocal(rden[:, :, h:h + 1], d).then_inc(rd_done, 1)
            dve.wait_ge(rd_done, MH)
            dve.wait_ge(h_raw, 2 * MH)
            dve.tensor_scalar(hvar[:], hss[:], 1.0 / MV, EPS, ALU.mult, ALU.add).then_inc(h_rs, 1)
            dve.wait_ge(h_rms, 1)
            newton(hrs, hrms, hr0, ht1, hvar, h_rs, 1)
            dve.wait_ge(h_rs, 5)
            link(dve.tensor_tensor(hrs[:], hrs[:], rden[:], ALU.mult))
            dve.wait_ge(o_out, 4)
            for h in range(MH):
                for t in range(TT):
                    dve.scalar_tensor_tensor(out=xr[:, t, h * MV:(h + 1) * MV], in0=ps[PV_BANK[h][t]][:, 0:MV],
                                             scalar=hrs[:, t, h:h + 1], in1=sigo[:, t, h * MV:(h + 1) * MV],
                                             op0=ALU.mult, op1=ALU.mult).then_inc(h_norm, 1)
            turn(1, 1, range(4))
            split(14)
            split(15)
            dve.wait_ge(unit_done, 14)
            for t in range(TT):
                add(t, 0, 4 + t)
            split(16)
            turn(2, 2, (0, 1))
            split(17)
            dve.wait_ge(unit_done, 16)
            for t in range(TT):
                add(t, 1, 6 + t)
            norm_sum(1, (resid, 4))
            turn(2, 2, (2, 3))
            norm_rs(1)
            split(18)
            split(19)

            def ffn_mul(j, up):
                dve.wait_ge(f_silu, j)
                dve.wait_ge(unit_done, up)
                for t in range(TT):
                    last = dve.scalar_tensor_tensor(out=f_h[:, t, :], in0=ps[UP_BANK][:, FC * t:FC * t + FC],
                                                    scalar=rs[:, t:t + 1], in1=f_sg[:, t, :], op0=ALU.mult,
                                                    op1=ALU.mult)
                last.then_inc(f_mul, 1)

            def ffn_lo(j):
                dve.wait_ge(f_hi, j)
                dve.tensor_tensor(f_htl[:], ps[HT_BANK][:].rearrange("p (k s) -> p k s", k=2), f32(f_hth[:]), ALU.subtract
                                  ).then_inc(f_lo, 1)

            ffn_mul(1, U_FFN + 2)
            with dve.Fori(0, (NFC - 1) // 2) as it:
                for jj in range(2):
                    a = U_FFN + 2 + 3 * jj
                    split(a + 2, it)
                    ffn_lo(2 * it + (jj + 1))
                    split(a + 3, it)
                    ffn_mul(2 * it + (jj + 2), RAW * it + (a + 2))
                    split(a + 4, it)
            ffn_lo(NFC)
            split(U_KV + 1)
            dve.wait_ge(y_half, 1)
            for t in range(TT):
                add(t, 0, Y_BANK[t][0])
            dve.wait_ge(unit_done, U_KV)
            for t in range(TT):
                add(t, 1, Y_BANK[t][1])
            norm_sum(2, (resid, 8))
            turn(3, 3, range(4))
            norm_rs(2)
            split(U_KV + 2)
            for c in range(KT):
                dve.wait_ge(x_hi, 32 + c // 2 * 2 + 2)
                turn_lo(3, c, yh2, yl2, 4)
            split(U_KV + 3)
            split(U_KV + 4)

            def rope_rotate(full, n_heads):
                a, b = full[:, :, :, 0:HALF], full[:, :, :, HALF:ROT]
                for g in range(TT):
                    cos = cs[:, g, 0, :].unsqueeze(1).to_broadcast([P, n_heads, HALF])
                    sin = cs[:, g, 1, :].unsqueeze(1).to_broadcast([P, n_heads, HALF])
                    w = [tmp[:, k, g, 0:n_heads, :] for k in range(4)]
                    dve.tensor_tensor(w[0], a[:, g], cos, ALU.mult)
                    dve.tensor_tensor(w[1], b[:, g], sin, ALU.mult)
                    dve.tensor_tensor(w[2], b[:, g], cos, ALU.mult)
                    link(dve.tensor_tensor(w[3], a[:, g], sin, ALU.mult))
                    dve.tensor_tensor(a[:, g], w[0], w[1], ALU.subtract)
                    last = dve.tensor_tensor(b[:, g], w[2], w[3], ALU.add)
                    if g == 0:
                        link(last)
                return last

            dve.wait_ge(kv_out, 2)
            rope_rotate(kvs[:, :, 0:KVH * HD].rearrange("p t (h d) -> p t h d", h=KVH), KVH).then_inc(k_rope, 1)
            split(U_KV + 5)

            def queries_out(n):
                dve.wait_ge(unit_done, U_Q + 2 * n + 2)
                dve.tensor_scalar(xr[:, 1, 512 * n:512 * n + 512], ps[(7, 1)[n]][:], rs[:, 1:2], None, ALU.mult
                                  ).then_inc(aq_out, 1)
                dve.wait_ge(aq_out, 2 * n + 2)
                rope_rotate(xr[:, :, 512 * n:512 * n + 512].rearrange("p t (h d) -> p t h d", h=4), 4
                            ).then_inc(q_rope, 1)

            def queries_turned(b):
                dve.wait_ge(q_t, b + 1)
                dve.tensor_copy(aqT[:, 2 * b:2 * b + 2, :], ps[QT_BANK[b]][:].rearrange("p (h s) -> p h s", h=2)
                                ).then_inc(qt_out, 1)

            def maxima(half):
                for g in range(3 * half, 3 * half + 3):
                    heads, t, h0, n = ATT_GROUPS[g]
                    dve.wait_ge(a_s, g + 1)
                    mask = (late_ts[:] if t else late_ts[:, P:S]).unsqueeze(1).to_broadcast([P, heads, n])
                    scg = sc[:, g, :].rearrange("p (h s) -> p h s", h=heads)
                    link(dve.tensor_tensor(scg, ps[ATT_SBANK[g]][:].rearrange("p (h s) -> p h s", h=heads), mask,
                                           ALU.add))
                    link(dve.tensor_reduce(mx[:, t, h0:h0 + heads], scg, AX, ALU.max))
                    dve.tensor_scalar(nb[:, t, h0:h0 + heads], mx[:, t, h0:h0 + heads], -HD ** -0.5, None, ALU.mult
                                      ).then_inc(a_nb, 1)

            def probabilities(half):
                for g in range(3 * half, 3 * half + 3):
                    heads, t, h0, n = ATT_GROUPS[g]
                    dve.wait_ge(a_exp, sum(ATT_GROUPS[k][0] for k in range(g + 1)))
                    link(dve.reciprocal(rsm[:, t, h0:h0 + heads], sm[:, t, h0:h0 + heads]))
                    scg = sc[:, g, :].rearrange("p (h s) -> p h s", h=heads)
                    dve.tensor_tensor(scg, scg, rsm[:, t, h0:h0 + heads].unsqueeze(2).to_broadcast([P, heads, n]),
                                      ALU.mult).then_inc(a_p, 1)

            def probs_turned(h):
                dve.wait_ge(a_pt, h + 1)
                dve.tensor_copy(pT[:, h, :], ps[ATT_BANK[h]][:, 0:384]).then_inc(a_pto, 1)

            def heads_lo(half):
                for h in range(4 * half, 4 * half + 4):
                    dve.wait_ge(a_hi, h + 1)
                    dve.tensor_tensor(xl[:, h, :], ps[ATT_BANK[h]][:, 0:S], f32(xh[:, h, :]), ALU.subtract
                                      ).then_inc(a_lo, 1)

            queries_out(0)
            split(U_O)
            queries_turned(1)
            maxima(0)
            split(U_O + 1)
            probabilities(0)
            queries_out(1)
            queries_turned(3)
            heads_lo(0)
            maxima(1)
            split(U_O + 2)
            probabilities(1)
            split(U_O + 3)
            probs_turned(5)
            probs_turned(7)
            heads_lo(1)
            split(U_O + 4)
            dve.wait_ge(unit_done, U_O + 3)
            for t in range(TT):
                add(t, 0, 2 + t)
            split(U_O + 5)

            def turn_f32(m):
                dve.wait_ge(x_turned, 16 + m + 1)
                for c in (2 * m, 2 * m + 1):
                    dve.tensor_scalar(hnT[:, c, :], ps[TURN_BANKS[4][m]][:, c % 2 * S:c % 2 * S + S],
                                      gains[:, 40 + c:40 + c + 1], None, ALU.mult).then_inc(r_tout, 1)

            turn_f32(1)
            dve.wait_ge(unit_done, U_O + 4)
            for t in range(TT):
                add(t, 1, 4 + t)
            norm_sum(3, (resid, 12))
            turn_f32(3)
            norm_rs(3)
            dve.wait_ge(c_late, 16 * 3)
            for t in range(TT):
                dve.scalar_tensor_tensor(out=xr[:, t, :], in0=x[:, t, :], scalar=rs[:, t:t + 1], in1=gmoe[:],
                                         op0=ALU.mult, op1=ALU.mult).then_inc(hn_ready, 1)
            dve.wait_ge(r_mm, 1)
            for t in range(TT):
                last = dve.tensor_scalar(lg[:, t, :], ps[2][:, NE * t:NE * t + NE], rs[:, t:t + 1], None, ALU.mult)
            link(last)

            def wide(col):
                return col[:].unsqueeze(2).to_broadcast([P, TT, NE])

            def first_max(src, m, i, oh):
                link(dve.tensor_reduce(m[:], src[:], AX, ALU.max))
                link(dve.tensor_tensor(eq[:], src[:], wide(m), ALU.is_equal))
                link(dve.scalar_tensor_tensor(out=cand[:], in0=eq[:], scalar=-float(NE), in1=iota_e8[:],
                                              op0=ALU.mult, op1=ALU.add))
                link(dve.tensor_reduce(i[:], cand[:], AX, ALU.min))
                link(dve.tensor_tensor(oh[:], iota_e[:], wide(i), ALU.is_equal))

            first_max(lg, m1, i1, oh1)
            link(dve.scalar_tensor_tensor(out=l2[:], in0=oh1[:], scalar=-3e38, in1=lg[:], op0=ALU.mult, op1=ALU.add))
            first_max(l2, m2, i2, oh2)
            dve.tensor_tensor(msk[:], oh1[:], oh2[:], ALU.add).then_inc(top_d, 1)
            dve.tensor_tensor(dd[:], m2[:], m1[:], ALU.subtract).then_inc(top_m, 1)
            dve.wait_ge(hn_hi, TT)
            dve.tensor_tensor(xrl[:], xr[:], f32(xrh[:]), ALU.subtract).then_inc(hn_lo, 1)
            dve.wait_ge(rk_mm, 1)
            dve.wait_ge(top_d, 1)
            link(dve.scalar_tensor_tensor(out=eq[:], in0=ps[5][:, 0:2 * NE].rearrange("p (t e) -> p t e", t=TT),
                                          scalar=1.0, in1=msk[:], op0=ALU.add, op1=ALU.mult))
            link(dve.tensor_scalar(rank[:, 0:NE, :], eq[:].rearrange("p t e -> p e t"), -1.0, None, ALU.add))
            dve.tensor_scalar(rank[:, NE, :], rank[:, 0, :], -float(SLOTS), None, ALU.add)
            link(dve.tensor_reduce(most[:], ps[5][:, 2 * NE:3 * NE], AX, ALU.max))
            dve.tensor_copy(flag[:], most[0:1, :]).then_inc(flag_set, 1)

            def place(e):
                for t in range(TT):
                    last = dve.tensor_scalar(ph[:, t, :], iota_s[:], rank[:, e, t:t + 1], None, ALU.is_equal)
                return last

            def place_r(e):
                for t in range(TT):
                    last = dve.tensor_scalar(phr[:, t, :], iota_s[:], rank[:, e, t:t + 1], None, ALU.is_equal)
                return last

            place_r(0).then_inc(moe_p, 1)
            place(0).then_inc(moe_bank, 4)
            dve.wait_ge(top_e, 1)
            link(dve.tensor_scalar(w2[:], ee[:], 1.0, None, ALU.add))
            link(dve.reciprocal(w1[:], w2[:]))
            link(dve.tensor_tensor(w2[:], ee[:], w1[:], ALU.mult))
            dve.tensor_tensor(cmb[:], oh1[:], wide(w1), ALU.mult)
            link(dve.tensor_tensor(cmb2[:], oh2[:], wide(w2), ALU.mult))
            link(dve.tensor_tensor(cmb[:], cmb[:], cmb2[:], ALU.add))
            cmb_et = cmb[:].rearrange("p t e -> p e t")
            link(dve.tensor_copy(cw[:, :, :, 0], cmb_et))
            dve.tensor_tensor(cw[:, :, :, 1], cmb_et, f32(cw[:, :, :, 0]), ALU.subtract)

            def expert_lo(q):
                for b in range(2):
                    dve.wait_ge(moe_xh, 2 * q + (b + 1))
                    dve.tensor_tensor(xel[:, 4 * b:4 * b + 4, :], ps[3 + b][:].rearrange("p (k s) -> p k s", k=4),
                                      f32(xeh[:, 4 * b:4 * b + 4, :]), ALU.subtract).then_inc(moe_xl, 1)

            expert_lo(0)

            def expert(q, e):
                c = (UE // RAW) * q

                def hidden_lo(j):
                    dve.wait_ge(moe_hth, NEC * q + (j + 1))
                    dve.tensor_tensor(htl[:], ps[2][:].rearrange("p (k s) -> p k s", k=4), f32(hth[:]), ALU.subtract
                                      ).then_inc(moe_htl, 1)

                for i in range(UE):
                    kind, j, half = UNITS[i - 1] if i else ("", 0, 0)
                    if (kind, half) == ("g", 1) and j:
                        hidden_lo(j - 1)
                    if (kind, half) == ("u", 1):
                        dve.wait_ge(unit_done, UE * q + (U_MOE + i))
                        dve.wait_ge(moe_silu, NEC * q + (j + 1))
                        dve.tensor_tensor(hh[:], sg[:], ps[1][:], ALU.mult).then_inc(moe_h, 1)
                    if (kind, j, half) == ("d", 1, 1):
                        dve.wait_ge(moe_ptr, q + 1)
                        dve.tensor_reduce(wcol[:], ps[7][:, S:S + 2], AX, ALU.add).then_inc(moe_w, 1)
                    if (kind, j, half) == ("d", 3, 1):
                        place(e + 1)
                        place_r(e + 1).then_inc(moe_p, 1)
                    if i == UE - 2:
                        hidden_lo(NEC - 1)
                        expert_lo(q + 1)
                    split(U_MOE + i + 2, c)
                for b in range(2):
                    dve.wait_ge(moe_yh, 2 * q + (b + 1))
                    dve.scalar_tensor_tensor(out=ywl[:, 512 * b:512 * b + 512], in0=ps[5 + b][:],
                                             scalar=wcol[:, 0:1], in1=f32(ywh[:, 512 * b:512 * b + 512]),
                                             op0=ALU.mult, op1=ALU.subtract).then_inc(moe_yl, 1)
                dve.wait_ge(moe_bank, 4 * q + 4)
                for k in range(4):
                    t, n = k // 2, k % 2
                    dve.wait_ge(moe_sc, 4 * q + (k + 1))
                    xs = x[:, t, 512 * n:512 * n + 512]
                    dve.tensor_tensor(xs, xs, ps[SC_BANK[k]][:], ALU.add).then_inc(moe_bank, 1)

            with dve.Fori(0, NE) as e:
                expert(e, e)
            dve.wait_ge(moe_bank, 4 * NE + 4)
            dve.wait_ge(flag_set, 1)
            over = dve.value_load(flag[0:1, 0:1], min_val=0, max_val=S)
            with dve.If(over > SLOTS):
                dve.tensor_scalar(rank[:], rank[:], -float(SLOTS), None, ALU.add).then_inc(flag_set, 1)
                dve.wait_ge(flag_set, 2)
                with dve.Fori(0, NE) as e:
                    expert(e + NE, e)
                dve.wait_ge(moe_bank, 8 * NE + 4)
            norm_sum(4)
            norm_rs(4)
            for t in range(TT):
                dve.scalar_tensor_tensor(out=xr[:, t, :], in0=x[:, t, :], scalar=rs[:, t:t + 1], in1=gfin[:],
                                         op0=ALU.mult, op1=ALU.mult).then_inc(fin, 1)

        @block.tensor
        def _(pe):
            def mm3(bank, sh, sl, mh, ml, start, stop):
                pe.matmul(bank, sh, mh, start=start, stop=False)
                pe.matmul(bank, sh, ml, start=False, stop=False)
                return pe.matmul(bank, sl, mh, start=False, stop=stop)

            def project(i, half, banks, sh, sl, between=None):
                pe.wait_ge(lo_split, i + 1)
                for t in range(TT):
                    if t == 1 and between is not None:
                        between()
                    for kk in range(4):
                        f = 4 * half + kk
                        last = mm3(ps[banks[t]][:], sh[:, f, t * P:(t + 1) * P], sl[:, f, t * P:(t + 1) * P],
                                   kn(wh, i % SPL)[:, kk, :], kn(wl, i % SPL)[:, kk, :],
                                   f == 0, f == KT - 1)
                last.then_inc(unit_done, 1)

            def turn(k, m, src):
                bank = ps[TURN_BANKS[k][m]]
                for c in (2 * m, 2 * m + 1):
                    for t in range(TT):
                        last = pe.transpose(bank[:, c % 2 * S + t * P:c % 2 * S + (t + 1) * P],
                                            src[:, t, c * P:(c + 1) * P], ident[:])
                last.then_inc(x_turned, 1)

            pe.wait_ge(pool_ready, POOL_ALL)
            pe.wait_ge(gn_here, 16 * 6)
            pe.transpose(ps[0][:, 0:48], grows[:], ident[0:48, 0:48]).then_inc(gains_t, 1)
            pe.wait_ge(xr0, 1)
            pe.wait_ge(xr1, 1)
            for m in range(4):
                turn(0, m, xr)
            pe.wait_ge(gains_ready, 1)
            for m in range(2):
                for half in range(2):
                    i = U_IN + 2 * m + half
                    pe.wait_ge(lo_split, i + 1)
                    pe.wait_ge(x_lo, 4 * half + 4 if m == 0 else KT)
                    for h in range(MH):
                        for kk in range(4):
                            f, cols_h = 4 * half + kk, slice(h * MK, (h + 1) * MK)
                            last = mm3(ps[4 * m + h][:, 0:S], kn(wh, i % SPL)[:, kk, cols_h],
                                       kn(wl, i % SPL)[:, kk, cols_h], xh[:, f, :], xl[:, f, :], f == 0, f == KT - 1)
                    last.then_inc(unit_done, 1)
            pe.wait_ge(g_lo, 1)
            pe.wait_ge(q_out, 4)
            for t in range(TT):
                for f in range(KT):
                    last = mm3(ps[0][:, 8 * t:8 * t + 8], xh[:, f, t * P:(t + 1) * P], xl[:, f, t * P:(t + 1) * P],
                               gh[:, f, :], gl[:, f, :], f == 0, f == KT - 1)
            last.then_inc(g_mm, 1)
            for half in range(2):
                project(U_IN + 4 + half, half, (1, 2), xh, xl)
            pe.wait_ge(g_sb, 1)
            for g in range(2):
                for t in range(TT):
                    last = pe.transpose(ps[0][0:MH, g * S + t * P:g * S + (t + 1) * P],
                                        gsb[:, t, g * MH:(g + 1) * MH], ident[:])
            last.then_inc(g_rows, 1)
            pe.wait_ge(k_out, 4)
            for half in range(2):
                project(U_IN + 6 + half, half, (3, 4), xh, xl)
            pe.wait_ge(r_done, 2)
            for a, (row, t) in enumerate([(7, 0), (7, 1), (0, 0), (0, 1)]):
                last = pe.transpose(ps[0][:, 4 * a:4 * a + 4], rows[:, row, t * P:(t + 1) * P], ident[0:MH, 0:MH])
            last.then_inc(z_t, 1)
            for half in range(2):
                project(U_IN + 8 + half, half, (5, 6), xh, xl)
            pe.wait_ge(z_cols, 1)
            for h in range(MH):
                last = pe.matmul(ps[7 * (h // 2)][:, S * (h % 2):S * (h % 2) + S], sel[:, h, :], rows[:, 8, :],
                                 start=True, stop=True)
                if h % 2:
                    last.then_inc(m_bc, 1)
            pe.wait_ge(va_out, 1)
            pe.wait_ge(vd_out, 1)
            for half in range(2):
                project(U_IN + 10 + half, half, (1, 2), xh, xl)
            pe.wait_ge(va_out, 2)
            pe.wait_ge(vd_out, 2)
            for h in range(MH):
                if h == 2:
                    pe.wait_ge(o_out, 2)
                pe.matmul(ps[3 + h][:, 0:S], kT[:, h, 0:P], qT[:, h, :], start=True, stop=True)
                pe.matmul(ps[3 + h][:, S:S + P], kT[:, h, P:S], qT[:, h, P:S], start=True, stop=True
                          ).then_inc(s_mm, 1)
            pe.wait_ge(v_one, 3)
            for h in range(MH):
                pe.wait_ge(p_done, MH if h >= 2 else h + 1)
                if h == 0:
                    pe.wait_ge(d_done, MH)
                if h == 1:
                    pe.wait_ge(o_out, 4)
                pe.matmul(ps[PV_BANK[h][0]][:, 0:MV + 1], E[:, h, 0:P], v[:, 0, h, :], start=True, stop=True
                          ).then_inc(pv_done, 1)
                b = ps[PV_BANK[h][1]][:, 0:MV + 1]
                pe.matmul(b, E[:, h, P:S], v[:, 0, h, :], start=True, stop=False)
                pe.matmul(b, E[:, h, S:S + P], v[:, 1, h, :], start=False, stop=True).then_inc(pv_done, 1)
            for m in range(4):
                pe.wait_ge(h_norm, max(2 * m + 2, 2 * (1, 2, 2, 3)[m]))
                turn(1, m, xr)
            for n in range(2):
                for half in range(2):
                    if (n, half) == (0, 0):
                        pe.wait_ge(h_norm, 8)
                    pe.wait_ge(x_lo, 8 + 4 * half + 4 if n == 0 else 16)
                    if (n, half) == (1, 1):
                        pe.wait_ge(resid, 2)
                        turn(2, 0, x)
                        turn(2, 1, x)
                    project(U_OUT + 2 * n + half, half, (4 + 2 * n, 5 + 2 * n), xh, xl)
            pe.wait_ge(resid, 4)
            turn(2, 2, x)
            turn(2, 3, x)

            def gate_up(i, bank, c=0, turned=None):
                pe.wait_ge(lo_split, RAW * c + (i + 1))
                for t in range(TT):
                    for f in range(KT):
                        if turned is not None and t == 0:
                            pe.wait_ge(x_lo, turned + f + 1)
                        last = mm3(ps[bank][:, FC * t:FC * t + FC], xh[:, f, t * P:(t + 1) * P],
                                   xl[:, f, t * P:(t + 1) * P], kc(wh, i % SPL)[:, f, :], kc(wl, i % SPL)[:, f, :],
                                   f == 0, f == KT - 1)
                last.then_inc(unit_done, 1)

            gate_up(U_FFN, GATE_BANK, turned=16)
            gate_up(U_FFN + 1, UP_BANK)
            for t in range(TT):
                for n in range(2):
                    pe.matmul(ps[Y_BANK[t][n]][:], zero[:, 0:P], zero[:], start=True, stop=False)

            def hidden(j):
                pe.wait_ge(f_mul, j)
                for k in range(2):
                    for t in range(TT):
                        last = pe.transpose(ps[HT_BANK][:, k * S + t * P:k * S + (t + 1) * P], f_h[:, t, k * P:(k + 1) * P],
                                            ident[:])
                last.then_inc(f_t, 1)

            def down(i, j, c, stop):
                pe.wait_ge(lo_split, RAW * c + (i + 1))
                pe.wait_ge(f_lo, j)
                for n in range(2):
                    for t in range(TT):
                        for k in range(2):
                            last = mm3(ps[Y_BANK[t][n]][:], f_hth[:, k, t * P:(t + 1) * P],
                                       f_htl[:, k, t * P:(t + 1) * P], fn(wh, i % SPL)[:, k, 512 * n:512 * n + 512],
                                       fn(wl, i % SPL)[:, k, 512 * n:512 * n + 512], False, stop and k == 1)
                    if stop and n == 0:
                        last.then_inc(y_half, 1)
                last.then_inc(unit_done, 1)

            with pe.Fori(0, (NFC - 1) // 2) as it:
                for jj in range(2):
                    a = U_FFN + 2 + 3 * jj
                    pe.wait_ge(f_silu, 2 * it + (jj + 1))
                    gate_up(a, GATE_BANK, it)
                    hidden(2 * it + (jj + 1))
                    gate_up(a + 1, UP_BANK, it)
                    down(a + 2, 2 * it + (jj + 1), it, False)
            hidden(NFC)
            down(U_KV - 1, NFC, 0, True)
            pe.wait_ge(resid, 6)
            pe.wait_ge(f_silu, NFC)
            turn(3, 0, x)
            turn(3, 1, x)
            pe.wait_ge(resid, 8)
            turn(3, 2, x)
            turn(3, 3, x)
            for half in range(2):
                pe.wait_ge(x_lo, 24 + 4 * half + 4)
                project(U_KV + half, half, (2, 3), xh, xl)
            for half in range(2):
                pe.wait_ge(x_lo, 32 + 4 * half + 4)
                project(U_Q + half, half, (6, 7), yh2, yl2)
            pe.wait_ge(k_rope, 1)
            for g in range(KVH):
                for t in range(TT):
                    last = pe.transpose(ps[4][:, g * S + t * P:g * S + (t + 1) * P], kvs[:, t, g * HD:(g + 1) * HD],
                                        ident[:])
            last.then_inc(k_t, 1)

            def turn_queries(n):
                pe.wait_ge(q_rope, n + 1)
                for h in range(4 * n, 4 * n + 4):
                    for t in range(TT):
                        last = pe.transpose(ps[QT_BANK[h // 2]][:, (h % 2) * S + t * P:(h % 2) * S + (t + 1) * P],
                                            xr[:, t, h * HD:(h + 1) * HD], ident[:])
                    if h % 2:
                        last.then_inc(q_t, 1)

            def scores(n):
                pe.wait_ge(qt_out, 2 * n + 2)
                for g in range(3 * n, 3 * n + 3):
                    heads, t, h0, m = ATT_GROUPS[g]
                    for a in range(heads):
                        h = h0 + a
                        last = pe.matmul(ps[ATT_SBANK[g]][:, a * m:(a + 1) * m], aqT[:, h, t * P:(t + 1) * P],
                                         akT[:, h // (AH // KVH), 0:m], start=True, stop=True)
                    last.then_inc(a_s, 1)

            def turn_probs(n):
                pe.wait_ge(a_p, 3 * n + 3)
                for h in range(4 * n, 4 * n + 4):
                    b = ps[ATT_BANK[h]]
                    g0, a0 = 3 * n + 2, (h % 4) * P
                    g1, a1 = 3 * n + h % 4 // 2, (h % 2) * S
                    pe.transpose(b[:, 0:P], sc[:, g0, a0:a0 + P], ident[:])
                    pe.transpose(b[:, P:S], sc[:, g1, a1:a1 + P], ident[:])
                    pe.transpose(b[:, S:S + P], sc[:, g1, a1 + P:a1 + S], ident[:]).then_inc(a_pt, 1)

            def values(n):
                pe.wait_ge(a_pto, 4 * n + 4)
                for h in range(4 * n, 4 * n + 4):
                    b = ps[ATT_BANK[h]]
                    g = KVH * HD + (h // (AH // KVH)) * HD
                    pe.matmul(b[:, 0:S], kvs[:, 0, g:g + HD], pT[:, h, 0:S], start=True, stop=False)
                    pe.matmul(b[:, P:S], kvs[:, 1, g:g + HD], pT[:, h, S:S + P], start=False, stop=True
                              ).then_inc(a_o, 1)

            project(U_Q + 2, 0, (0, 1), yh2, yl2, between=lambda: turn_queries(0))
            pe.wait_ge(kt_out, 1)
            scores(0)
            project(U_Q + 3, 1, (0, 1), yh2, yl2)
            turn_probs(0)
            turn_queries(1)
            values(0)
            scores(1)
            pe.wait_ge(a_lo, 4)
            project(U_O, 0, (2, 3), xh, xl)
            project(U_O + 1, 0, (4, 5), xh, xl)
            turn_probs(1)
            values(1)
            pe.wait_ge(a_lo, AH)
            project(U_O + 2, 1, (2, 3), xh, xl)

            def turn_first_half():
                pe.wait_ge(resid, 10)
                turn(4, 0, x)
                turn(4, 1, x)

            project(U_O + 3, 1, (4, 5), xh, xl, between=turn_first_half)
            pe.wait_ge(resid, 12)
            turn(4, 2, x)
            turn(4, 3, x)
            pe.wait_ge(c_late, 16 * 3)
            pe.wait_ge(r_tout, KT)
            for t in range(TT):
                for f in range(KT):
                    last = pe.matmul(ps[2][:, NE * t:NE * t + NE], hnT[:, f, t * P:(t + 1) * P], rt[:, f, :],
                                     start=(f == 0), stop=(f == KT - 1))
            last.then_inc(r_mm, 1)
            pe.wait_ge(top_d, 1)
            pe.matmul(ps[5][:, 0:NE], before[:], msk[:, 0, :], start=True, stop=True)
            pe.matmul(ps[5][:, NE:2 * NE], ones[:], msk[:, 0, :], start=True, stop=False)
            pe.matmul(ps[5][:, NE:2 * NE], before[:], msk[:, 1, :], start=False, stop=True)
            pe.matmul(ps[5][:, 2 * NE:3 * NE], ones[:], msk[:, 0, :], start=True, stop=False)
            pe.matmul(ps[5][:, 2 * NE:3 * NE], ones[:], msk[:, 1, :], start=False, stop=True).then_inc(rk_mm, 1)
            pe.wait_ge(hn_lo, 1)

            def gather():
                for b in range(2):
                    for kk in range(4):
                        f = 4 * b + kk
                        for t in range(TT):
                            for k, src in enumerate((xrh, xrl)):
                                last = pe.matmul(ps[3 + b][:, kk * SLOTS:(kk + 1) * SLOTS],
                                                 src[:, t, f * P:(f + 1) * P], phr[:, t, :],
                                                 start=(t == 0 and k == 0), stop=(t == 1 and k == 1))
                    last.then_inc(moe_xg, 1)

            pe.wait_ge(moe_p, 1)
            gather()

            def expert(q, e):
                def hidden(j):
                    pe.wait_ge(moe_h, NEC * q + (j + 1))
                    for k in range(4):
                        last = pe.transpose(ps[2][:, k * P:(k + 1) * P], hh[:, k * P:(k + 1) * P], ident[:])
                    last.then_inc(moe_t, 1)

                pe.wait_ge(moe_xl, 2 * q + 2)
                for i in range(UE):
                    kind, j, half = UNITS[i]
                    n = U_MOE + i
                    if i == UE - 2:
                        hidden(NEC - 1)
                        pe.wait_ge(moe_p, q + 2)
                        pe.wait_ge(moe_bank, 4 * q + 4)
                        gather()
                    if (kind, half) == ("g", 0) and j:
                        pe.wait_ge(moe_silu, NEC * q + j)
                    pe.wait_ge(lo_split, UE * q + (n + 1))
                    if kind in "gu":
                        for kk in range(4):
                            f = 4 * half + kk
                            last = mm3(ps["gu".index(kind)][:], xeh[:, f, :], xel[:, f, :], kn(wh, n % SPL)[:, kk, :],
                                       kn(wl, n % SPL)[:, kk, :], f == 0, f == KT - 1)
                    else:
                        pe.wait_ge(moe_htl, NEC * q + (j + 1))
                        for kk in range(2):
                            f = 2 * half + kk
                            for b in range(2):
                                last = mm3(ps[5 + b][:], hth[:, f, :], htl[:, f, :],
                                           fn(wh, n % SPL)[:, kk, 512 * b:512 * b + 512],
                                           fn(wl, n % SPL)[:, kk, 512 * b:512 * b + 512],
                                           j == 0 and f == 0, j == NEC - 1 and f == 3)
                    last.then_inc(unit_done, 1)
                    if (kind, half) == ("g", 1) and j:
                        hidden(j - 1)
                    if (kind, j, half) == ("u", 2, 1):
                        pe.wait_ge(moe_bank, 4 * q + 4)
                        for t in range(TT):
                            pe.transpose(ps[7][:, t * P:(t + 1) * P], ph[:, t, :], ident[:])
                        for t in range(TT):
                            last = pe.matmul(ps[7][:, S:S + 2], phr[:, t, :], cw[:, e, t, :], start=(t == 0),
                                             stop=(t == 1))
                        last.then_inc(moe_pt, 1)
                pe.wait_ge(moe_yl, 2 * q + 2)
                pe.wait_ge(moe_ptr, q + 1)
                for k in range(4):
                    t, n = k // 2, k % 2
                    if k == 3:
                        pe.wait_ge(moe_bank, 4 * q + 5)
                    pe.matmul(ps[SC_BANK[k]][:], phT[:, t * P:(t + 1) * P], ywh[:, 512 * n:512 * n + 512],
                              start=True, stop=False)
                    pe.matmul(ps[SC_BANK[k]][:], phT[:, t * P:(t + 1) * P], ywl[:, 512 * n:512 * n + 512],
                              start=False, stop=True).then_inc(moe_sc, 1)

            with pe.Fori(0, NE) as e:
                expert(e, e)
            pe.wait_ge(flag_set, 1)
            over = pe.value_load(flag[0:1, 0:1], min_val=0, max_val=S)
            with pe.If(over > SLOTS):
                with pe.Fori(0, NE) as e:
                    expert(e + NE, e)


_INS = ['x', 'mlstm_norm', 'mlstm_w_in', 'mlstm_b_if', 'mlstm_out_norm', 'mlstm_w_out', 'ffn_norm', 'dense_w_gu',
        'dense_w_down', 'moe_router', 'moe_w_gu', 'moe_w_down', 'kv_norm', 'kv_w', 'moba_norm', 'moba_w_q',
        'moba_w_o', 'final_norm']


def rope_table():
    import numpy as _np

    freq = (500000.0 ** (-_np.arange(0, ROT, 2) / ROT)).astype(_np.float32)
    angle = _np.arange(S, dtype=_np.float32)[:, None] * freq[None, :]
    return _np.stack([_np.cos(angle), _np.sin(angle)], axis=1).astype(_np.float32)


def kernel(**inputs):
    import numpy as _np
    import concourse.bacc as _bacc
    from concourse import mybir as _mybir
    from concourse.bass_utils import run_bass_kernel_spmd as _run

    nc = _bacc.Bacc("TRN2", target_bir_lowering=False, num_devices=1)
    arrays, args = {}, []
    for name in _INS + ['rope']:
        a = _np.ascontiguousarray(inputs[name]) if name != 'rope' else rope_table()
        arrays[f"in_{name}_dram"] = a
        args.append(nc.dram_tensor(f"in_{name}_dram", a.shape, _mybir.dt.from_np(a.dtype), kind="ExternalInput").ap())
    args.append(nc.dram_tensor("out_0_dram", (1, S, D), F32, kind="ExternalOutput").ap())
    yoco_block(nc, *args)
    r = _run(nc, [arrays], core_ids=[0])
    return r.results[0]["out_0_dram"]
```

```python
from contextlib import ExitStack

import concourse.bass as bass
from concourse import mybir

ALU = mybir.AluOpType
ACT = mybir.ActivationFunctionType
F32 = mybir.dt.float32
F32R = mybir.dt.float32r
I32 = mybir.dt.int32
AX = mybir.AxisListType.X

P = 128
EPS = 1e-6
FAR = 1e30

D = 1024
S = 256
TT = S // P
KT = D // P
MH, MK, MV = 4, 128, 256
AH, KVH, HD = 8, 2, 128
ROT = HD // 4
HALF = ROT // 2
FF = 2816
FC = 256
NFC = FF // FC
NE = 8
FE = 3584
EC = 512
NEC = FE // EC
SLOTS = 128

UNIT = 2048
RAW = 6
SPL = 3
U_IN = 0
U_OUT = U_IN + 12
U_FFN = U_OUT + 4
U_KV = U_FFN + 3 * NFC
U_Q = U_KV + 2
U_O = U_Q + 4
U_MOE = U_O + 4
UE = 6 * NEC
assert UE % RAW == 0 and RAW % SPL == 0


def expert_units():
    order = []
    for j in range(NEC):
        order += [("g", j, 0), ("g", j, 1), ("u", j, 0), ("u", j, 1)]
        if j:
            order += [("d", j - 1, 0), ("d", j - 1, 1)]
    return order + [("d", NEC - 1, 0), ("d", NEC - 1, 1)]


UNITS = expert_units()

TURN_BANKS = [(4, 5, 6, 7), (0, 7, 3, 4), (0, 1, 2, 3), (4, 5, 0, 1), (6, 7, 0, 1)]
GATE_BANK, UP_BANK, RB_BANK = 4, 0, 5
Y_BANK = [(2, 6), (3, 7)]
PV_BANK = [(0, 7), (1, 2), (3, 4), (5, 6)]
ATT_GROUPS = [(2, 1, 0, S), (2, 1, 2, S), (4, 0, 0, P), (2, 1, 4, S), (2, 1, 6, S), (4, 0, 4, P)]
ATT_SBANK = [5, 6, 7, 0, 1, 6]
QT_BANK = [2, 3, 6, 7]
ATT_BANK = [2, 3, 4, 5, 7, 0, 1, 6]
SC_BANK = [7, 3, 4, 5]
POOL_ALL = 9


def yoco_block(nc, x_in, mlstm_norm, w_in, b_if, out_norm, w_out, ffn_norm, w_gu, w_down, router,
               e_gu, e_down, kv_norm, kv_w, moba_norm, w_q, w_o, final_norm, rope, out):
    with ExitStack() as ctx:
        def sem(name):
            return ctx.enter_context(nc.semaphore(name))

        def keep(name, shape, dt=F32):
            return ctx.enter_context(nc.sbuf_tensor(name, shape, dt))

        raw = keep("raw", [P, RAW, UNIT])
        wh = keep("wh", [P, SPL, UNIT], F32R)
        wl = keep("wl", [P, SPL, UNIT], F32R)
        x = keep("x", [P, TT, D])
        xr = keep("xr", [P, TT, D])
        xh = keep("xh", [P, KT, S], F32R)
        xl = keep("xl", [P, KT, S], F32R)
        ident = keep("ident", [P, P])
        ones = keep("ones", [P, P])
        onerow = keep("onerow", [MH, S])
        zero = keep("zero", [P, 512], F32R)
        before = keep("before", [P, P])
        before_r = keep("before_r", [P, P], F32R)
        ones_r = keep("ones_r", [P, P], F32R)
        late_st = keep("late_st", [P, S])
        late_ts = keep("late_ts", [P, S])
        iota_s = keep("iota_s", [P, SLOTS])
        iota_e = keep("iota_e", [P, TT, NE])
        iota_e8 = keep("iota_e8", [P, TT, NE])
        sel = keep("sel", [MH, MH, P])
        grows = keep("grows", [48, P])
        gains = keep("gains", [P, 48])
        cs = keep("cs", [P, TT, 2, HALF])
        bif = keep("bif", [MH, 2])
        ss = keep("ss", [P, TT])
        eps = keep("eps", [P, 1])
        warm = keep("warm", [P, 1])
        rms = keep("rms", [P, TT])
        var = keep("var", [P, TT])
        r0 = keep("r0", [P, TT])
        t1 = keep("t1", [P, TT])
        rs = keep("rs", [P, TT])
        rt = keep("rt", [P, KT, NE])
        gfin = keep("gfin", [P, D])
        gmoe = keep("gmoe", [P, D])

        phase = ExitStack()

        def sb(name, shape, dt=F32):
            return phase.enter_context(nc.sbuf_tensor(name, shape, dt))

        graw = sb("graw", [P, KT, 2 * MH])
        gh = sb("gh", [P, KT, 2 * MH], F32R)
        gl = sb("gl", [P, KT, 2 * MH], F32R)
        qT = sb("qT", [P, MH, S])
        kT = sb("kT", [P, MH, S])
        v = sb("v", [P, TT, MH, MV + 1])
        sigo = sb("sigo", [P, TT, D])
        gsb = sb("gsb", [P, TT, 2 * MH])
        rows = sb("rows", [MH, 9, S])
        cols = sb("cols", [P, 4, MH])
        enm = sb("enm", [P, TT, MH])
        E = sb("E", [P, MH, 384])
        den = sb("den", [P, TT, MH])
        rden = sb("rden", [P, TT, MH])
        hss = sb("hss", [P, TT, MH])
        hrms = sb("hrms", [P, TT, MH])
        hrs = sb("hrs", [P, TT, MH])
        hvar = sb("hvar", [P, TT, MH])
        hr0 = sb("hr0", [P, TT, MH])
        ht1 = sb("ht1", [P, TT, MH])
        nqs = sb("nqs", [P, TT, MH])
        junk = sb("junk", [P, TT, MH, MV])
        phase.close()
        rs_wide = sb("rs_wide", [P, TT, P])
        rs_row = sb("rs_row", [P, S])
        f_g = sb("f_g", [P, 2, S])
        f_sg = sb("f_sg", [P, 2, S])
        f_h = sb("f_h", [P, 2, S])
        f_hth = sb("f_hth", [P, 2, 2, S], F32R)
        f_htl = sb("f_htl", [P, 2, 2, S], F32R)
        phase.close()
        yh2 = sb("yh2", [P, KT, S], F32R)
        yl2 = sb("yl2", [P, KT, S], F32R)
        kvs = sb("kvs", [P, TT, 2 * KVH * HD])
        aqT = sb("aqT", [P, AH, S])
        akT = sb("akT", [P, KVH, S])
        tmp = sb("tmp", [P, 4, TT, AH, HALF])
        sc = sb("sc", [P, 6, 512])
        mx = sb("mx", [P, TT, AH])
        nb = sb("nb", [P, TT, AH])
        sm = sb("sm", [P, TT, AH])
        rsm = sb("rsm", [P, TT, AH])
        pT = sb("pT", [P, AH, 384])
        phase.close()
        hnT = sb("hnT", [P, KT, S])
        xrh = sb("xrh", [P, TT, D], F32R)
        xrl = sb("xrl", [P, TT, D], F32R)
        xeh = sb("xeh", [P, KT, SLOTS], F32R)
        xel = sb("xel", [P, KT, SLOTS], F32R)
        ph = sb("ph", [P, TT, SLOTS])
        phr = sb("phr", [P, TT, SLOTS], F32R)
        phT = sb("phT", [SLOTS, S], F32R)
        xe = sb("xe", [SLOTS, D])
        sg = sb("sg", [P, EC])
        hh = sb("hh", [P, EC])
        hth = sb("hth", [P, 2, 4, SLOTS], F32R)
        htl = sb("htl", [P, 2, 4, SLOTS], F32R)
        ywh = sb("ywh", [SLOTS, D], F32R)
        ywl = sb("ywl", [SLOTS, D], F32R)
        wcol = sb("wcol", [SLOTS, 1])
        lg = sb("lg", [P, TT, NE])
        l2 = sb("l2", [P, TT, NE])
        eq = sb("eq", [P, TT, NE])
        cand = sb("cand", [P, TT, NE])
        oh1 = sb("oh1", [P, TT, NE])
        oh2 = sb("oh2", [P, TT, NE])
        m1 = sb("m1", [P, TT])
        m2 = sb("m2", [P, TT])
        i1 = sb("i1", [P, TT])
        i2 = sb("i2", [P, TT])
        dd = sb("dd", [P, TT])
        ee = sb("ee", [P, TT])
        w1 = sb("w1", [P, TT])
        w2 = sb("w2", [P, TT])
        msk = sb("msk", [P, TT, NE], F32R)
        cmb = sb("cmb", [P, TT, NE])
        cmb2 = sb("cmb2", [P, TT, NE])
        rank = sb("rank", [P, NE + 1, TT])
        cw = sb("cw", [P, NE, TT, 2], F32R)
        most = sb("most", [P, 1])
        flag = sb("flag", [1, 1], I32)
        phase.close()

        ps = [ctx.enter_context(nc.psum_tensor(f"ps{b}", [P, 512], F32)) for b in range(8)]

        raw_full = [sem(f"raw_full{i}") for i in range(RAW)]
        hi_split = sem("hi_split")
        lo_split = sem("lo_split")
        unit_done = sem("unit_done")
        x_here = sem("x_here")
        gn_here = sem("gn_here")
        c_here = sem("c_here")
        c_late = sem("c_late")
        pool_ready = sem("pool_ready")
        pool_zero = sem("pool_zero")
        gains_t = sem("gains_t")
        gains_ready = sem("gains_ready")
        nrm_a = sem("nrm_a")
        nrm_d = sem("nrm_d")
        xr0 = sem("xr0")
        xr1 = sem("xr1")
        x_turned = sem("x_turned")
        x_hi = sem("x_hi")
        x_lo = sem("x_lo")
        resid = sem("resid")
        q_out = sem("q_out")
        k_out = sem("k_out")
        va_out = sem("va_out")
        vd_out = sem("vd_out")
        v_one = sem("v_one")
        o_out = sem("o_out")
        g_hi = sem("g_hi")
        g_lo = sem("g_lo")
        g_mm = sem("g_mm")
        g_sb = sem("g_sb")
        g_rows = sem("g_rows")
        chain = sem("chain")
        r_abs = sem("r_abs")
        r_ln = sem("r_ln")
        r_done = sem("r_done")
        z_t = sem("z_t")
        z_cols = sem("z_cols")
        e_nm = sem("e_nm")
        m_bc = sem("m_bc")
        d_done = sem("d_done")
        e_done = sem("e_done")
        s_mm = sem("s_mm")
        p_done = sem("p_done")
        pv_done = sem("pv_done")
        rd_done = sem("rd_done")
        h_raw = sem("h_raw")
        h_rms = sem("h_rms")
        h_rs = sem("h_rs")
        h_norm = sem("h_norm")
        y_half = sem("y_half")
        f_silu = sem("f_silu")
        f_mul = sem("f_mul")
        rs_w = sem("rs_w")
        rs_mm = sem("rs_mm")
        rs_out = sem("rs_out")
        f_gate = sem("f_gate")
        f_hi = sem("f_hi")
        f_lo = sem("f_lo")
        kv_out = sem("kv_out")
        aq_out = sem("aq_out")
        k_rope = sem("k_rope")
        q_rope = sem("q_rope")
        k_t = sem("k_t")
        q_t = sem("q_t")
        kt_out = sem("kt_out")
        qt_out = sem("qt_out")
        a_s = sem("a_s")
        a_nb = sem("a_nb")
        a_exp = sem("a_exp")
        a_p = sem("a_p")
        a_pt = sem("a_pt")
        a_pto = sem("a_pto")
        a_o = sem("a_o")
        a_hi = sem("a_hi")
        a_lo = sem("a_lo")
        xg_ready = sem("xg_ready")
        hn_hi = sem("hn_hi")
        hn_lo = sem("hn_lo")
        r_tout = sem("r_tout")
        r_mm = sem("r_mm")
        top_d = sem("top_d")
        top_e = sem("top_e")
        top_m = sem("top_m")
        rk_mm = sem("rk_mm")
        flag_set = sem("flag_set")
        moe_bank = sem("moe_bank")
        moe_p = sem("moe_p")
        moe_xg = sem("moe_xg")
        moe_xc = sem("moe_xc")
        moe_xt = sem("moe_xt")
        moe_xh = sem("moe_xh")
        moe_xl = sem("moe_xl")
        moe_silu = sem("moe_silu")
        moe_h = sem("moe_h")
        moe_t = sem("moe_t")
        moe_hth = sem("moe_hth")
        moe_htl = sem("moe_htl")
        moe_pt = sem("moe_pt")
        moe_ptr = sem("moe_ptr")
        moe_w = sem("moe_w")
        moe_yh = sem("moe_yh")
        moe_yl = sem("moe_yl")
        moe_sc = sem("moe_sc")
        fin = sem("fin")
        stored = sem("stored")

        x_v = x_in[0].rearrange("(t p) d -> p t d", p=P)
        out_v = out[0].rearrange("(t p) d -> p t d", p=P)

        def rows512(w):
            return w.rearrange("(k p) n -> p k n", p=P)

        def kn(buf, slot):
            return buf[:, slot, :].rearrange("p (k n) -> p k n", k=4)

        def kc(buf, slot):
            return buf[:, slot, :].rearrange("p (k n) -> p k n", k=8)

        def fn(buf, slot):
            return buf[:, slot, :].rearrange("p (k n) -> p k n", k=2)

        def f32(ap):
            return ap.bitcast(F32)

        def att_heads(g):
            heads, t, h0, n = ATT_GROUPS[g]
            return [(h0 + a, t, sc[:, g, a * n:(a + 1) * n]) for a in range(heads)]

        block = ctx.enter_context(nc.Block())

        @block.sync
        def _(sp):
            def load(n, i, dst, src, after=None):
                if after is not None:
                    sp.wait_ge(lo_split, after)
                sp.dma_start(dst, src).then_inc(raw_full[i % RAW], 16)

            def free(n):
                return n - RAW + 1 if n >= RAW else None

            def load_kn(n, w, col, half, step=None):
                src = rows512(w)[:, 4 * half:4 * half + 4, col:col + 512]
                load(n, n, kn(raw, n % RAW), src, free(n))

            for t in range(TT):
                sp.dma_start(x[:, t, :], x_v[:, t, :]).then_inc(x_here, 16)
            for k, g in enumerate([mlstm_norm[0], out_norm[0], ffn_norm[0]]):
                sp.dma_start(grows[8 * k:8 * k + 8, :], g.rearrange("(k p) -> k p", p=P)).then_inc(gn_here, 16)
            sp.wait_ge(gn_here, 16 * 6)
            for j in range(6):
                for half in range(2):
                    load_kn(U_IN + 2 * j + half, w_in[0], 512 * j, half)
            for j in range(2):
                for half in range(2):
                    load_kn(U_OUT + 2 * j + half, w_out[0], 512 * j, half)

            def ffn_gu(i, after, col):
                sp.wait_ge(lo_split, after)
                sp.dma_start(kc(raw, i % RAW), rows512(w_gu[0])[:, :, bass.ds(col, FC)]
                             ).then_inc(raw_full[i % RAW], 16)

            def ffn_down(i, after, row):
                src = w_down[0][bass.ds(row, FC), :].rearrange("(k p) n -> p k n", p=P)
                sp.wait_ge(lo_split, after)
                sp.dma_start(fn(raw, i % RAW), src).then_inc(raw_full[i % RAW], 16)

            ffn_gu(U_FFN, U_FFN - RAW + 1, 0)
            ffn_gu(U_FFN + 1, U_FFN + 1 - RAW + 1, FF)
            with sp.Fori(0, (NFC - 1) // 2) as it:
                for jj in range(2):
                    i = U_FFN + 2 + 3 * jj
                    ffn_gu(i, 6 * it + (i - RAW + 1), (2 * it + (jj + 1)) * FC)
                    ffn_gu(i + 1, 6 * it + (i + 1 - RAW + 1), (2 * it + (jj + 1)) * FC + FF)
                    ffn_down(i + 2, 6 * it + (i + 2 - RAW + 1), (2 * it + jj) * FC)
            ffn_down(U_KV - 1, U_KV - 1 - RAW + 1, (NFC - 1) * FC)

            for half in range(2):
                load_kn(U_KV + half, kv_w, 0, half)
            for j in range(2):
                for half in range(2):
                    load_kn(U_Q + 2 * j + half, w_q[0], 512 * j, half)
            for half in range(2):
                for j in range(2):
                    load_kn(U_O + 2 * half + j, w_o[0], 512 * j, half)

            def load_expert(e, q, first, last):
                gu = e_gu[0].rearrange("e (k p) n -> e p k n", p=P)
                dn = e_down[0].rearrange("e (k p) n -> e p k n", p=P)
                for i in range(first, last):
                    kind, j, half = UNITS[i]
                    n = U_MOE + i
                    if kind == "d":
                        k = 4 * j + 2 * half
                        dst, src = fn(raw, n % RAW), dn[e, :, k:k + 2, :]
                    else:
                        c = EC * j + (FE if kind == "u" else 0)
                        dst, src = kn(raw, n % RAW), gu[e, :, 4 * half:4 * half + 4, c:c + EC]
                    sp.wait_ge(lo_split, q * UE + (n - RAW + 1))
                    sp.dma_start(dst, src).then_inc(raw_full[n % RAW], 16)

            with sp.Fori(0, NE) as e:
                load_expert(e, e, 0, UE)
            sp.wait_ge(flag_set, 1)
            over = sp.value_load(flag[0:1, 0:1], min_val=0, max_val=S)
            with sp.If(over > SLOTS):
                load_expert(0, NE, 0, UE)
                with sp.Fori(1, NE) as e:
                    load_expert(e, e + NE, 0, UE)
                load_expert(0, 2 * NE, 0, 3)
            for t in range(TT):
                for n in range(2):
                    sp.wait_ge(fin, 2 * t + n + 1)
                    sp.dma_start(out_v[:, t, 512 * n:512 * n + 512], xr[:, t, 512 * n:512 * n + 512]
                                 ).then_inc(stored, 16)
            sp.wait_ge(stored, 16 * 2 * TT)

        @block.gpsimd
        def _(pool):
            pool.memset(ident[:], 0.0).then_inc(pool_zero, 1)
            pool.memset(ones[:], 1.0).then_inc(pool_zero, 1)
            pool.memset(late_st[:], 0.0).then_inc(pool_zero, 1)
            pool.memset(late_ts[:], 0.0).then_inc(pool_zero, 1)
            pool.memset(sel[:], 0.0).then_inc(pool_zero, 1)
            pool.memset(onerow[:], 1.0).then_inc(pool_ready, 1)
            pool.wait_ge(pool_zero, 5)
            pool.affine_select(out=ident[:], in_=ident[:], compare_op=ALU.not_equal, fill=1.0, base=0,
                               pattern=[[-1, P]], channel_multiplier=1).then_inc(pool_ready, 1)
            pool.affine_select(out=before[:], in_=ones[:], compare_op=ALU.is_gt, fill=0.0, base=0,
                               pattern=[[1, P]], channel_multiplier=-1).then_inc(pool_ready, 1)
            pool.affine_select(out=late_st[:, 0:P], in_=late_st[:, 0:P], compare_op=ALU.is_ge, fill=FAR,
                               base=0, pattern=[[1, P]], channel_multiplier=-1).then_inc(pool_ready, 1)
            pool.affine_select(out=late_ts[:, P:S], in_=late_ts[:, P:S], compare_op=ALU.is_ge, fill=-FAR,
                               base=0, pattern=[[-1, P]], channel_multiplier=1).then_inc(pool_ready, 1)
            pool.affine_select(out=sel[:], in_=sel[:], compare_op=ALU.not_equal, fill=1.0, base=0,
                               pattern=[[-1, MH], [0, P]], channel_multiplier=1).then_inc(pool_ready, 1)
            pool.iota(iota_s[:], pattern=[[1, SLOTS]], base=0, channel_multiplier=0,
                      allow_small_or_imprecise_dtypes=True).then_inc(pool_ready, 1)
            pool.iota(iota_e[:], pattern=[[0, TT], [1, NE]], base=0, channel_multiplier=0,
                      allow_small_or_imprecise_dtypes=True).then_inc(pool_ready, 1)
            pool.iota(iota_e8[:], pattern=[[0, TT], [1, NE]], base=NE, channel_multiplier=0,
                      allow_small_or_imprecise_dtypes=True).then_inc(pool_ready, 1)

        @block.scalar
        def _(act):
            def split(i, c=0):
                act.wait_ge(raw_full[i % RAW], 16 * c + 16 * (i // RAW + 1))
                if i >= SPL:
                    act.wait_ge(unit_done, RAW * c + (i - SPL + 1))
                act.activation(wh[:, i % SPL, :], raw[:, i % RAW, :], ACT.Copy).then_inc(hi_split, 1)

            def norm_square(i, tile0, out=xr[:, 0, :]):
                act.wait_ge(*tile0)
                act.activation(out, x[:, 0, :], ACT.Square, accum_out=ss[:, 0:1]).then_inc(nrm_a, 1)

            def norm_root(i):
                act.wait_ge(nrm_d, 6 * i + 1)
                act.wait_ge(nrm_a, 2 * i + 1)
                act.activation(rms[:], ss[:], ACT.Sqrt, scale=1.0 / D, bias=eps[:, 0:1]).then_inc(nrm_a, 1)

            def turn_hi(k, c, dst, gain):
                act.activation(dst[:, c, :], ps[TURN_BANKS[k][c // 2]][:, c % 2 * S:c % 2 * S + S], ACT.Copy,
                               scale=gains[:, 8 * gain + c:8 * gain + c + 1]).then_inc(x_hi, 1)

            def turn(k, gain, pairs):
                for m in pairs:
                    act.wait_ge(x_turned, 4 * k + m + 1)
                    turn_hi(k, 2 * m, xh, gain)
                    turn_hi(k, 2 * m + 1, xh, gain)

            def gain_rows(k, g):
                act.dma_start(grows[8 * k:8 * k + 8, :], g.rearrange("(k p) -> k p", p=P)).then_inc(gn_here, 16)

            act.wait_ge(v_one, 1)
            act.activation(warm[:], eps[:], ACT.Sqrt)
            gain_rows(3, kv_norm)
            gain_rows(4, moba_norm[0])
            gain_rows(5, ffn_norm[1])
            norm_square(0, (x_here, 16 * TT))
            norm_root(0)
            act.wait_ge(nrm_d, 6)
            act.activation(xr[:, 0, :], x[:, 0, :], ACT.Copy, scale=rs[:, 0:1]).then_inc(xr0, 1)
            split(0)
            act.wait_ge(gains_ready, 1)
            turn(0, 0, range(4))
            act.dma_start(graw[:], rows512(w_in[0])[:, :, 3072:3080]).then_inc(c_here, 16)
            act.dma_start(bif[:], b_if[0].rearrange("b h -> h b"), allow_slow_non_contiguous=True).then_inc(c_here, 16)
            act.dma_start(cs[:], rope.rearrange("(t p) c h -> p t c h", p=P)).then_inc(c_here, 16)
            split(1)
            split(2)
            act.wait_ge(c_here, 16 * 3)
            act.activation(gh[:], graw[:], ACT.Copy).then_inc(g_hi, 1)
            split(3)
            act.dma_start(rt[:], rows512(router[0])).then_inc(c_late, 16)
            act.dma_start(gmoe[:], ffn_norm[1].partition_broadcast(P)).then_inc(c_late, 16)
            act.dma_start(gfin[:], final_norm.partition_broadcast(P)).then_inc(c_late, 16)
            act.wait_ge(unit_done, 2)
            for h in range(MH):
                act.activation(qT[:, h, :], ps[h][:, 0:S], ACT.Copy).then_inc(q_out, 1)
            split(4)
            split(5)
            split(6)
            split(7)
            act.wait_ge(unit_done, 6)
            act.activation(v[:, 0, 0:2, 0:MV], ps[1][:].rearrange("p (h n) -> p h n", h=2), ACT.Copy
                           ).then_inc(va_out, 1)
            act.wait_ge(r_abs, 1)
            act.activation(rows[:, 3, :], rows[:, 2, :], ACT.Exp, scale=-1.0).then_inc(r_ln, 1)
            act.wait_ge(r_ln, 1)
            act.activation(rows[:, 4, :], rows[:, 3, :], ACT.Ln, bias=1.0).then_inc(r_ln, 1)
            split(8)
            split(9)
            act.wait_ge(unit_done, 8)
            act.activation(v[:, 0, 2:4, 0:MV], ps[3][:].rearrange("p (h n) -> p h n", h=2), ACT.Copy
                           ).then_inc(va_out, 1)
            split(10)
            act.wait_ge(z_cols, 1)
            act.activation(enm[:], cols[:, 2:4, :], ACT.Exp, scale=-1.0).then_inc(e_nm, 1)
            split(11)
            act.wait_ge(unit_done, 10)
            for t in range(TT):
                act.activation(sigo[:, t, 0:512], ps[5 + t][:], ACT.Sigmoid).then_inc(o_out, 1)
            split(12)
            for h in range(MH):
                act.wait_ge(d_done, h + 1)
                act.activation(E[:, h, :], E[:, h, :], ACT.Exp, scale=-1.0).then_inc(e_done, 1)
            split(13)
            act.wait_ge(unit_done, 12)
            for t in range(TT):
                act.activation(sigo[:, t, 512:1024], ps[1 + t][:], ACT.Sigmoid).then_inc(o_out, 1)
            split(14)
            act.activation(warm[:], eps[:], ACT.Sqrt)
            for half in range(2):
                for h in (2 * half, 2 * half + 1):
                    act.wait_ge(rd_done, h + 1)
                    for t in range(TT):
                        act.activation(junk[:, t, h, :], ps[PV_BANK[h][t]][:, 0:MV], ACT.Square,
                                       scale=rden[:, t, h:h + 1], accum_out=hss[:, t, h:h + 1]).then_inc(h_raw, 1)
                act.wait_ge(h_raw, MH * (half + 1))
                act.activation(hrms[:, :, 2 * half:2 * half + 2], hss[:, :, 2 * half:2 * half + 2], ACT.Sqrt,
                               scale=1.0 / MV, bias=eps[:, 0:1]).then_inc(h_rms, 1)
            turn(1, 1, range(4))
            split(15)
            split(16)
            turn(2, 2, (0, 1))
            split(17)
            turn(2, 2, (2, 3))
            norm_square(1, (resid, 3))
            norm_root(1)
            split(18)

            def silu_chunk(j):
                act.wait_ge(f_gate, j)
                act.activation(f_sg[:], f_g[:], ACT.Silu).then_inc(f_silu, 1)

            def ffn_hi(j, slot):
                act.wait_ge(f_mul, j)
                act.activation(f_hth[:, slot], f_h[:], ACT.Copy).then_inc(f_hi, 1)

            silu_chunk(1)
            split(19)
            with act.Fori(0, (NFC - 1) // 2) as it:
                for jj in range(2):
                    a = U_FFN + 2 + 3 * jj
                    split(a + 2, it)
                    ffn_hi(2 * it + (jj + 1), jj)
                    split(a + 3, it)
                    silu_chunk(2 * it + (jj + 2))
                    split(a + 4, it)
            ffn_hi(NFC, 0)
            split(U_KV + 1)
            turn(3, 3, range(4))
            norm_square(2, (resid, 7))
            norm_root(2)
            split(U_KV + 2)
            for c in range(KT):
                act.wait_ge(x_lo, 24 + c // 2 * 2 + 2)
                turn_hi(3, c, yh2, 4)
            split(U_KV + 3)
            act.wait_ge(nrm_d, 18)
            act.wait_ge(unit_done, U_Q)
            for t in range(TT):
                act.activation(kvs[:, t, :], ps[2 + t][:], ACT.Copy, scale=rs[:, t:t + 1]).then_inc(kv_out, 1)
            split(U_KV + 4)
            split(U_KV + 5)

            def queries_out(n):
                act.wait_ge(unit_done, U_Q + 2 * n + 2)
                act.activation(xr[:, 0, 512 * n:512 * n + 512], ps[(6, 0)[n]][:], ACT.Copy, scale=rs[:, 0:1]
                               ).then_inc(aq_out, 1)

            def queries_turned(b):
                act.wait_ge(q_t, b + 1)
                act.activation(aqT[:, 2 * b:2 * b + 2, :], ps[QT_BANK[b]][:].rearrange("p (h s) -> p h s", h=2),
                               ACT.Copy).then_inc(qt_out, 1)

            def exps(half):
                for g in range(3 * half, 3 * half + 3):
                    act.wait_ge(a_nb, g + 1)
                    for h, t, ap in att_heads(g):
                        act.activation(ap, ap, ACT.Exp, bias=nb[:, t, h:h + 1], scale=HD ** -0.5,
                                       accum_out=sm[:, t, h:h + 1]).then_inc(a_exp, 1)

            def probs_turned(h):
                act.wait_ge(a_pt, h + 1)
                act.activation(pT[:, h, :], ps[ATT_BANK[h]][:, 0:384], ACT.Copy).then_inc(a_pto, 1)

            def heads_hi(half):
                for h in range(4 * half, 4 * half + 4):
                    act.wait_ge(a_o, h + 1)
                    act.activation(xh[:, h, :], ps[ATT_BANK[h]][:, 0:S], ACT.Copy).then_inc(a_hi, 1)

            queries_out(0)
            act.wait_ge(k_t, 1)
            act.activation(akT[:], ps[4][:].rearrange("p (h s) -> p h s", h=KVH), ACT.Copy).then_inc(kt_out, 1)
            split(U_O)
            queries_turned(0)
            split(U_O + 1)
            exps(0)
            queries_out(1)
            for h in range(4):
                probs_turned(h)
            queries_turned(2)
            heads_hi(0)
            split(U_O + 2)
            exps(1)
            split(U_O + 3)
            probs_turned(4)
            probs_turned(6)
            heads_hi(1)
            split(U_O + 4)
            split(U_O + 5)

            def turn_f32(m):
                act.wait_ge(x_turned, 16 + m + 1)
                for c in (2 * m, 2 * m + 1):
                    act.activation(hnT[:, c, :], ps[TURN_BANKS[4][m]][:, c % 2 * S:c % 2 * S + S], ACT.Copy,
                                   scale=gains[:, 40 + c:40 + c + 1]).then_inc(r_tout, 1)

            turn_f32(0)
            norm_square(3, (resid, 11), xeh[:].rearrange("p k s -> p (k s)"))
            turn_f32(2)
            norm_root(3)
            act.wait_ge(xg_ready, 4)
            act.wait_ge(nrm_d, 24)
            for t in range(TT):
                act.activation(xrh[:, t, :], xr[:, t, :], ACT.Copy, scale=rs[:, t:t + 1]).then_inc(hn_hi, 1)
            act.wait_ge(top_m, 1)
            act.activation(ee[:], dd[:], ACT.Exp).then_inc(top_e, 1)
            split(U_MOE + 2)

            def gathered(q):
                act.wait_ge(moe_xg, 2 * q + 1)
                act.activation(xe[:, 0:512], ps[3][:], ACT.Copy).then_inc(moe_xc, 1)

            def expert_hi(q):
                for b in range(2):
                    act.wait_ge(moe_xt, 2 * q + (b + 1))
                    act.activation(xeh[:, 4 * b:4 * b + 4, :], ps[3 + b][:].rearrange("p (k s) -> p k s", k=4),
                                   ACT.Copy).then_inc(moe_xh, 1)

            gathered(0)
            expert_hi(0)

            def expert(q, more=True):
                c = (UE // RAW) * q

                def hidden_hi(j):
                    act.wait_ge(moe_t, NEC * q + (j + 1))
                    act.activation(hth[:, j % 2], ps[2][:].rearrange("p (k s) -> p k s", k=4), ACT.Copy).then_inc(moe_hth, 1)

                for i in range(UE):
                    kind, j, half = UNITS[i - 1] if i else ("", 0, 0)
                    if (kind, half) == ("g", 1):
                        act.wait_ge(unit_done, UE * q + (U_MOE + i))
                        if j:
                            act.wait_ge(moe_h, NEC * q + j)
                        act.activation(sg[:], ps[0][:], ACT.Silu).then_inc(moe_silu, 1)
                        if j:
                            hidden_hi(j - 1)
                    if (kind, j, half) == ("u", 2, 1):
                        act.wait_ge(moe_pt, q + 1)
                        act.activation(phT[:], ps[7][:, 0:S], ACT.Copy).then_inc(moe_ptr, 1)
                    if i == UE - 6 and more:
                        gathered(q + 1)
                    if i == UE - 4 and more:
                        expert_hi(q + 1)
                    if i == UE - 3:
                        hidden_hi(NEC - 1)
                    if 0 < i < UE - 2 or i and more:
                        split(U_MOE + i + 2, c)
                act.wait_ge(unit_done, UE * q + (U_MOE + UE))
                act.wait_ge(moe_w, q + 1)
                for b in range(2):
                    act.activation(ywh[:, 512 * b:512 * b + 512], ps[5 + b][:], ACT.Copy, scale=wcol[:, 0:1]
                                   ).then_inc(moe_yh, 1)
                if more:
                    split(U_MOE + UE + 2, c)

            with act.Fori(0, NE - 1) as e:
                expert(e)
            expert(NE - 1, more=False)
            act.wait_ge(flag_set, 1)
            over = act.value_load(flag[0:1, 0:1], min_val=0, max_val=S)
            with act.If(over > SLOTS):
                for i in range(3):
                    split(U_MOE + i, (UE // RAW) * NE)
                gathered(NE)
                expert_hi(NE)
                with act.Fori(0, NE) as e:
                    expert(e + NE)
                act.wait_ge(moe_bank, 8 * NE + 4)
            act.activation(warm[:], eps[:], ACT.Sqrt)
            norm_square(4, (moe_bank, 4 * NE + 3))
            act.wait_ge(moe_bank, 4 * NE + 4)
            act.activation(xr[:, 1, :], x[:, 1, :], ACT.Square, accum_out=ss[:, 1:2]).then_inc(nrm_a, 1)
            act.wait_ge(nrm_a, 10)
            act.activation(rms[:], ss[:], ACT.Sqrt, scale=1.0 / D, bias=eps[:, 0:1]).then_inc(nrm_a, 1)

        @block.vector
        def _(dve):
            links = [0]

            def link(ins):
                links[0] += 1
                ins.then_inc(chain, 1)
                dve.wait_ge(chain, links[0])

            def split(i, c=0):
                dve.wait_ge(hi_split, RAW * c + (i + 1))
                dve.tensor_tensor(wl[:, i % SPL, :], raw[:, i % RAW, :], f32(wh[:, i % SPL, :]), ALU.subtract
                                  ).then_inc(lo_split, 1)

            def norm_sum(i, tile1=None, out=xr[:, 1, :]):
                if tile1 is not None:
                    dve.wait_ge(*tile1)
                dve.tensor_tensor_reduce(out, x[:, 1, :], x[:, 1, :], 1.0, 0.0, ALU.mult, ALU.add,
                                         ss[:, 1:2]).then_inc(nrm_d, 1)

            def norm_rs(i):
                dve.wait_ge(nrm_a, 2 * i + 1)
                dve.wait_ge(nrm_d, 6 * i + 1)
                dve.tensor_scalar(var[:], ss[:], 1.0 / D, EPS, ALU.mult, ALU.add).then_inc(nrm_d, 1)
                dve.wait_ge(nrm_a, 2 * i + 2)
                newton(rs[:], rms[:], r0[:], t1[:], var[:], nrm_d, 6 * i + 2)
                dve.wait_ge(nrm_d, 6 * i + 6)

            def newton(r, root, first, t, w, done, n):
                dve.reciprocal(first, root).then_inc(done, 1)
                dve.wait_ge(done, n + 1)
                dve.scalar_tensor_tensor(out=t, in0=first, scalar=-0.5, in1=first, op0=ALU.mult, op1=ALU.mult
                                         ).then_inc(done, 1)
                dve.wait_ge(done, n + 2)
                dve.tensor_tensor(t, t, w, ALU.mult).then_inc(done, 1)
                dve.wait_ge(done, n + 3)
                dve.scalar_tensor_tensor(out=r, in0=t, scalar=1.5, in1=first, op0=ALU.add, op1=ALU.mult
                                         ).then_inc(done, 1)

            def turn_lo(k, c, hi, lo, gain):
                dve.scalar_tensor_tensor(out=lo[:, c, :], in0=ps[TURN_BANKS[k][c // 2]][:, c % 2 * S:c % 2 * S + S],
                                         scalar=gains[:, 8 * gain + c:8 * gain + c + 1],
                                         in1=f32(hi[:, c, :]), op0=ALU.mult, op1=ALU.subtract).then_inc(x_lo, 1)

            def turn(k, gain, pairs):
                for m in pairs:
                    dve.wait_ge(x_hi, 8 * k + 2 * m + 2)
                    turn_lo(k, 2 * m, xh, xl, gain)
                    turn_lo(k, 2 * m + 1, xh, xl, gain)

            def add(t, n, bank):
                dve.tensor_tensor(x[:, t, 512 * n:512 * n + 512], x[:, t, 512 * n:512 * n + 512], ps[bank][:],
                                  ALU.add).then_inc(resid, 1)

            dve.memset(eps[:], EPS).then_inc(v_one, 1)
            dve.memset(f32(zero[:]), 0.0).then_inc(v_one, 1)
            dve.memset(v[:, :, :, MV:MV + 1], 1.0).then_inc(v_one, 1)
            norm_sum(0, (x_here, 16 * TT))
            norm_rs(0)
            dve.tensor_scalar(xr[:, 1, :], x[:, 1, :], rs[:, 1:2], None, ALU.mult).then_inc(xr1, 1)
            dve.wait_ge(gains_t, 1)
            dve.tensor_copy(gains[:], ps[0][:, 0:48]).then_inc(gains_ready, 1)
            dve.wait_ge(gains_ready, 1)
            split(0)
            turn(0, 0, range(4))
            split(1)
            split(2)
            split(3)
            dve.wait_ge(g_hi, 1)
            dve.tensor_tensor(gl[:], graw[:], f32(gh[:]), ALU.subtract).then_inc(g_lo, 1)
            split(4)
            dve.wait_ge(unit_done, 4)
            for h in range(MH):
                dve.tensor_copy(kT[:, h, :], ps[4 + h][:, 0:S]).then_inc(k_out, 1)
            split(5)
            dve.wait_ge(g_mm, 1)
            dve.tensor_copy(gsb[:], ps[0][:, 0:16].rearrange("p (t g) -> p t g", t=TT)).then_inc(g_sb, 1)
            split(6)
            dve.wait_ge(unit_done, 6)
            dve.tensor_copy(v[:, 1, 0:2, 0:MV], ps[2][:].rearrange("p (h n) -> p h n", h=2)).then_inc(vd_out, 1)
            dve.wait_ge(g_rows, 1)
            dve.tensor_scalar(rows[:, 0, :], ps[0][0:MH, 0:S], bif[:, 0:1], None, ALU.add).then_inc(r_done, 1)
            link(dve.tensor_scalar(rows[:, 1, :], ps[0][0:MH, S:2 * S], bif[:, 1:2], None, ALU.add))
            dve.scalar_tensor_tensor(out=rows[:, 2, :], in0=rows[:, 1, :], scalar=-1.0, in1=rows[:, 1, :],
                                     op0=ALU.mult, op1=ALU.max).then_inc(r_abs, 1)
            split(7)
            dve.wait_ge(r_ln, 2)
            link(dve.scalar_tensor_tensor(out=rows[:, 5, :], in0=rows[:, 1, :], scalar=0.0, in1=rows[:, 4, :],
                                          op0=ALU.min, op1=ALU.subtract))
            dve.wait_ge(pool_ready, POOL_ALL)
            link(dve.tensor_tensor_scan(rows[:, 6, :], onerow[:], rows[:, 5, :], 0.0, ALU.mult, ALU.add))
            dve.wait_ge(r_done, 1)
            link(dve.tensor_tensor(rows[:, 7, :], rows[:, 0, :], rows[:, 6, :], ALU.subtract))
            link(dve.tensor_tensor_scan(rows[:, 8, :], rows[:, 7, :], rows[:, 7, :], 0.0, ALU.max, ALU.max))
            dve.tensor_tensor(rows[:, 0, :], rows[:, 6, :], rows[:, 8, :], ALU.add).then_inc(r_done, 1)
            split(8)
            dve.wait_ge(unit_done, 8)
            dve.tensor_copy(v[:, 1, 2:4, 0:MV], ps[4][:].rearrange("p (h n) -> p h n", h=2)).then_inc(vd_out, 1)
            split(9)
            dve.wait_ge(z_t, 1)
            dve.tensor_copy(cols[:], ps[0][:, 0:16].rearrange("p (a h) -> p a h", a=4)).then_inc(z_cols, 1)
            split(10)
            split(11)
            dve.wait_ge(z_cols, 1)
            for h in range(MH):
                dve.wait_ge(m_bc, h // 2 + 1)
                mb = ps[7 * (h // 2)][:, S * (h % 2):S * (h % 2) + S]
                dve.scalar_tensor_tensor(out=E[:, h, 0:S], in0=mb, scalar=cols[:, 0, h:h + 1], in1=late_st[:],
                                         op0=ALU.subtract, op1=ALU.max)
                dve.scalar_tensor_tensor(out=E[:, h, S:S + P], in0=mb[:, P:S], scalar=cols[:, 1, h:h + 1],
                                         in1=late_st[:, 0:P], op0=ALU.subtract, op1=ALU.max).then_inc(d_done, 1)
            split(12)
            split(13)
            for h in range(MH):
                dve.wait_ge(s_mm, h + 1)
                dve.wait_ge(e_done, h + 1)
                dve.scalar_tensor_tensor(out=E[:, h, :], in0=ps[3 + h][:, 0:384], scalar=MK ** -0.5, in1=E[:, h, :],
                                         op0=ALU.mult, op1=ALU.mult).then_inc(p_done, 1)
            dve.wait_ge(e_nm, 1)

            def denominator(h):
                for t in range(TT):
                    dve.wait_ge(pv_done, 2 * h + t + 1)
                    last = dve.tensor_copy(nqs[:, t, h:h + 1], ps[PV_BANK[h][t]][:, MV:MV + 1])
                link(last)
                nq, d = nqs[:, :, h:h + 1], den[:, :, h:h + 1]
                link(dve.scalar_tensor_tensor(out=d, in0=nq, scalar=-1.0, in1=nq, op0=ALU.mult, op1=ALU.max))
                link(dve.tensor_tensor(d, d, enm[:, :, h:h + 1], ALU.max))
                dve.reciprocal(rden[:, :, h:h + 1], d).then_inc(rd_done, 1)

            def head_norm(half):
                two = slice(2 * half, 2 * half + 2)
                dve.wait_ge(h_raw, MH * (half + 1))
                dve.tensor_scalar(hvar[:, :, two], hss[:, :, two], 1.0 / MV, EPS, ALU.mult, ALU.add).then_inc(h_rs, 1)
                dve.wait_ge(h_rms, half + 1)
                newton(hrs[:, :, two], hrms[:, :, two], hr0[:, :, two], ht1[:, :, two], hvar[:, :, two], h_rs,
                       5 * half + 1)
                dve.wait_ge(h_rs, 5 * half + 5)
                link(dve.tensor_tensor(hrs[:, :, two], hrs[:, :, two], rden[:, :, two], ALU.mult))

            def heads_out(half):
                for h in (2 * half, 2 * half + 1):
                    for t in range(TT):
                        dve.scalar_tensor_tensor(out=xr[:, t, h * MV:(h + 1) * MV], in0=ps[PV_BANK[h][t]][:, 0:MV],
                                                 scalar=hrs[:, t, h:h + 1], in1=sigo[:, t, h * MV:(h + 1) * MV],
                                                 op0=ALU.mult, op1=ALU.mult).then_inc(h_norm, 1)

            dve.wait_ge(o_out, 4)
            denominator(0)
            denominator(1)
            dve.wait_ge(rd_done, 2)
            denominator(2)
            head_norm(0)
            denominator(3)
            heads_out(0)
            dve.wait_ge(rd_done, MH)
            head_norm(1)
            turn(1, 1, (0, 1))
            heads_out(1)
            turn(1, 1, (2, 3))
            split(14)
            split(15)
            dve.wait_ge(unit_done, 14)
            for t in range(TT):
                add(t, 0, 1 + t)
            split(16)
            turn(2, 2, (0, 1))
            split(17)
            dve.wait_ge(unit_done, 16)
            for t in range(TT):
                add(t, 1, 5 + t)
            norm_sum(1, (resid, 4))
            turn(2, 2, (2, 3))
            norm_rs(1)
            dve.wait_ge(pool_ready, POOL_ALL)
            dve.tensor_copy(before_r[:], before[:]).then_inc(v_one, 1)
            dve.tensor_copy(ones_r[:], ones[:]).then_inc(v_one, 1)
            for t in range(TT):
                last = dve.tensor_scalar(rs_wide[:, t, :], ones[:], rs[:, t:t + 1], None, ALU.mult)
            last.then_inc(rs_w, 1)
            split(18)
            dve.wait_ge(rs_mm, 1)
            dve.tensor_copy(rs_row[:], ps[RB_BANK][:, 0:S]).then_inc(rs_out, 1)
            dve.wait_ge(rs_out, 1)

            def ffn_gate(gate):
                dve.wait_ge(unit_done, gate)
                dve.tensor_tensor(f_g[:], ps[GATE_BANK][:].rearrange("p (k s) -> p k s", k=2),
                                  rs_row[:].unsqueeze(1).to_broadcast([P, 2, S]), ALU.mult).then_inc(f_gate, 1)

            def ffn_mul(j, up):
                dve.wait_ge(f_silu, j)
                dve.wait_ge(unit_done, up)
                dve.tensor_tensor(f_h[:], f_sg[:], ps[UP_BANK][:].rearrange("p (k s) -> p k s", k=2), ALU.mult
                                  ).then_inc(f_mul, 1)

            def ffn_lo(j, slot):
                dve.wait_ge(f_hi, j)
                dve.tensor_tensor(f_htl[:, slot], f_h[:], f32(f_hth[:, slot]), ALU.subtract).then_inc(f_lo, 1)

            ffn_gate(U_FFN + 1)
            split(19)
            ffn_mul(1, U_FFN + 2)
            with dve.Fori(0, (NFC - 1) // 2) as it:
                for jj in range(2):
                    a = U_FFN + 2 + 3 * jj
                    split(a + 2, it)
                    ffn_lo(2 * it + (jj + 1), jj)
                    ffn_gate(RAW * it + (a + 1))
                    split(a + 3, it)
                    ffn_mul(2 * it + (jj + 2), RAW * it + (a + 2))
                    split(a + 4, it)
            ffn_lo(NFC, 0)

            def add_scaled(t, n):
                xs = x[:, t, 512 * n:512 * n + 512]
                dve.scalar_tensor_tensor(out=xs, in0=ps[Y_BANK[t][n]][:], scalar=rs[:, t:t + 1], in1=xs, op0=ALU.mult,
                                         op1=ALU.add).then_inc(resid, 1)

            dve.wait_ge(y_half, 1)
            for t in range(TT):
                add_scaled(t, 0)
            split(U_KV + 1)
            dve.wait_ge(unit_done, U_KV)
            for t in range(TT):
                add_scaled(t, 1)
            turn(3, 3, (0, 1))
            norm_sum(2, (resid, 8))
            turn(3, 3, (2, 3))
            norm_rs(2)
            split(U_KV + 2)
            for c in range(KT):
                dve.wait_ge(x_hi, 32 + c // 2 * 2 + 2)
                turn_lo(3, c, yh2, yl2, 4)
            split(U_KV + 3)
            split(U_KV + 4)

            def rope_rotate(full, n_heads):
                a, b = full[:, :, :, 0:HALF], full[:, :, :, HALF:ROT]
                for g in range(TT):
                    cos = cs[:, g, 0, :].unsqueeze(1).to_broadcast([P, n_heads, HALF])
                    sin = cs[:, g, 1, :].unsqueeze(1).to_broadcast([P, n_heads, HALF])
                    w = [tmp[:, k, g, 0:n_heads, :] for k in range(4)]
                    dve.tensor_tensor(w[0], a[:, g], cos, ALU.mult)
                    dve.tensor_tensor(w[1], b[:, g], sin, ALU.mult)
                    dve.tensor_tensor(w[2], b[:, g], cos, ALU.mult)
                    link(dve.tensor_tensor(w[3], a[:, g], sin, ALU.mult))
                    dve.tensor_tensor(a[:, g], w[0], w[1], ALU.subtract)
                    last = dve.tensor_tensor(b[:, g], w[2], w[3], ALU.add)
                    if g == 0:
                        link(last)
                return last

            dve.wait_ge(kv_out, 2)
            rope_rotate(kvs[:, :, 0:KVH * HD].rearrange("p t (h d) -> p t h d", h=KVH), KVH).then_inc(k_rope, 1)
            split(U_KV + 5)

            def queries_out(n):
                dve.wait_ge(unit_done, U_Q + 2 * n + 2)
                dve.tensor_scalar(xr[:, 1, 512 * n:512 * n + 512], ps[(7, 1)[n]][:], rs[:, 1:2], None, ALU.mult
                                  ).then_inc(aq_out, 1)
                dve.wait_ge(aq_out, 2 * n + 2)
                rope_rotate(xr[:, :, 512 * n:512 * n + 512].rearrange("p t (h d) -> p t h d", h=4), 4
                            ).then_inc(q_rope, 1)

            def queries_turned(b):
                dve.wait_ge(q_t, b + 1)
                dve.tensor_copy(aqT[:, 2 * b:2 * b + 2, :], ps[QT_BANK[b]][:].rearrange("p (h s) -> p h s", h=2)
                                ).then_inc(qt_out, 1)

            def maxima(half):
                for g in range(3 * half, 3 * half + 3):
                    heads, t, h0, n = ATT_GROUPS[g]
                    dve.wait_ge(a_s, g + 1)
                    mask = (late_ts[:] if t else late_ts[:, P:S]).unsqueeze(1).to_broadcast([P, heads, n])
                    scg = sc[:, g, :].rearrange("p (h s) -> p h s", h=heads)
                    link(dve.tensor_tensor(scg, ps[ATT_SBANK[g]][:].rearrange("p (h s) -> p h s", h=heads), mask,
                                           ALU.add))
                    link(dve.tensor_reduce(mx[:, t, h0:h0 + heads], scg, AX, ALU.max))
                    dve.tensor_scalar(nb[:, t, h0:h0 + heads], mx[:, t, h0:h0 + heads], -HD ** -0.5, None, ALU.mult
                                      ).then_inc(a_nb, 1)

            def probabilities(half):
                for g in range(3 * half, 3 * half + 3):
                    heads, t, h0, n = ATT_GROUPS[g]
                    dve.wait_ge(a_exp, sum(ATT_GROUPS[k][0] for k in range(g + 1)))
                    link(dve.reciprocal(rsm[:, t, h0:h0 + heads], sm[:, t, h0:h0 + heads]))
                    scg = sc[:, g, :].rearrange("p (h s) -> p h s", h=heads)
                    dve.tensor_tensor(scg, scg, rsm[:, t, h0:h0 + heads].unsqueeze(2).to_broadcast([P, heads, n]),
                                      ALU.mult).then_inc(a_p, 1)

            def probs_turned(h):
                dve.wait_ge(a_pt, h + 1)
                dve.tensor_copy(pT[:, h, :], ps[ATT_BANK[h]][:, 0:384]).then_inc(a_pto, 1)

            def heads_lo(half):
                for h in range(4 * half, 4 * half + 4):
                    dve.wait_ge(a_hi, h + 1)
                    dve.tensor_tensor(xl[:, h, :], ps[ATT_BANK[h]][:, 0:S], f32(xh[:, h, :]), ALU.subtract
                                      ).then_inc(a_lo, 1)

            queries_out(0)
            split(U_O)
            queries_turned(1)
            maxima(0)
            probabilities(0)
            queries_out(1)
            queries_turned(3)
            split(U_O + 1)
            heads_lo(0)
            maxima(1)
            split(U_O + 2)
            probabilities(1)
            split(U_O + 3)
            probs_turned(5)
            probs_turned(7)
            heads_lo(1)
            split(U_O + 4)
            dve.wait_ge(unit_done, U_O + 3)
            for t in range(TT):
                add(t, 0, 2 + t)
            split(U_O + 5)

            def turn_f32(m):
                dve.wait_ge(x_turned, 16 + m + 1)
                for c in (2 * m, 2 * m + 1):
                    dve.tensor_scalar(hnT[:, c, :], ps[TURN_BANKS[4][m]][:, c % 2 * S:c % 2 * S + S],
                                      gains[:, 40 + c:40 + c + 1], None, ALU.mult).then_inc(r_tout, 1)

            turn_f32(1)

            def times_gain(n):
                cols_n = slice(512 * n, 512 * n + 512)
                for t in range(TT):
                    dve.tensor_tensor(xr[:, t, cols_n], x[:, t, cols_n], gmoe[:, cols_n], ALU.mult
                                      ).then_inc(xg_ready, 1)

            dve.wait_ge(c_late, 16 * 3)
            times_gain(0)
            dve.wait_ge(unit_done, U_O + 4)
            for t in range(TT):
                add(t, 1, 4 + t)
            norm_sum(3, (resid, 12), xe[:])
            turn_f32(3)
            times_gain(1)
            norm_rs(3)
            dve.wait_ge(r_mm, 1)
            for t in range(TT):
                last = dve.tensor_scalar(lg[:, t, :], ps[2 + t][:, 0:NE], rs[:, t:t + 1], None, ALU.mult)
            link(last)

            def wide(col):
                return col[:].unsqueeze(2).to_broadcast([P, TT, NE])

            def first_max(src, m, i, oh):
                link(dve.tensor_reduce(m[:], src[:], AX, ALU.max))
                link(dve.tensor_tensor(eq[:], src[:], wide(m), ALU.is_equal))
                link(dve.scalar_tensor_tensor(out=cand[:], in0=eq[:], scalar=-float(NE), in1=iota_e8[:],
                                              op0=ALU.mult, op1=ALU.add))
                link(dve.tensor_reduce(i[:], cand[:], AX, ALU.min))
                link(dve.tensor_tensor(oh[:], iota_e[:], wide(i), ALU.is_equal))

            def tokens_lo(t):
                dve.scalar_tensor_tensor(out=xrl[:, t, :], in0=xr[:, t, :], scalar=rs[:, t:t + 1],
                                         in1=f32(xrh[:, t, :]), op0=ALU.mult, op1=ALU.subtract).then_inc(hn_lo, 1)

            first_max(lg, m1, i1, oh1)
            link(dve.scalar_tensor_tensor(out=l2[:], in0=oh1[:], scalar=-3e38, in1=lg[:], op0=ALU.mult, op1=ALU.add))
            first_max(l2, m2, i2, oh2)
            dve.tensor_tensor(msk[:], oh1[:], oh2[:], ALU.add).then_inc(top_d, 1)
            dve.tensor_tensor(dd[:], m2[:], m1[:], ALU.subtract).then_inc(top_m, 1)
            dve.wait_ge(hn_hi, TT)
            tokens_lo(0)
            dve.wait_ge(rk_mm, 1)
            dve.wait_ge(top_d, 1)
            link(dve.scalar_tensor_tensor(out=eq[:], in0=ps[5][:, 0:2 * NE].rearrange("p (t e) -> p t e", t=TT),
                                          scalar=1.0, in1=f32(msk[:]), op0=ALU.add, op1=ALU.mult))
            link(dve.tensor_scalar(rank[:, 0:NE, :], eq[:].rearrange("p t e -> p e t"), -1.0, None, ALU.add))
            dve.tensor_scalar(rank[:, NE, :], rank[:, 0, :], -float(SLOTS), None, ALU.add)
            link(dve.tensor_reduce(most[:], ps[5][:, 2 * NE:3 * NE], AX, ALU.max))
            dve.tensor_copy(flag[:], most[0:1, :]).then_inc(flag_set, 1)

            def place(e):
                for t in range(TT):
                    last = dve.tensor_scalar(ph[:, t, :], iota_s[:], rank[:, e, t:t + 1], None, ALU.is_equal)
                return last

            def place_r(e):
                for t in range(TT):
                    last = dve.tensor_scalar(phr[:, t, :], iota_s[:], rank[:, e, t:t + 1], None, ALU.is_equal)
                return last

            place_r(0).then_inc(moe_p, 1)
            tokens_lo(1)
            place(0).then_inc(moe_bank, 4)
            def gathered(q):
                dve.wait_ge(moe_xg, 2 * q + 2)
                dve.tensor_copy(xe[:, 512:1024], ps[4][:]).then_inc(moe_xc, 1)

            def expert_lo(q):
                for b in range(2):
                    dve.wait_ge(moe_xh, 2 * q + (b + 1))
                    dve.tensor_tensor(xel[:, 4 * b:4 * b + 4, :], ps[3 + b][:].rearrange("p (k s) -> p k s", k=4),
                                      f32(xeh[:, 4 * b:4 * b + 4, :]), ALU.subtract).then_inc(moe_xl, 1)

            gathered(0)
            expert_lo(0)
            split(U_MOE + 2)
            dve.wait_ge(top_e, 1)
            link(dve.tensor_scalar(w2[:], ee[:], 1.0, None, ALU.add))
            link(dve.reciprocal(w1[:], w2[:]))
            link(dve.tensor_tensor(w2[:], ee[:], w1[:], ALU.mult))
            dve.tensor_tensor(cmb[:], oh1[:], wide(w1), ALU.mult)
            link(dve.tensor_tensor(cmb2[:], oh2[:], wide(w2), ALU.mult))
            link(dve.tensor_tensor(cmb[:], cmb[:], cmb2[:], ALU.add))
            cmb_et = cmb[:].rearrange("p t e -> p e t")
            link(dve.tensor_copy(cw[:, :, :, 0], cmb_et))
            dve.tensor_tensor(cw[:, :, :, 1], cmb_et, f32(cw[:, :, :, 0]), ALU.subtract)

            def expert(q, e, more=True):
                c = (UE // RAW) * q

                def hidden_lo(j):
                    dve.wait_ge(moe_hth, NEC * q + (j + 1))
                    dve.tensor_tensor(htl[:, j % 2], ps[2][:].rearrange("p (k s) -> p k s", k=4), f32(hth[:, j % 2]), ALU.subtract
                                      ).then_inc(moe_htl, 1)

                for i in range(UE):
                    kind, j, half = UNITS[i - 1] if i else ("", 0, 0)
                    if (kind, half) == ("g", 1) and j:
                        hidden_lo(j - 1)
                    if (kind, half) == ("u", 1):
                        dve.wait_ge(unit_done, UE * q + (U_MOE + i))
                        dve.wait_ge(moe_silu, NEC * q + (j + 1))
                        dve.tensor_tensor(hh[:], sg[:], ps[1][:], ALU.mult).then_inc(moe_h, 1)
                    if (kind, j, half) == ("d", 1, 1):
                        dve.wait_ge(moe_ptr, q + 1)
                        dve.tensor_reduce(wcol[:], ps[7][:, S:S + 2], AX, ALU.add).then_inc(moe_w, 1)
                    if (kind, j, half) == ("d", 3, 1) and more:
                        place(e + 1)
                        place_r(e + 1).then_inc(moe_p, 1)
                    if i == UE - 6 and more:
                        gathered(q + 1)
                    if i == UE - 4 and more:
                        expert_lo(q + 1)
                    if i == UE - 3:
                        hidden_lo(NEC - 1)
                    if 0 < i < UE - 2 or i == UE - 2 and more:
                        split(U_MOE + i + 2, c)
                for b in range(2):
                    dve.wait_ge(moe_yh, 2 * q + (b + 1))
                    dve.scalar_tensor_tensor(out=ywl[:, 512 * b:512 * b + 512], in0=ps[5 + b][:],
                                             scalar=wcol[:, 0:1], in1=f32(ywh[:, 512 * b:512 * b + 512]),
                                             op0=ALU.mult, op1=ALU.subtract).then_inc(moe_yl, 1)
                dve.wait_ge(moe_bank, 4 * q + 4)
                for k in range(4):
                    n, t = k // 2, k % 2
                    dve.wait_ge(moe_sc, 4 * q + (k + 1))
                    xs = x[:, t, 512 * n:512 * n + 512]
                    dve.tensor_tensor(xs, xs, ps[SC_BANK[k]][:], ALU.add).then_inc(moe_bank, 1)
                if more:
                    split(U_MOE + UE + 1, c)
                    split(U_MOE + UE + 2, c)

            with dve.Fori(0, NE - 1) as e:
                expert(e, e)
            expert(NE - 1, NE - 1, more=False)
            dve.wait_ge(moe_bank, 4 * NE + 4)
            dve.wait_ge(flag_set, 1)
            over = dve.value_load(flag[0:1, 0:1], min_val=0, max_val=S)
            with dve.If(over > SLOTS):
                dve.tensor_scalar(rank[:], rank[:], -float(SLOTS), None, ALU.add).then_inc(flag_set, 1)
                dve.wait_ge(flag_set, 2)
                place(0)
                place_r(0).then_inc(moe_p, 1)
                for i in range(3):
                    split(U_MOE + i, (UE // RAW) * NE)
                gathered(NE)
                expert_lo(NE)
                with dve.Fori(0, NE) as e:
                    expert(e + NE, e)
                dve.wait_ge(moe_bank, 8 * NE + 4)
            dve.wait_ge(nrm_a, 10)
            dve.tensor_scalar(var[:], ss[:], 1.0 / D, EPS, ALU.mult, ALU.add).then_inc(nrm_d, 1)
            dve.wait_ge(nrm_a, 11)
            newton(rs[:], rms[:], r0[:], t1[:], var[:], nrm_d, 25)
            dve.wait_ge(nrm_d, 29)
            for t in range(TT):
                for n in range(2):
                    cols_n = slice(512 * n, 512 * n + 512)
                    dve.scalar_tensor_tensor(out=xr[:, t, cols_n], in0=x[:, t, cols_n], scalar=rs[:, t:t + 1],
                                             in1=gfin[:, cols_n], op0=ALU.mult, op1=ALU.mult).then_inc(fin, 1)

        @block.tensor
        def _(pe):
            def mm3(bank, sh, sl, mh, ml, start, stop):
                pe.matmul(bank, sh, mh, start=start, stop=False)
                pe.matmul(bank, sh, ml, start=False, stop=False)
                return pe.matmul(bank, sl, mh, start=False, stop=stop)

            def keep_warm(n, bank):
                for _ in range(n):
                    pe.matmul(ps[bank][:], zero[:, 0:P], zero[:], start=True, stop=True)

            def project(i, half, banks, sh, sl, between=None):
                pe.wait_ge(lo_split, i + 1)
                for t in range(TT):
                    if t == 1 and between is not None:
                        between()
                    for kk in range(4):
                        f = 4 * half + kk
                        last = mm3(ps[banks[t]][:], sh[:, f, t * P:(t + 1) * P], sl[:, f, t * P:(t + 1) * P],
                                   kn(wh, i % SPL)[:, kk, :], kn(wl, i % SPL)[:, kk, :],
                                   f == 0, f == KT - 1)
                last.then_inc(unit_done, 1)

            def turn(k, m, src):
                bank = ps[TURN_BANKS[k][m]]
                for c in (2 * m, 2 * m + 1):
                    for t in range(TT):
                        last = pe.transpose(bank[:, c % 2 * S + t * P:c % 2 * S + (t + 1) * P],
                                            src[:, t, c * P:(c + 1) * P], ident[:])
                last.then_inc(x_turned, 1)

            pe.wait_ge(v_one, 2)
            keep_warm(10, 3)
            pe.wait_ge(pool_ready, POOL_ALL)
            pe.wait_ge(gn_here, 16 * 6)
            pe.transpose(ps[0][:, 0:48], grows[:], ident[0:48, 0:48]).then_inc(gains_t, 1)
            keep_warm(12, 3)
            pe.wait_ge(xr0, 1)
            pe.wait_ge(xr1, 1)
            for m in range(4):
                turn(0, m, xr)
            pe.wait_ge(gains_ready, 1)
            keep_warm(27, 3)
            def gates(t, half):
                if (t, half) == (0, 0):
                    pe.wait_ge(g_lo, 1)
                    pe.wait_ge(q_out, 4)
                for f in range(4 * half, 4 * half + 4):
                    last = mm3(ps[0][:, 8 * t:8 * t + 8], xh[:, f, t * P:(t + 1) * P], xl[:, f, t * P:(t + 1) * P],
                               gh[:, f, :], gl[:, f, :], f == 0, f == KT - 1)
                if (t, half) == (1, 1):
                    last.then_inc(g_mm, 1)

            for m in range(2):
                for half in range(2):
                    i = U_IN + 2 * m + half
                    pe.wait_ge(lo_split, i + 1)
                    pe.wait_ge(x_lo, 4 * half + 4 if m == 0 else KT)
                    for h in range(MH):
                        for kk in range(4):
                            f, cols_h = 4 * half + kk, slice(h * MK, (h + 1) * MK)
                            last = mm3(ps[4 * m + h][:, 0:S], kn(wh, i % SPL)[:, kk, cols_h],
                                       kn(wl, i % SPL)[:, kk, cols_h], xh[:, f, :], xl[:, f, :], f == 0, f == KT - 1)
                        if h == MH - 1:
                            last.then_inc(unit_done, 1)
                        if (m, half) == (1, 1):
                            gates(h // 2, h % 2)
            for half in range(2):
                project(U_IN + 4 + half, half, (1, 2), xh, xl)
            pe.wait_ge(g_sb, 1)
            for g in range(2):
                for t in range(TT):
                    last = pe.transpose(ps[0][0:MH, g * S + t * P:g * S + (t + 1) * P],
                                        gsb[:, t, g * MH:(g + 1) * MH], ident[:])
            last.then_inc(g_rows, 1)
            pe.wait_ge(k_out, 4)
            for half in range(2):
                project(U_IN + 6 + half, half, (3, 4), xh, xl)
            pe.wait_ge(r_done, 2)
            for a, (row, t) in enumerate([(7, 0), (7, 1), (0, 0), (0, 1)]):
                last = pe.transpose(ps[0][:, 4 * a:4 * a + 4], rows[:, row, t * P:(t + 1) * P], ident[0:MH, 0:MH])
            last.then_inc(z_t, 1)
            for half in range(2):
                project(U_IN + 8 + half, half, (5, 6), xh, xl)
            pe.wait_ge(z_cols, 1)
            for h in range(MH):
                last = pe.matmul(ps[7 * (h // 2)][:, S * (h % 2):S * (h % 2) + S], sel[:, h, :], rows[:, 8, :],
                                 start=True, stop=True)
                if h % 2:
                    last.then_inc(m_bc, 1)
            pe.wait_ge(va_out, 1)
            pe.wait_ge(vd_out, 1)
            for half in range(2):
                project(U_IN + 10 + half, half, (1, 2), xh, xl)
            pe.wait_ge(va_out, 2)
            pe.wait_ge(vd_out, 2)
            for h in range(MH):
                if h == 2:
                    pe.wait_ge(o_out, 2)
                pe.matmul(ps[3 + h][:, 0:S], kT[:, h, 0:P], qT[:, h, :], start=True, stop=True)
                pe.matmul(ps[3 + h][:, S:S + P], kT[:, h, P:S], qT[:, h, P:S], start=True, stop=True
                          ).then_inc(s_mm, 1)
            pe.wait_ge(v_one, 3)
            for h in range(MH):
                pe.wait_ge(p_done, MH if h >= 2 else h + 1)
                if h == 0:
                    pe.wait_ge(d_done, MH)
                if h == 1:
                    pe.wait_ge(o_out, 4)
                pe.matmul(ps[PV_BANK[h][0]][:, 0:MV + 1], E[:, h, 0:P], v[:, 0, h, :], start=True, stop=True
                          ).then_inc(pv_done, 1)
                b = ps[PV_BANK[h][1]][:, 0:MV + 1]
                pe.matmul(b, E[:, h, P:S], v[:, 0, h, :], start=True, stop=False)
                pe.matmul(b, E[:, h, S:S + P], v[:, 1, h, :], start=False, stop=True).then_inc(pv_done, 1)

            def turn_heads(half):
                for m in (2 * half, 2 * half + 1):
                    pe.wait_ge(h_norm, 2 * m + 2)
                    turn(1, m, xr)

            turn_heads(0)
            keep_warm(5, 1)
            pe.wait_ge(x_lo, 12)
            project(U_OUT, 0, (1, 2), xh, xl, between=lambda: turn_heads(1))
            pe.wait_ge(x_lo, 16)
            project(U_OUT + 1, 1, (1, 2), xh, xl)
            for half in range(2):
                if half == 1:
                    pe.wait_ge(resid, 2)
                    turn(2, 0, x)
                    turn(2, 1, x)
                project(U_OUT + 2 + half, half, (5, 6), xh, xl)
            def gate_up(i, bank, c=0, first=False):
                pe.wait_ge(lo_split, RAW * c + (i + 1))
                for k in range(2):
                    for f in range(KT):
                        if first and (k, f) == (0, 4):
                            pe.wait_ge(resid, 4)
                            turn(2, 2, x)
                            turn(2, 3, x)
                            keep_warm(5, 7)
                        if first and k == 0:
                            pe.wait_ge(x_lo, 16 + f + 1)
                        last = mm3(ps[bank][:, S * k:S * k + S], kc(wh, i % SPL)[:, f, k * P:(k + 1) * P],
                                   kc(wl, i % SPL)[:, f, k * P:(k + 1) * P], xh[:, f, :], xl[:, f, :],
                                   f == 0, f == KT - 1)
                last.then_inc(unit_done, 1)

            gate_up(U_FFN, GATE_BANK, first=True)
            pe.wait_ge(rs_w, 1)
            for t in range(TT):
                last = pe.matmul(ps[RB_BANK][:, t * P:(t + 1) * P], rs_wide[:, t, :], ident[:], start=True, stop=True)
            last.then_inc(rs_mm, 1)
            gate_up(U_FFN + 1, UP_BANK)
            for t in range(TT):
                for n in range(2):
                    pe.matmul(ps[Y_BANK[t][n]][:], zero[:, 0:P], zero[:], start=True, stop=False)

            def down(i, j, slot, c, stop):
                pe.wait_ge(lo_split, RAW * c + (i + 1))
                pe.wait_ge(f_lo, j)
                for n in range(2):
                    for t in range(TT):
                        if stop and (n, t) == (1, 1):
                            pe.wait_ge(f_gate, NFC)
                            pe.wait_ge(resid, 6)
                            turn(3, 0, x)
                            turn(3, 1, x)
                        for k in range(2):
                            last = mm3(ps[Y_BANK[t][n]][:], f_hth[:, slot, k, t * P:(t + 1) * P],
                                       f_htl[:, slot, k, t * P:(t + 1) * P],
                                       fn(wh, i % SPL)[:, k, 512 * n:512 * n + 512],
                                       fn(wl, i % SPL)[:, k, 512 * n:512 * n + 512], False, stop and k == 1)
                    if stop and n == 0:
                        last.then_inc(y_half, 1)
                last.then_inc(unit_done, 1)

            with pe.Fori(0, (NFC - 1) // 2) as it:
                for jj in range(2):
                    a = U_FFN + 2 + 3 * jj
                    pe.wait_ge(f_gate, 2 * it + (jj + 1))
                    gate_up(a, GATE_BANK, it)
                    pe.wait_ge(f_mul, 2 * it + (jj + 1))
                    gate_up(a + 1, UP_BANK, it)
                    down(a + 2, 2 * it + (jj + 1), jj, it, False)
            down(U_KV - 1, NFC, 0, 0, True)
            keep_warm(6, 0)
            pe.wait_ge(resid, 8)
            turn(3, 2, x)
            turn(3, 3, x)
            keep_warm(3, 2)
            for half in range(2):
                pe.wait_ge(x_lo, 24 + 4 * half + 4)
                project(U_KV + half, half, (2, 3), xh, xl)
            for half in range(2):
                pe.wait_ge(x_lo, 32 + 4 * half + 4)
                project(U_Q + half, half, (6, 7), yh2, yl2)
            pe.wait_ge(k_rope, 1)
            for g in range(KVH):
                for t in range(TT):
                    last = pe.transpose(ps[4][:, g * S + t * P:g * S + (t + 1) * P], kvs[:, t, g * HD:(g + 1) * HD],
                                        ident[:])
            last.then_inc(k_t, 1)

            def turn_queries(n):
                pe.wait_ge(q_rope, n + 1)
                for h in range(4 * n, 4 * n + 4):
                    for t in range(TT):
                        last = pe.transpose(ps[QT_BANK[h // 2]][:, (h % 2) * S + t * P:(h % 2) * S + (t + 1) * P],
                                            xr[:, t, h * HD:(h + 1) * HD], ident[:])
                    if h % 2:
                        last.then_inc(q_t, 1)

            def scores(n):
                pe.wait_ge(qt_out, 2 * n + 2)
                for g in range(3 * n, 3 * n + 3):
                    heads, t, h0, m = ATT_GROUPS[g]
                    for a in range(heads):
                        h = h0 + a
                        last = pe.matmul(ps[ATT_SBANK[g]][:, a * m:(a + 1) * m], aqT[:, h, t * P:(t + 1) * P],
                                         akT[:, h // (AH // KVH), 0:m], start=True, stop=True)
                    last.then_inc(a_s, 1)

            def turn_probs(n):
                pe.wait_ge(a_p, 3 * n + 3)
                for h in range(4 * n, 4 * n + 4):
                    b = ps[ATT_BANK[h]]
                    g0, a0 = 3 * n + 2, (h % 4) * P
                    g1, a1 = 3 * n + h % 4 // 2, (h % 2) * S
                    pe.transpose(b[:, 0:P], sc[:, g0, a0:a0 + P], ident[:])
                    pe.transpose(b[:, P:S], sc[:, g1, a1:a1 + P], ident[:])
                    pe.transpose(b[:, S:S + P], sc[:, g1, a1 + P:a1 + S], ident[:]).then_inc(a_pt, 1)

            def values(n):
                pe.wait_ge(a_pto, 4 * n + 4)
                for h in range(4 * n, 4 * n + 4):
                    b = ps[ATT_BANK[h]]
                    g = KVH * HD + (h // (AH // KVH)) * HD
                    pe.matmul(b[:, 0:S], kvs[:, 0, g:g + HD], pT[:, h, 0:S], start=True, stop=False)
                    pe.matmul(b[:, P:S], kvs[:, 1, g:g + HD], pT[:, h, S:S + P], start=False, stop=True
                              ).then_inc(a_o, 1)

            project(U_Q + 2, 0, (0, 1), yh2, yl2, between=lambda: turn_queries(0))
            pe.wait_ge(kt_out, 1)
            scores(0)
            project(U_Q + 3, 1, (0, 1), yh2, yl2)
            keep_warm(5, 3)
            turn_probs(0)
            turn_queries(1)
            values(0)
            scores(1)
            pe.wait_ge(a_lo, 4)
            project(U_O, 0, (2, 3), xh, xl)
            project(U_O + 1, 0, (4, 5), xh, xl)
            turn_probs(1)
            values(1)
            pe.wait_ge(a_lo, AH)
            project(U_O + 2, 1, (2, 3), xh, xl)

            def turn_first_half():
                pe.wait_ge(resid, 10)
                turn(4, 0, x)
                turn(4, 1, x)

            project(U_O + 3, 1, (4, 5), xh, xl, between=turn_first_half)
            def logits(half):
                pe.wait_ge(r_tout, 4 * half + 4)
                for t in range(TT):
                    for f in range(4 * half, 4 * half + 4):
                        last = pe.matmul(ps[2 + t][:, 0:NE], hnT[:, f, t * P:(t + 1) * P], rt[:, f, :],
                                         start=(f == 0), stop=(f == KT - 1))
                return last

            pe.wait_ge(c_late, 16 * 3)
            logits(0)
            pe.wait_ge(resid, 12)
            turn(4, 2, x)
            turn(4, 3, x)
            logits(1).then_inc(r_mm, 1)
            keep_warm(9, 6)
            pe.wait_ge(v_one, 5)
            pe.wait_ge(top_d, 1)
            pe.matmul(ps[5][:, 0:NE], before_r[:], msk[:, 0, :], start=True, stop=True)
            pe.matmul(ps[5][:, NE:2 * NE], ones_r[:], msk[:, 0, :], start=True, stop=False)
            pe.matmul(ps[5][:, NE:2 * NE], before_r[:], msk[:, 1, :], start=False, stop=True)
            pe.matmul(ps[5][:, 2 * NE:3 * NE], ones_r[:], msk[:, 0, :], start=True, stop=False)
            pe.matmul(ps[5][:, 2 * NE:3 * NE], ones_r[:], msk[:, 1, :], start=False, stop=True).then_inc(rk_mm, 1)

            def gather(first=False):
                for b in range(2):
                    for t in range(TT):
                        for k, src in enumerate((xrh, xrl)):
                            if first and k == 1:
                                pe.wait_ge(hn_lo, t + 1)
                            last = pe.matmul(ps[3 + b][:], phr[:, t, :], src[:, t, 512 * b:512 * b + 512],
                                             start=(t == 0 and k == 0), stop=(t == 1 and k == 1))
                    last.then_inc(moe_xg, 1)

            def turn_gathered(q):
                pe.wait_ge(moe_xc, 2 * q + 2)
                for f in range(KT):
                    last = pe.transpose(ps[3 + f // 4][:, f % 4 * P:(f % 4 + 1) * P], xe[:, f * P:(f + 1) * P], ident[:])
                    if f % 4 == 3:
                        last.then_inc(moe_xt, 1)

            keep_warm(4, 6)
            pe.wait_ge(moe_p, 1)
            gather(first=True)
            keep_warm(4, 6)
            turn_gathered(0)
            keep_warm(7, 6)

            def expert(q, e, more=True):
                def hidden(j):
                    pe.wait_ge(moe_h, NEC * q + (j + 1))
                    for k in range(4):
                        last = pe.transpose(ps[2][:, k * P:(k + 1) * P], hh[:, k * P:(k + 1) * P], ident[:])
                    last.then_inc(moe_t, 1)

                pe.wait_ge(moe_xl, 2 * q + 2)
                for i in range(UE):
                    kind, j, half = UNITS[i]
                    n = U_MOE + i
                    if i == UE - 6 and more:
                        pe.wait_ge(moe_p, q + 2)
                        pe.wait_ge(moe_bank, 4 * q + 4)
                        gather()
                    if i == UE - 4 and more:
                        turn_gathered(q + 1)
                    if i == UE - 3:
                        hidden(NEC - 1)
                    if (kind, j, half) == ("d", 0, 0):
                        pe.wait_ge(moe_bank, 4 * q + 4)
                    if (kind, half) == ("g", 0) and j:
                        pe.wait_ge(moe_silu, NEC * q + j)
                    pe.wait_ge(lo_split, UE * q + (n + 1))
                    if kind in "gu":
                        for kk in range(4):
                            f = 4 * half + kk
                            last = mm3(ps["gu".index(kind)][:], xeh[:, f, :], xel[:, f, :], kn(wh, n % SPL)[:, kk, :],
                                       kn(wl, n % SPL)[:, kk, :], f == 0, f == KT - 1)
                    else:
                        pe.wait_ge(moe_htl, NEC * q + (j + 1))
                        for kk in range(2):
                            f = 2 * half + kk
                            for b in range(2):
                                last = mm3(ps[5 + b][:], hth[:, j % 2, f, :], htl[:, j % 2, f, :],
                                           fn(wh, n % SPL)[:, kk, 512 * b:512 * b + 512],
                                           fn(wl, n % SPL)[:, kk, 512 * b:512 * b + 512],
                                           j == 0 and f == 0, j == NEC - 1 and f == 3)
                    last.then_inc(unit_done, 1)
                    if (kind, half) == ("g", 1) and j:
                        hidden(j - 1)
                    if (kind, j, half) == ("u", 2, 1):
                        pe.wait_ge(moe_bank, 4 * q + 4)
                        for t in range(TT):
                            pe.transpose(ps[7][:, t * P:(t + 1) * P], ph[:, t, :], ident[:])
                        for t in range(TT):
                            last = pe.matmul(ps[7][:, S:S + 2], phr[:, t, :], cw[:, e, t, :], start=(t == 0),
                                             stop=(t == 1))
                        last.then_inc(moe_pt, 1)
                pe.wait_ge(moe_ptr, q + 1)
                for k in range(4):
                    n, t = k // 2, k % 2
                    pe.wait_ge(moe_yl, 2 * q + (n + 1))
                    pe.matmul(ps[SC_BANK[k]][:], phT[:, t * P:(t + 1) * P], ywh[:, 512 * n:512 * n + 512],
                              start=True, stop=False)
                    pe.matmul(ps[SC_BANK[k]][:], phT[:, t * P:(t + 1) * P], ywl[:, 512 * n:512 * n + 512],
                              start=False, stop=True).then_inc(moe_sc, 1)

            with pe.Fori(0, NE - 1) as e:
                expert(e, e)
            expert(NE - 1, NE - 1, more=False)
            pe.wait_ge(flag_set, 1)
            over = pe.value_load(flag[0:1, 0:1], min_val=0, max_val=S)
            with pe.If(over > SLOTS):
                pe.wait_ge(moe_p, NE + 1)
                pe.wait_ge(moe_bank, 4 * NE + 4)
                gather()
                turn_gathered(NE)
                with pe.Fori(0, NE) as e:
                    expert(e + NE, e)


_INS = ['x', 'mlstm_norm', 'mlstm_w_in', 'mlstm_b_if', 'mlstm_out_norm', 'mlstm_w_out', 'ffn_norm', 'dense_w_gu',
        'dense_w_down', 'moe_router', 'moe_w_gu', 'moe_w_down', 'kv_norm', 'kv_w', 'moba_norm', 'moba_w_q',
        'moba_w_o', 'final_norm']


def rope_table():
    import numpy as _np

    freq = (500000.0 ** (-_np.arange(0, ROT, 2) / ROT)).astype(_np.float32)
    angle = _np.arange(S, dtype=_np.float32)[:, None] * freq[None, :]
    return _np.stack([_np.cos(angle), _np.sin(angle)], axis=1).astype(_np.float32)


def kernel(**inputs):
    import numpy as _np
    import concourse.bacc as _bacc
    from concourse import mybir as _mybir
    from concourse.bass_utils import run_bass_kernel_spmd as _run

    nc = _bacc.Bacc("TRN2", target_bir_lowering=False, num_devices=1)
    arrays, args = {}, []
    for name in _INS + ['rope']:
        a = _np.ascontiguousarray(inputs[name]) if name != 'rope' else rope_table()
        arrays[f"in_{name}_dram"] = a
        args.append(nc.dram_tensor(f"in_{name}_dram", a.shape, _mybir.dt.from_np(a.dtype), kind="ExternalInput").ap())
    args.append(nc.dram_tensor("out_0_dram", (1, S, D), F32, kind="ExternalOutput").ap())
    yoco_block(nc, *args)
    r = _run(nc, [arrays], core_ids=[0])
    return r.results[0]["out_0_dram"]
```
